# Optimizing a Trainium2 kernel written in Bass

```python
import jax, jax.numpy as jnp
from jax import lax
import numpy as np
import math

D_MODEL = 1024
BATCH = 1
SEQ = 256
DEPTH = 2

HEAD_DIM = 64
HEADS_PER_GROUP = 8
DILATION_GROUPS = ((128, 1), (512, 4), (2048, 16))
N_GROUPS = len(DILATION_GROUPS)
N_ATTN_HEADS = N_GROUPS * HEADS_PER_GROUP
QKV_WIDTH = N_ATTN_HEADS * HEAD_DIM
ATTN_OUT = HEADS_PER_GROUP * HEAD_DIM
CONV_WIDTH = D_MODEL
CONV_K = 3
D_FF = ((8 * D_MODEL // 3) + 127) // 128 * 128
IN_WIDTH = 3 * QKV_WIDTH + 3 * CONV_WIDTH + 2 * D_MODEL
NUM_BUCKETS = 32
MAX_DISTANCE = 2048
BLOCK = 128
N_SUB = 3
EPS = 1e-6
NEG_INF = -1e30


def _t5_bucket(dist):
    exact = NUM_BUCKETS // 2
    d = np.maximum(dist, 1).astype(np.float32)
    large = exact + (np.log(d / exact) / np.log(MAX_DISTANCE / exact) * (NUM_BUCKETS - exact)).astype(np.int32)
    large = np.minimum(large, NUM_BUCKETS - 1)
    return np.where(dist < exact, dist, large).astype(np.int32)

def _rmsnorm(x, g):
    xf = x.astype(jnp.float32)
    y = xf * lax.rsqrt(jnp.mean(xf * xf, axis=-1, keepdims=True) + EPS) * g.astype(jnp.float32)
    return y.astype(x.dtype)

def _swiglu(h, w_gate, w_up, w_down):
    return (jax.nn.silu(h @ w_gate) * (h @ w_up)) @ w_down

def _causal_dwconv(u, w):
    rhs = w.astype(u.dtype).reshape(CONV_K, 1, u.shape[-1])
    return lax.conv_general_dilated(u, rhs, window_strides=(1,), padding=[(CONV_K - 1, 0)],
                                    dimension_numbers=("NWC", "WIO", "NWC"),
                                    feature_group_count=u.shape[-1])

def _dilated_window_attention(q, k, v, bias_tab, window, dilation):
    B, S, H, E = q.shape
    span = window // dilation
    L = S // dilation
    nb = -(-L // BLOCK)
    Lp = nb * BLOCK

    def to_sub(t):
        t = t.reshape(B, L, dilation, H, E)
        return jnp.pad(t, ((0, 0), (0, Lp - L), (0, 0), (0, 0), (0, 0)))

    qs, ks, vs = to_sub(q), to_sub(k), to_sub(v)
    qb = qs.reshape(B, nb, BLOCK, dilation, H, E)

    def key_blocks(t):
        tp = jnp.pad(t, ((0, 0), (BLOCK, 0), (0, 0), (0, 0), (0, 0)))
        prev = tp[:, :Lp].reshape(B, nb, BLOCK, dilation, H, E)
        cur = t.reshape(B, nb, BLOCK, dilation, H, E)
        return jnp.concatenate([prev, cur], axis=2)

    kb, vb = key_blocks(ks), key_blocks(vs)

    i = np.arange(BLOCK)[:, None]
    j = np.arange(2 * BLOCK)[None, :]
    rel = i - j + BLOCK
    band = (rel >= 0) & (rel <= span)
    first_ok = (np.arange(nb)[:, None, None] > 0) | (j[None] >= BLOCK)
    mask = jnp.asarray(band[None] & first_ok)[None, :, None, None]
    bucket = jnp.asarray(_t5_bucket(np.maximum(rel, 0) * dilation))
    bias = jnp.transpose(bias_tab[bucket].astype(jnp.float32), (2, 0, 1))

    logits = jnp.einsum("bnqrhe,bnkrhe->bnrhqk", qb, kb).astype(jnp.float32) * (HEAD_DIM ** -0.5)
    logits = jnp.where(mask, logits + bias, NEG_INF)
    m = jnp.max(logits, axis=-1, keepdims=True)
    p = jnp.exp(logits - m)
    s = jnp.sum(p, axis=-1)
    o = jnp.einsum("bnrhqk,bnkrhe->bnqrhe", p, vb.astype(jnp.float32))
    s_q = jnp.transpose(s, (0, 1, 4, 2, 3))
    o = o / s_q[..., None]
    lse = jnp.transpose(m[..., 0] + jnp.log(s), (0, 1, 4, 2, 3))
    o = o.reshape(B, Lp, dilation, H, E)[:, :L].reshape(B, S, H, E)
    lse = lse.reshape(B, Lp, dilation, H)[:, :L].reshape(B, S, H)
    return o, lse

def _mixer(h, w_in, conv_w, w_conv_out, w_attn_out, w_o, rel_bias):
    B, S, _ = h.shape
    u = h @ w_in
    splits = np.cumsum([QKV_WIDTH, QKV_WIDTH, QKV_WIDTH, CONV_WIDTH, CONV_WIDTH, CONV_WIDTH, D_MODEL])
    q, k, v, cb, cc, ch, g_conv, g_attn = jnp.split(u, splits, axis=-1)

    y_conv = (cb * _causal_dwconv(cc * ch, conv_w)) @ w_conv_out

    q = q.reshape(B, S, N_GROUPS, HEADS_PER_GROUP, HEAD_DIM)
    k = k.reshape(B, S, N_GROUPS, HEADS_PER_GROUP, HEAD_DIM)
    v = v.reshape(B, S, N_GROUPS, HEADS_PER_GROUP, HEAD_DIM)
    outs, lses = [], []
    for g, (window, dilation) in enumerate(DILATION_GROUPS):
        tab = rel_bias[:, g * HEADS_PER_GROUP:(g + 1) * HEADS_PER_GROUP]
        o_g, lse_g = _dilated_window_attention(q[:, :, g], k[:, :, g], v[:, :, g], tab, window, dilation)
        outs.append(o_g)
        lses.append(lse_g)
    alpha = jax.nn.softmax(jnp.stack(lses, axis=0), axis=0)
    o = jnp.sum(alpha[..., None] * jnp.stack(outs, axis=0), axis=0)
    y_attn = o.reshape(B, S, ATTN_OUT).astype(h.dtype) @ w_attn_out

    merged = jax.nn.sigmoid(g_conv) * y_conv + jax.nn.sigmoid(g_attn) * y_attn
    return merged @ w_o

def first_inputs(seed: int = 0) -> dict:
    key = jax.random.key(seed)
    ks = jax.random.split(key, 16)
    f32 = jnp.float32

    def nrm(k, shape, fan_in):
        return jax.random.normal(k, shape, f32) * (fan_in ** -0.5)

    return {
        "x": jax.random.normal(ks[0], (BATCH, SEQ, D_MODEL), f32),
        "c": jax.random.normal(ks[1], (BATCH, D_MODEL), f32),
        "ada_w": nrm(ks[2], (DEPTH, D_MODEL, N_SUB * 3 * D_MODEL), D_MODEL),
        "ada_b": 0.02 * jax.random.normal(ks[3], (DEPTH, N_SUB * 3 * D_MODEL), f32),
        "norm_g": 1.0 + 0.05 * jax.random.normal(ks[4], (DEPTH, N_SUB, D_MODEL), f32),
        "ffn_w_gate": nrm(ks[5], (DEPTH, 2, D_MODEL, D_FF), D_MODEL),
        "ffn_w_up": nrm(ks[6], (DEPTH, 2, D_MODEL, D_FF), D_MODEL),
        "ffn_w_down": nrm(ks[7], (DEPTH, 2, D_FF, D_MODEL), D_FF),
        "w_in": nrm(ks[8], (DEPTH, D_MODEL, IN_WIDTH), D_MODEL),
        "conv_w": nrm(ks[9], (DEPTH, CONV_K, CONV_WIDTH), CONV_K),
        "w_conv_out": nrm(ks[10], (DEPTH, CONV_WIDTH, D_MODEL), CONV_WIDTH),
        "w_attn_out": nrm(ks[11], (DEPTH, ATTN_OUT, D_MODEL), ATTN_OUT),
        "w_o": nrm(ks[12], (DEPTH, D_MODEL, D_MODEL), D_MODEL),
        "rel_bias": 0.5 * jax.random.normal(ks[13], (NUM_BUCKETS, N_ATTN_HEADS), f32),
        "final_g": 1.0 + 0.05 * jax.random.normal(ks[14], (D_MODEL,), f32),
    }

def first_block(x, c, ada_w, ada_b, norm_g, ffn_w_gate, ffn_w_up, ffn_w_down, w_in, conv_w,
              w_conv_out, w_attn_out, w_o, rel_bias, final_g):
    cs = jax.nn.silu(c)
    B = c.shape[0]
    for l in range(DEPTH):
        mod = (cs @ ada_w[l] + ada_b[l]).reshape(B, N_SUB, 3, D_MODEL)[:, :, :, None, :]
        h = _rmsnorm(x, norm_g[l, 0]) * (1.0 + mod[:, 0, 1]) + mod[:, 0, 0]
        x = x + 0.5 * mod[:, 0, 2] * _swiglu(h, ffn_w_gate[l, 0], ffn_w_up[l, 0], ffn_w_down[l, 0])
        h = _rmsnorm(x, norm_g[l, 1]) * (1.0 + mod[:, 1, 1]) + mod[:, 1, 0]
        x = x + mod[:, 1, 2] * _mixer(h, w_in[l], conv_w[l], w_conv_out[l], w_attn_out[l], w_o[l], rel_bias)
        h = _rmsnorm(x, norm_g[l, 2]) * (1.0 + mod[:, 2, 1]) + mod[:, 2, 0]
        x = x + 0.5 * mod[:, 2, 2] * _swiglu(h, ffn_w_gate[l, 1], ffn_w_up[l, 1], ffn_w_down[l, 1])
    return _rmsnorm(x, final_g)


MLSTM_INNER = 2 * D_MODEL
MLSTM_HEADS = 4
MLSTM_HEAD_DIM = MLSTM_INNER // MLSTM_HEADS
MLSTM_CONV = 4
QKV_BLOCK = 4
MLSTM_CHUNK = 128
S5_GROUP = 16
S5_GROUPS = D_MODEL // S5_GROUP
S5_STATE = 64
S5_CHUNK = 128
DT_MIN = 0.001
DT_MAX = 0.1
D_FF_2 = 2816
N_EXPERTS = 8
TOP_K = 2
N_EVEN = (DEPTH + 1) // 2
N_ODD = DEPTH // 2
DEEPNORM_ALPHA = (2 * DEPTH) ** 0.25
DEEPNORM_BETA = (8 * DEPTH) ** -0.25
LN_EPS = 1e-5


def layer_norm(x, g, b):
    xf = x.astype(jnp.float32)
    mu = jnp.mean(xf, -1, keepdims=True)
    var = jnp.mean(jnp.square(xf - mu), -1, keepdims=True)
    return ((xf - mu) * lax.rsqrt(var + LN_EPS) * g.astype(jnp.float32) + b.astype(jnp.float32)).astype(x.dtype)

def causal_depthwise_conv(x, w, b):
    K, C = w.shape
    y = lax.conv_general_dilated(x, w[:, None, :].astype(x.dtype), window_strides=(1,), padding=[(K - 1, 0)],
                                 dimension_numbers=('NWC', 'WIO', 'NWC'), feature_group_count=C)
    return y + b

def block_diag_proj(x, w):
    nb, blk, _ = w.shape
    xb = x.reshape(x.shape[:-1] + (nb, blk))
    return jnp.einsum('bsni,nio->bsno', xb, w).reshape(x.shape)

def swiglu(x, w13, w2):
    gate, up = jnp.split(x @ w13, 2, axis=-1)
    return (jax.nn.silu(gate) * up) @ w2

def mlstm_chunkwise(q, k, v, log_i, log_f):
    Bsz, NH, S, DH = q.shape
    L = MLSTM_CHUNK
    NC = S // L

    def chunks(t):
        return jnp.moveaxis(t.reshape((Bsz, NH, NC, L) + t.shape[3:]), 2, 0)

    causal = jnp.tril(jnp.ones((L, L), dtype=bool))

    def step(carry, inp):
        C, n, m = carry
        qc, kc, vc, ic, fc = inp
        b = jnp.cumsum(fc, axis=-1)
        d_log = jnp.where(causal, b[..., :, None] - b[..., None, :] + ic[..., None, :], -jnp.inf)
        inter = b + m[..., None]
        m_t = jnp.maximum(inter, jnp.max(d_log, axis=-1))
        scores = jnp.einsum('bhtd,bhsd->bhts', qc, kc) * jnp.exp(d_log - m_t[..., None])
        dec = jnp.exp(inter - m_t)
        num = jnp.einsum('bhts,bhse->bhte', scores, vc) + dec[..., None] * jnp.einsum('bhtd,bhde->bhte', qc, C)
        den = jnp.sum(scores, -1) + dec * jnp.einsum('bhtd,bhd->bht', qc, n)
        h = num / jnp.maximum(jnp.abs(den), jnp.exp(-m_t))[..., None]
        b_last = b[..., -1]
        g = b_last[..., None] - b + ic
        m_new = jnp.maximum(b_last + m, jnp.max(g, axis=-1))
        wk = jnp.exp(g - m_new[..., None])[..., None] * kc
        dC = jnp.exp(b_last + m - m_new)
        C_new = dC[..., None, None] * C + jnp.einsum('bhsd,bhse->bhde', wk, vc)
        n_new = dC[..., None] * n + jnp.sum(wk, axis=2)
        return (C_new, n_new, m_new), h

    init = (jnp.zeros((Bsz, NH, DH, DH), jnp.float32), jnp.zeros((Bsz, NH, DH), jnp.float32),
            jnp.zeros((Bsz, NH), jnp.float32))
    _, h = lax.scan(step, init, (chunks(q), chunks(k), chunks(v), chunks(log_i), chunks(log_f)))
    return jnp.moveaxis(h, 0, 2).reshape(Bsz, NH, S, DH)

def mlstm_mixer(u, w_in, conv_w, conv_b, wq, wk, wv, w_gates, b_gates, norm_w, skip, w_out):
    Bsz, S, _ = u.shape
    xm, z = jnp.split(u @ w_in, 2, axis=-1)
    xc = jax.nn.silu(causal_depthwise_conv(xm, conv_w, conv_b))
    q = block_diag_proj(xc, wq)
    k = block_diag_proj(xc, wk)
    v = block_diag_proj(xm, wv)
    wg_q, wg_k, wg_v = jnp.split(w_gates, 3, axis=0)
    gates = (q @ wg_q + k @ wg_k + v @ wg_v + b_gates).astype(jnp.float32)
    i_pre, f_pre = jnp.split(gates, 2, axis=-1)
    log_f = jax.nn.log_sigmoid(f_pre)

    def heads(t):
        return t.reshape(Bsz, S, MLSTM_HEADS, MLSTM_HEAD_DIM).transpose(0, 2, 1, 3).astype(jnp.float32)

    h = mlstm_chunkwise(heads(q) * (MLSTM_HEAD_DIM ** -0.5), heads(k), heads(v),
                        i_pre.transpose(0, 2, 1), log_f.transpose(0, 2, 1))
    mu = jnp.mean(h, -1, keepdims=True)
    var = jnp.mean(jnp.square(h - mu), -1, keepdims=True)
    h = ((h - mu) * lax.rsqrt(var + LN_EPS)).transpose(0, 2, 1, 3).reshape(Bsz, S, MLSTM_INNER).astype(u.dtype)
    h = (h * norm_w + skip * xc) * jax.nn.silu(z)
    return h @ w_out

def _complex_affine_combine(e1, e2):
    a1r, a1i, b1r, b1i = e1
    a2r, a2i, b2r, b2i = e2
    return (a2r * a1r - a2i * a1i, a2r * a1i + a2i * a1r,
            a2r * b1r - a2i * b1i + b2r, a2r * b1i + a2i * b1r + b2i)

def s5_mixer(u, lam_re, lam_im, b_re, b_im, c_re, c_im, d_skip, log_dt, w_glu, b_glu):
    Bsz, S, _ = u.shape
    G, P, H = b_re.shape
    L = S5_CHUNK
    NC = S // L
    f32 = lambda t: t.astype(jnp.float32)
    lr, li = f32(lam_re), f32(lam_im)
    dt = jnp.exp(f32(log_dt))[:, None]
    mag = jnp.exp(lr * dt)
    ar, ai = mag * jnp.cos(li * dt), mag * jnp.sin(li * dt)
    den = lr * lr + li * li
    kr = ((ar - 1.0) * lr + ai * li) / den
    ki = (ai * lr - (ar - 1.0) * li) / den
    br, bi = f32(b_re), f32(b_im)
    bbar_re = kr[..., None] * br - ki[..., None] * bi
    bbar_im = kr[..., None] * bi + ki[..., None] * br
    cr, ci = f32(c_re), f32(c_im)
    steps = jnp.arange(1, L + 1, dtype=jnp.float32)[:, None, None]
    pmag = jnp.exp(steps * lr * dt)
    pr = (pmag * jnp.cos(steps * li * dt))[:, None]
    pi_ = (pmag * jnp.sin(steps * li * dt))[:, None]
    uf = f32(u).reshape(Bsz, NC, L, G, H).transpose(1, 2, 0, 3, 4)

    def step(carry, uc):
        xr0, xi0 = carry
        bur = jnp.einsum('lbgh,gph->lbgp', uc, bbar_re)
        bui = jnp.einsum('lbgh,gph->lbgp', uc, bbar_im)
        a_r = jnp.broadcast_to(ar, bur.shape)
        a_i = jnp.broadcast_to(ai, bur.shape)
        _, _, sr, si = lax.associative_scan(_complex_affine_combine, (a_r, a_i, bur, bui), axis=0)
        xr = pr * xr0 - pi_ * xi0 + sr
        xi = pr * xi0 + pi_ * xr0 + si
        y = jnp.einsum('ghp,lbgp->lbgh', cr, xr) - jnp.einsum('ghp,lbgp->lbgh', ci, xi)
        return (xr[-1], xi[-1]), y

    init = (jnp.zeros((Bsz, G, P), jnp.float32), jnp.zeros((Bsz, G, P), jnp.float32))
    _, y = lax.scan(step, init, uf)
    y = y.transpose(2, 0, 1, 3, 4).reshape(Bsz, S, G * H) + f32(d_skip) * f32(u)
    g = jax.nn.gelu(y).astype(u.dtype)
    val, gate = jnp.split(g @ w_glu + b_glu, 2, axis=-1)
    return val * jax.nn.sigmoid(gate)

def moe_ffn(u, w_router, w13, w2):
    Bsz, S, D = u.shape
    t = u.reshape(-1, D)
    logits = (t @ w_router).astype(jnp.float32)
    top_val, top_idx = lax.top_k(logits, TOP_K)
    top_w = jax.nn.softmax(top_val, axis=-1)
    out = jnp.zeros_like(t)
    for e in range(N_EXPERTS):
        gate_e = jnp.sum(jnp.where(top_idx == e, top_w, 0.0), axis=-1).astype(t.dtype)
        out = out + gate_e[:, None] * swiglu(t, w13[e], w2[e])
    return out.reshape(Bsz, S, D)

def second_inputs(seed: int = 0) -> dict:
    key = jax.random.key(seed)
    ks = iter(jax.random.split(key, 40))
    f32 = jnp.float32

    def nrm(shape, std):
        return std * jax.random.normal(next(ks), shape, f32)

    D, Di, NH, G, P, H, F, E = D_MODEL, MLSTM_INNER, MLSTM_HEADS, S5_GROUPS, S5_STATE, S5_GROUP, D_FF_2, N_EXPERTS
    beta = DEEPNORM_BETA
    x = nrm((BATCH, SEQ, D), 1.0)
    c = nrm((BATCH, D), 1.0)
    ada_w = nrm((DEPTH, D, 6 * D), 0.2 * D ** -0.5)
    ada_b = nrm((DEPTH, 6 * D), 0.01)
    ln_mix_g = 1.0 + nrm((DEPTH, D), 0.01)
    ln_mix_b = nrm((DEPTH, D), 0.01)
    ln_ffn_g = 1.0 + nrm((DEPTH, D), 0.01)
    ln_ffn_b = nrm((DEPTH, D), 0.01)
    mlstm_w_in = nrm((N_EVEN, D, 2 * Di), D ** -0.5)
    mlstm_conv_w = nrm((N_EVEN, MLSTM_CONV, Di), MLSTM_CONV ** -0.5)
    mlstm_conv_b = nrm((N_EVEN, Di), 0.01)
    mlstm_wq = nrm((N_EVEN, Di // QKV_BLOCK, QKV_BLOCK, QKV_BLOCK), QKV_BLOCK ** -0.5)
    mlstm_wk = nrm((N_EVEN, Di // QKV_BLOCK, QKV_BLOCK, QKV_BLOCK), QKV_BLOCK ** -0.5)
    mlstm_wv = nrm((N_EVEN, Di // QKV_BLOCK, QKV_BLOCK, QKV_BLOCK), QKV_BLOCK ** -0.5)
    mlstm_w_gates = nrm((N_EVEN, 3 * Di, 2 * NH), (3 * Di) ** -0.5)
    mlstm_b_gates = jnp.concatenate([nrm((N_EVEN, NH), 0.1),
                                     jnp.linspace(3.0, 6.0, NH, dtype=f32)[None] + nrm((N_EVEN, NH), 0.01)], axis=-1)
    mlstm_norm_w = 1.0 + nrm((N_EVEN, Di), 0.01)
    mlstm_skip = 1.0 + nrm((N_EVEN, Di), 0.01)
    mlstm_w_out = nrm((N_EVEN, Di, D), beta * Di ** -0.5)
    ffn_w13 = nrm((N_EVEN, D, 2 * F), D ** -0.5)
    ffn_w2 = nrm((N_EVEN, F, D), beta * F ** -0.5)
    s5_lambda_re = -0.5 + nrm((N_ODD, G, P), 0.01)
    s5_lambda_im = jnp.tile((math.pi * jnp.arange(P, dtype=f32))[None, None, :], (N_ODD, G, 1))
    s5_b_re = nrm((N_ODD, G, P, H), (2 * H) ** -0.5)
    s5_b_im = nrm((N_ODD, G, P, H), (2 * H) ** -0.5)
    s5_c_re = nrm((N_ODD, G, H, P), (2 * P) ** -0.5)
    s5_c_im = nrm((N_ODD, G, H, P), (2 * P) ** -0.5)
    s5_d = nrm((N_ODD, D), 1.0)
    s5_log_dt = jax.random.uniform(next(ks), (N_ODD, G), f32, math.log(DT_MIN), math.log(DT_MAX))
    s5_w_glu = jnp.concatenate([nrm((N_ODD, D, D), beta * D ** -0.5), nrm((N_ODD, D, D), D ** -0.5)], axis=-1)
    s5_b_glu = nrm((N_ODD, 2 * D), 0.01)
    moe_router = nrm((N_ODD, D, E), D ** -0.5)
    moe_w13 = nrm((N_ODD, E, D, 2 * F), D ** -0.5)
    moe_w2 = nrm((N_ODD, E, F, D), beta * F ** -0.5)
    return {"x": x, "c": c, "ada_w": ada_w, "ada_b": ada_b, "ln_mix_g": ln_mix_g, "ln_mix_b": ln_mix_b,
            "ln_ffn_g": ln_ffn_g, "ln_ffn_b": ln_ffn_b,
            "mlstm_w_in": mlstm_w_in, "mlstm_conv_w": mlstm_conv_w, "mlstm_conv_b": mlstm_conv_b,
            "mlstm_wq": mlstm_wq, "mlstm_wk": mlstm_wk, "mlstm_wv": mlstm_wv, "mlstm_w_gates": mlstm_w_gates,
            "mlstm_b_gates": mlstm_b_gates, "mlstm_norm_w": mlstm_norm_w, "mlstm_skip": mlstm_skip,
            "mlstm_w_out": mlstm_w_out, "ffn_w13": ffn_w13, "ffn_w2": ffn_w2,
            "s5_lambda_re": s5_lambda_re, "s5_lambda_im": s5_lambda_im, "s5_b_re": s5_b_re, "s5_b_im": s5_b_im,
            "s5_c_re": s5_c_re, "s5_c_im": s5_c_im, "s5_d": s5_d, "s5_log_dt": s5_log_dt,
            "s5_w_glu": s5_w_glu, "s5_b_glu": s5_b_glu,
            "moe_router": moe_router, "moe_w13": moe_w13, "moe_w2": moe_w2}

def second_block(x, c, ada_w, ada_b, ln_mix_g, ln_mix_b, ln_ffn_g, ln_ffn_b,
              mlstm_w_in, mlstm_conv_w, mlstm_conv_b, mlstm_wq, mlstm_wk, mlstm_wv, mlstm_w_gates,
              mlstm_b_gates, mlstm_norm_w, mlstm_skip, mlstm_w_out, ffn_w13, ffn_w2,
              s5_lambda_re, s5_lambda_im, s5_b_re, s5_b_im, s5_c_re, s5_c_im, s5_d, s5_log_dt,
              s5_w_glu, s5_b_glu, moe_router, moe_w13, moe_w2):
    cond = jax.nn.silu(c)
    for i in range(DEPTH):
        j = i // 2
        mod = cond @ ada_w[i] + ada_b[i]
        sh_m, sc_m, g_m, sh_f, sc_f, g_f = [t[:, None, :] for t in jnp.split(mod, 6, axis=-1)]
        u = x * (1.0 + sc_m) + sh_m
        if i % 2 == 0:
            y = mlstm_mixer(u, mlstm_w_in[j], mlstm_conv_w[j], mlstm_conv_b[j], mlstm_wq[j], mlstm_wk[j],
                            mlstm_wv[j], mlstm_w_gates[j], mlstm_b_gates[j], mlstm_norm_w[j], mlstm_skip[j],
                            mlstm_w_out[j])
        else:
            y = s5_mixer(u, s5_lambda_re[j], s5_lambda_im[j], s5_b_re[j], s5_b_im[j], s5_c_re[j], s5_c_im[j],
                         s5_d[j], s5_log_dt[j], s5_w_glu[j], s5_b_glu[j])
        x = layer_norm(DEEPNORM_ALPHA * x + (1.0 + g_m) * y, ln_mix_g[i], ln_mix_b[i])
        u = x * (1.0 + sc_f) + sh_f
        if i % 2 == 0:
            y = swiglu(u, ffn_w13[j], ffn_w2[j])
        else:
            y = moe_ffn(u, moe_router[j], moe_w13[j], moe_w2[j])
        x = layer_norm(DEEPNORM_ALPHA * x + (1.0 + g_f) * y, ln_ffn_g[i], ln_ffn_b[i])
    return x


def setup_inputs(seed=0):
    out = dict(first_inputs(seed))
    for name, value in second_inputs(seed + 1).items():
        if name != "x":
            out[name + "_2"] = value
    return out


def reference(
    x, c, ada_w, ada_b, norm_g, ffn_w_gate, ffn_w_up, ffn_w_down, w_in, conv_w, w_conv_out,
    w_attn_out, w_o, rel_bias, final_g, c_2, ada_w_2, ada_b_2, ln_mix_g_2, ln_mix_b_2,
    ln_ffn_g_2, ln_ffn_b_2, mlstm_w_in_2, mlstm_conv_w_2, mlstm_conv_b_2, mlstm_wq_2,
    mlstm_wk_2, mlstm_wv_2, mlstm_w_gates_2, mlstm_b_gates_2, mlstm_norm_w_2, mlstm_skip_2,
    mlstm_w_out_2, ffn_w13_2, ffn_w2_2, s5_lambda_re_2, s5_lambda_im_2, s5_b_re_2, s5_b_im_2,
    s5_c_re_2, s5_c_im_2, s5_d_2, s5_log_dt_2, s5_w_glu_2, s5_b_glu_2, moe_router_2, moe_w13_2,
    moe_w2_2,
):
    x = first_block(
        x, c, ada_w, ada_b, norm_g, ffn_w_gate, ffn_w_up, ffn_w_down, w_in, conv_w, w_conv_out,
        w_attn_out, w_o, rel_bias, final_g,
    )
    return second_block(
        x, c_2, ada_w_2, ada_b_2, ln_mix_g_2, ln_mix_b_2, ln_ffn_g_2, ln_ffn_b_2, mlstm_w_in_2,
        mlstm_conv_w_2, mlstm_conv_b_2, mlstm_wq_2, mlstm_wk_2, mlstm_wv_2, mlstm_w_gates_2,
        mlstm_b_gates_2, mlstm_norm_w_2, mlstm_skip_2, mlstm_w_out_2, ffn_w13_2, ffn_w2_2,
        s5_lambda_re_2, s5_lambda_im_2, s5_b_re_2, s5_b_im_2, s5_c_re_2, s5_c_im_2, s5_d_2,
        s5_log_dt_2, s5_w_glu_2, s5_b_glu_2, moe_router_2, moe_w13_2, moe_w2_2,
    )


_drawn_inputs = setup_inputs


def setup_inputs(seed=0):
    import zlib

    import numpy as np

    out = dict(_drawn_inputs(seed))
    spreads = {}
    factors = {'ada_b_2': 3.736,
     'ln_mix_g_2': 3.49,
     'ln_mix_b_2': 3.45,
     'ln_ffn_g_2': 3.708,
     'ln_ffn_b_2': 3.578,
     'mlstm_conv_b_2': 8.0,
     'mlstm_norm_w_2': 8.0,
     'mlstm_skip_2': 8.0,
     's5_lambda_re_2': 64.0,
     's5_lambda_im_2': 64.0,
     's5_b_re_2': 64.0,
     's5_b_im_2': 62.944,
     's5_c_re_2': 41.848,
     's5_c_im_2': 59.536,
     's5_log_dt_2': 60.096,
     's5_b_glu_2': 8.0}
    for name, (base, spread) in spreads.items():
        noise = np.random.default_rng([zlib.crc32(name.encode()), seed]).standard_normal(out[name].shape)
        drawn = base * np.exp(spread * noise) if base else spread * noise
        out[name] = __import__('jax').numpy.asarray(drawn.astype(out[name].dtype))
    for name, factor in factors.items():
        out[name] = (out[name] * factor).astype(out[name].dtype)
    return out
```

```python
from contextlib import ExitStack

import numpy as np

import concourse.bass as bass
from concourse import mybir

F32 = mybir.dt.float32
U32 = mybir.dt.uint32
ALU = mybir.AluOpType
ACT = mybir.ActivationFunctionType
AX = mybir.AxisListType.X

P = 128
D = 1024
S = 256
DEPTH = 2
DT = D // P
TT = S // P
FT = 22
HD = 64
HG = 8
NG = 3
WINDOWS = ((128, 1), (512, 4), (2048, 16))
BUCKETS = 32
MAX_DISTANCE = 2048
QT = NG * HG * HD // P
VW = NG * HG * HD
MT = 16
MH = 4
MK = 4
MC = 4
ST = 32
NE = 8
EPS = 1e-6
LN_EPS = 1e-5
NEG = -1e30
ALPHA = (2 * DEPTH) ** 0.25
PI2 = 2.0 * np.pi
SIN_SCALE = 6.283185
PI2_A = 6.28125
PI2_B = 0.00193500518798828125
PI2_C = PI2 - PI2_A - PI2_B
ROUND = 1.5 * 2.0 ** 23

SLOTS = 3
WIDE = 2 * FT * P
BANKS = 8
LIN = 4


class Linear:

    def __init__(self, chunks, groups, width, source, adas=0, **also):
        self.chunks, self.groups, self.width, self.source = chunks, groups, width, source
        self.adas, self.also = adas, also
        self.full, self.free = [0] * LIN, [0] * LIN
        self.at = []
        for j in range(chunks):
            row = []
            for m in range(groups):
                b = (j * groups + m) % LIN
                row.append((b, self.full[b], self.free[b]))
                self.free[b] += 1
                if m < groups - 1:
                    self.full[b] += 1
            self.at.append(row)
            if j == SLOTS - 1:
                self.per_full, self.per_free = list(self.full), list(self.free)
        self.order = [(kind, n) for n in range(max(chunks, adas))
                      for kind, many in (("ada", adas), ("main", chunks)) if n < many]
        both = bool(chunks and adas)
        self.rounds = (min(chunks, adas) if both else max(chunks, adas)) // SLOTS
        self.step = 2 if both else 1

    def counts(self):
        c = {"chunk": self.chunks + self.adas, "of " + self.source: self.chunks, **self.also}
        for b in range(LIN):
            c[f"full{b}"] = self.full[b]
            c[f"free{b}"] = self.free[b]
        if self.adas:
            c.update({"of ada": self.adas, "ada_cols": self.adas, "free4": 1})
        return c


def uses(**banks):
    c = {}
    for name, n in banks.items():
        c[f"full{name[1:]}"] = n
        c[f"free{name[1:]}"] = n
    return c


def with_(counts, **more):
    return {**counts, **more}


def stages():
    up = lambda src, adas=0: Linear(11, 4, 32 * P, src, adas)
    down = lambda src: Linear(4, 2, 44 * P, src)
    norm = with_(uses(b5=1), squares=1, root=1, h=1)
    ln = with_(uses(b5=1, b6=1), mean=1, squares=1, root=1, h=1)
    logits = with_(uses(b4=4, b5=4), maxima=1, probs=HG, bias_in=16)
    mix = uses(b4=4, b5=4, b6=1, b7=1)
    prologue = {
        "load_x": uses(b0=1, b1=1, b2=1, b3=1),
        "bias_rows": uses(b4=1),
        "ada0": Linear(0, 4, 32 * P, "none", adas=6),
    }
    layer = {
        "norm0": norm, "up0": up("up", 6), "down0": down("down"),
        "norm1": norm,
        "qk": Linear(6, 4, 32 * P, "w_qk", 6), "v": Linear(3, 4, 32 * P, "w_v"),
        "logits0": logits,
        "ccch": Linear(4, 4, 32 * P, "w_ccch"),
        "mix0": mix, "logits1": logits,
        "cb": Linear(2, 4, 32 * P, "w_cb"), "gate_a": Linear(2, 4, 32 * P, "w_gates"),
        "mix1": mix, "logits2": logits,
        "gate_b": Linear(2, 4, 32 * P, "w_gates"), "conv_out": Linear(2, 4, 32 * P, "w_conv_out"),
        "mix2": mix, "combine": with_(uses(b6=1, b7=1), shift=1, weights=1, mixed=1),
        "attn_out": Linear(1, 8, 32 * P, "w_attn_out", merged=1),
        "wo": Linear(2, 4, 32 * P, "w_o"),
        "norm2": norm, "up2": up("up", 6), "down2": down("down"),
    }
    second = {
        "final_norm": with_(norm, h=0),
        "mod3": {"h": 1},
        "xm": Linear(4, 4, 32 * P, "m_xm", 3), "z": Linear(4, 4, 32 * P, "m_z", 3),
        "mconv": {"conv": MT, "xc": 1},
        "q": Linear(1, 16, 16 * P, "m_q"), "k": Linear(1, 16, 16 * P, "m_k"),
        "vT": Linear(1, 16, 16 * P, "m_v"), "vtok": Linear(1, 8, 16 * P, "m_v_again"),
        "gates": with_(uses(b4=1, b5=1), gate_logs=1, rows=1),
        "rows_t": with_(uses(b4=1, b5=1, b6=1), floor=1, decays=1),
        "scores": uses(b0=1, b1=1, b2=1, b3=1),
        "numer": with_(uses(b0=2, b1=2, b2=2, b3=2, b7=1), mvar=1, mroot=1, hn=1),
        "h_t": with_(uses(b0=2, b1=2, b2=2, b3=2), mh=1),
        "m_out": Linear(4, 2, 32 * P, "m_out"), "ln0": ln,
        "up3": up("up_3", 12), "down3": down("down_3"),
        "ln1": ln,
        "s5_b": with_(uses(b0=1, b1=1, b2=1, b3=1), s5_dt=1, s5_turns=1, s5_trig=1, s5_bar=1),
        "s5": with_(uses(b0=DT, b1=DT, b2=DT, b3=DT, b4=DT), turns=DT, waves=DT,
                    sums=DT, back=DT, reals=DT, states=DT),
        "s5_gelu": {"y": 1, "gelu": 1},
        "glu": Linear(4, 4, 32 * P, "glu"), "ln2": ln,
        "router": with_(uses(b4=1, b5=1), top=1, ratio=1, gate=1),
        "spread": uses(b0=1, b1=1, b2=1, b3=1),
    }
    expert = {"upE": up("up_e"), "downE": down("down_e")}
    epilogue = {"ln3": ln, "store": uses(b0=1, b1=1, b2=1, b3=1)}
    return [(prologue, 1), (layer, DEPTH), (second, 1), (expert, NE), (epilogue, 1)]


class Plan:

    def __init__(self):
        self.stage, self.base, self.period = {}, {}, {}
        total = {}
        for part, times in stages():
            start, run = dict(total), dict(total)
            for name, what in part.items():
                self.stage[name] = what
                self.base[name] = dict(run)
                for k, n in (what.counts() if isinstance(what, Linear) else what).items():
                    run[k] = run.get(k, 0) + n
            period = {k: n - start.get(k, 0) for k, n in run.items()}
            if times > 1:
                assert period["chunk"] % SLOTS == 0
            for name in part:
                self.period[name] = period
            total = {k: start.get(k, 0) + n * times for k, n in period.items()}
        self.total = total


class Place:

    def __init__(self, plan, name, rep=0):
        self.name, self.what, self.rep = name, plan.stage[name], rep
        self.base, self.period = plan.base[name], plan.period[name]

    def of(self, signal, k=0, i=0, per=0):
        n = self.base.get(signal, 0) + k
        for reg, step in ((self.rep, self.period.get(signal, 0)), (i, per)):
            if isinstance(reg, int):
                n = n + reg * step
            elif step:
                n = reg * step + n
        return n

    def slot(self, pos, i=0, step=1):
        n = self.base.get("chunk", 0) + pos
        use = n // SLOTS
        for reg, per in ((self.rep, self.period["chunk"] // SLOTS), (i, step)):
            if isinstance(reg, int):
                use = use + reg * per
            elif per:
                use = reg * per + use
        return n % SLOTS, use


def walk(p, loop, main=None, ada=None):
    lin, do = p.what, {"main": main, "ada": ada}
    first = SLOTS * lin.step * lin.rounds
    if lin.rounds > 1:
        for i in loop(lin.rounds):
            for pos, (kind, n) in enumerate(lin.order[:SLOTS * lin.step]):
                if do[kind]:
                    do[kind](n, i, p.slot(pos, i, lin.step))
    else:
        first = 0
    for pos, (kind, n) in enumerate(lin.order):
        if pos >= first and do[kind]:
            do[kind](n, 0, p.slot(pos))


def loop_on(eng):
    def loop(times):
        with eng.Fori(0, times) as i:
            yield i
    return loop


def at(i, step, k):
    return i * step + k if not isinstance(i, int) else i * step + k


class Steps:

    def __init__(self, eng, periods):
        self.eng, self.periods = eng, periods
        self.n, self.rounds = 0, []

    def one(self):
        self.n += 1
        return 1

    def count(self):
        n = self.n
        for reg, step in self.rounds:
            n = reg * step + n
        return n

    def loop(self, name, times):
        with self.eng.Fori(0, times) as i:
            start = self.n
            self.rounds.append((i, self.periods.get(name, 1)))
            yield i
            self.rounds.pop()
            self.periods[name] = self.n - start
        self.n = start + self.periods[name] * times


def vector_columns():
    cols, n = {}, 0
    for name, k in (("c", DT), ("c_2", DT), ("ada_b", DEPTH * 9 * DT), ("ada_b_2", DEPTH * 6 * DT),
                    ("norm_g", DEPTH * 3 * DT),
                    ("conv_w", DEPTH * 3 * DT), ("final_g", DT),
                    ("ln_mix_g_2", DEPTH * DT), ("ln_mix_b_2", DEPTH * DT), ("ln_ffn_g_2", DEPTH * DT),
                    ("ln_ffn_b_2", DEPTH * DT), ("mlstm_conv_w_2", MC * MT), ("mlstm_conv_b_2", MT),
                    ("mlstm_norm_w_2", MT), ("mlstm_skip_2", MT), ("s5_d_2", DT),
                    ("s5_b_glu_2", 2 * DT), ("s5_lambda_re_2", ST), ("s5_lambda_im_2", ST),
                    ("s5_log_dt_2", ST)):
        cols[name] = n
        n += k
    return cols, n


VEC, VECS = vector_columns()


def build(nc, dram, out, periods):
    plan = Plan()
    with ExitStack() as ctx:
        sb = lambda name, shape, dt=F32: ctx.enter_context(nc.sbuf_tensor(name, shape, dt))
        sem = lambda name: ctx.enter_context(nc.semaphore(name))

        psum = ctx.enter_context(nc.psum_tensor("psum", [P, BANKS * 512], F32))
        bank = lambda b: psum[:, b * 512:(b + 1) * 512]
        half = lambda b, k=0: psum[:, b * 512 + k * S:b * 512 + (k + 1) * S]

        ring = sb("ring", [P, SLOTS, WIDE])
        x = sb("x_t", [P, DT, S])
        h = sb("h_t", [P, DT, S])
        work = sb("work", [P, 112 * S])
        vec = sb("vec", [P, VECS])
        ident = sb("ident", [P, P])
        ones = sb("ones", [P, P])
        cond = sb("cond", [P, 2 * DT])
        lvec = sb("lvec", [P, 6 * DT])
        mod = sb("mod", [P, 6 * DT])
        mod_next = sb("mod_next", [P, 6 * DT])
        ada_sum = sb("ada_sum", [P, SLOTS, 512])
        mod1 = sb("mod1", [P, 6 * DT])
        gain = sb("gain", [P, DT])
        rms = sb("rms", [P, S])
        small = sb("small", [P, 256])
        att = sb("att", [P, 5, NG, TT * HG])
        bgate = sb("bgate", [P, TT * 2 * MH])
        iota8 = sb("iota8", [P, NE])
        index8 = sb("index8", [P, TT, NE], U32)

        def tiles(a, n):
            return work[:, a * S:(a + n) * S].rearrange("p (t s) -> p t s", s=S)

        def flat(a, n):
            return work[:, a * S:(a + n) * S]

        vcol = lambda name, k=0, n=1: vec[:, VEC[name] + k:VEC[name] + k + n]

        mid, act2 = tiles(0, FT), tiles(FT, 2)
        qk = tiles(0, 2 * QT)
        vtok = flat(24, 12).rearrange("p (t n) -> p t n", t=TT)
        logit = flat(36, 12).rearrange("p (h n) -> p h n", h=HG)
        prob_t = flat(48, 12).rearrange("p (h n) -> p h n", h=HG)
        o_g = flat(60, 12).rearrange("p (g t n) -> p g t n", g=NG, t=TT)
        u_t, conv_t, sig_c, sig_a = tiles(72, DT), tiles(80, DT), tiles(88, DT), tiles(96, DT)
        bias = flat(104, 8).rearrange("p (h n) -> p h n", h=HG)
        cc2 = tiles(48, 2)
        o_tok = flat(36, 4).rearrange("p (t n) -> p t n", t=TT)
        o_t = tiles(40, 4)
        merged = u_t
        xm, zs, xc = tiles(0, MT), tiles(16, MT), tiles(32, MT)
        mq, mk, mvt = tiles(48, MT), tiles(64, MT), tiles(80, MT)
        mv = flat(96, MT).rearrange("p (t n) -> p t n", t=TT)
        decay = flat(0, 6).rearrange("p (h n) -> p h n", h=MH)
        score = flat(6, 6).rearrange("p (h n) -> p h n", h=MH)
        row = lambda k: work[0:MH, (12 + k) * S:(13 + k) * S] if k < 4 else work[0:MH, (76 + k) * S:(77 + k) * S]
        hn = flat(80, MT).rearrange("p (t n) -> p t n", t=TT)
        mh = tiles(0, MT)
        tri = flat(10, 1)[:, 0:P]
        w_gate_m = flat(8, 2)[:, 0:3 * MT * 2 * MH].rearrange("p (k n) -> p k n", n=2 * MH)
        b_re, b_im = flat(0, 4), flat(4, 4)
        c_re, c_im = flat(8, 4), flat(12, 4)
        bar_re, bar_im = flat(16, 4), flat(20, 4)
        bar_t = flat(24, 8).rearrange("p (r f n) -> p r f n", r=2, f=DT)
        time = flat(34, 1)
        quad = lambda a: tiles(a, 4)
        turn, turn4, wave_s, wave_c = quad(36), quad(40), quad(44), quad(48)
        pr = [quad(52 + 4 * k) for k in range(4)]
        sum_r, sum_i, st_r, st_i = quad(68), quad(72), quad(76), quad(80)
        xs_r, xs_i, near = quad(84), quad(88), quad(92)
        y_t = tiles(96, DT)
        s5s = flat(104, 3).rearrange("p (k n) -> p k n", n=ST)
        val2 = tiles(110, 2)
        spread_g, acc, y2 = tiles(24, NE), tiles(32, DT), tiles(40, 2)
        w_router = flat(42, 1)[:, 0:DT * NE].rearrange("p (k n) -> p k n", n=NE)
        x_tok = flat(0, 8).rearrange("p (t n) -> p t n", t=TT)
        y_tok = flat(44, 8).rearrange("p (t n) -> p t n", t=TT)
        one_hot = work[0:BUCKETS, 8 * S:8 * S + 383]
        off_mask = work[0:NG * HG, 10 * S:10 * S + 383]
        table = work[0:BUCKETS, 12 * S:12 * S + NG * HG]
        bias_row = work[0:NG * HG, 13 * S:13 * S + 384]

        signal = {k: sem(k.replace(" ", "_")) for k in sorted(plan.total)
                  if k != "chunk" and not k.startswith("of ")}
        bank_free = [signal[f"free{b}"] for b in range(BANKS)]
        bank_full = [signal[f"full{b}"] for b in range(BANKS)]
        chunk_in = [sem(f"chunk_in{s}") for s in range(SLOTS)]
        chunk_done = [sem(f"chunk_done{s}") for s in range(SLOTS)]
        small_in = sem("small_in")
        ones_set = sem("ones_set")
        cond_set = sem("cond_set")
        rows_out = sem("rows_out")
        table_out = sem("table_out")
        s5_in = sem("s5_in")
        route_in = sem("route_in")
        mgate_in = sem("mgate_in")
        y_set_act = sem("y_set_act")
        y_set_dve = sem("y_set_dve")
        stored = sem("stored")
        x_summed = sem("x_summed")
        act_done = sem("act_done")
        dve_done = sem("dve_done")
        pool_done = sem("pool_done")




        block = ctx.enter_context(nc.Block())

        def place(name, rep=0):
            return Place(plan, name, rep)

        def reads(p, b, k=0, i=0, per=0):
            return p.of(f"free{b}", k + 1, i, per)

        def products(p, b, k=0, i=0, per=0):
            return p.of(f"full{b}", k + 1, i, per)

        def group_end(p, j, m, i, where):
            if m == p.what.groups - 1:
                return chunk_done[where[0]], where[1] + 2
            b, k, _ = p.what.at[j][m]
            return bank_full[b], products(p, b, k, i, 0 if isinstance(i, int) else p.what.per_full[b])






        @block.sync
        def _(sp):
            for dst, src in ((x_tok, dram["x"]), (ident[:, :], dram["ident"]), (vec[:, :], dram["vec"]),
                             (one_hot, dram["one_hot"]), (off_mask, dram["off_mask"]),
                             (table, dram["rel_bias"]),
                             (bgate[:, :], dram["b_gates"]),
                             (iota8[:, :], dram["iota8"])):
                sp.dma_start(dst, src).then_inc(small_in, 16)

            def stream(p):
                def load(source, width):
                    def chunk(n, i, where):
                        slot, use = where
                        src = dram[source][p.of("of " + source, n, i, SLOTS)]
                        sp.wait_ge(chunk_done[slot], use + 1)
                        sp.dma_start(ring[:, slot, 0:width], src).then_inc(chunk_in[slot], 16)
                    return chunk

                walk(p, loop_on(sp), load(p.what.source, p.what.width), load("ada", 32 * P))

            for part, times in stages():
                names = [n for n in part if isinstance(plan.stage[n], Linear)]
                if not names:
                    continue
                if times > 1:
                    with sp.Fori(0, times) as rep:
                        for n in names:
                            stream(place(n, rep))
                else:
                    for n in names:
                        stream(place(n))
            sp.wait_ge(y_set_act, 2)
            sp.wait_ge(y_set_dve, 2)
            sp.dma_start(out.rearrange("b (t p) d -> p (b t) d", p=P), y_tok).then_inc(stored, 16)
            sp.wait_ge(stored, 16)

        @block.tensor
        def _(pe):
            loop = loop_on(pe)

            def chunk_landed(where):
                slot, use = where
                pe.wait_ge(chunk_in[slot], use * 16 + 16)
                return slot

            def close(ins, p, j, m, slot):
                b = p.what.at[j][m][0]
                if m == p.what.groups - 1:
                    ins.then_inc(chunk_done[slot], 1)
                else:
                    ins.then_inc(signal[f"full{b}"], 1)

            def linear(p, moving, ready=None):
                lin = p.what
                depth = lin.width // P // lin.groups
                carried.update(p=p, main=lin.chunks)

                def chunk(j, i, where):
                    if j == 0 and ready:
                        pe.wait_ge(signal["h"], ready.of("h", 1))
                    slot = chunk_landed(where)
                    for m in range(lin.groups):
                        b, _, k_free = lin.at[j][m]
                        pe.wait_ge(bank_free[b], reads(p, b, k_free, i, 0 if isinstance(i, int) else lin.per_free[b]))
                        for k in range(depth):
                            w = ring[:, slot, (m * depth + k) * P:(m * depth + k + 1) * P]
                            mm = pe.matmul(half(b), w, moving(k, j * lin.groups + m), start=(k == 0),
                                           stop=(k == depth - 1))
                        close(mm, p, j, m, slot)
                    if j < lin.adas:
                        ada(p, j, i)

                walk(p, loop, chunk, ada_where)

            carried = {}

            def ada_where(n, i, where):
                carried[n] = where
                if n >= carried["main"]:
                    ada(carried["p"], n, i)

            def ada(p, n, i):
                if n == 0:
                    pe.wait_ge(bank_free[4], reads(p, 4))
                slot, use = carried[n]
                pe.wait_ge(chunk_done[slot], use + 2)
                for m in range(4):
                    c = 4 * 512 + n * 4 + m
                    o = psum[:, c:c + 1] if isinstance(i, int) else psum[:, bass.ds(i * 12 + c, 1)]
                    mm = pe.matmul(o, ada_sum[:, n % SLOTS, m * P:(m + 1) * P], ones[:, 0:1],
                                   start=True, stop=True)
                mm.then_inc(signal["ada_cols"], 1)

            def over_features(b, src):
                for k in range(DT):
                    mm = pe.matmul(half(b), ones[:, :], src[:, k, :], start=(k == 0), stop=(k == DT - 1))
                mm.then_inc(signal[f"full{b}"], 1)

            def norm(p):
                pe.wait_ge(signal["squares"], p.of("squares", 1))
                pe.wait_ge(bank_free[5], reads(p, 5))
                over_features(5, h)

            def layer_norm(p):
                for b in range(LIN):
                    pe.wait_ge(bank_free[b], reads(p, b))
                if p.name in ("ln2", "ln3"):
                    pe.wait_ge(x_summed, 1 if p.name == "ln2" else 2)
                pe.wait_ge(bank_free[5], reads(p, 5))
                over_features(5, x)
                pe.wait_ge(signal["squares"], p.of("squares", 1))
                pe.wait_ge(bank_free[6], reads(p, 6))
                over_features(6, h)

            def ffn(up, down, ready=None):
                linear(up, lambda k, n: h[:, k, :], ready)
                for b in range(LIN):
                    pe.wait_ge(bank_free[b], reads(down, b))
                linear(down, lambda k, n: mid[:, k, :])

            def v_product(p):
                for j in range(3):
                    slot = chunk_landed(p.slot(j))
                    for m in range(4):
                        b, _, k_free = p.what.at[j][m]
                        t, n = m // 2, m % 2
                        pe.wait_ge(bank_free[b], reads(p, b, k_free))
                        for k in range(DT):
                            mm = pe.matmul(half(b), h[:, k, t * P:(t + 1) * P],
                                           ring[:, slot, k * 512 + n * S:k * 512 + (n + 1) * S],
                                           start=(k == 0), stop=(k == DT - 1))
                        close(mm, p, j, m, slot)

            def logits(p, g):
                for n in range(HG):
                    b, off, f = 4 + n % 2, HD * (n % 2), g * HG // 2 + n // 2
                    q, k = qk[off:off + HD, f, :], qk[off:off + HD, QT + f, :]
                    pe.wait_ge(bank_free[b], reads(p, b, n // 2))
                    o = bank(b)
                    pe.matmul(o[:, 0:P], q[:, 0:P], k[:, 0:P], start=True, stop=True)
                    pe.matmul(o[:, P:P + S], q[:, P:S], k, start=True, stop=True)\
                        .then_inc(signal[f"full{b}"], 1)

            def mix(p, g, lp):
                for n in range(HG):
                    b = 4 + n % 2
                    pe.wait_ge(signal["probs"], lp.of("probs", n + 1))
                    pe.wait_ge(bank_free[b], reads(p, b, n // 2))
                    for c in range(3):
                        mm = pe.transpose(bank(b)[:, c * P:(c + 1) * P],
                                          logit[:, n, c * P:(c + 1) * P], ident[:, :])
                    mm.then_inc(signal[f"full{b}"], 1)
                pe.wait_ge(bank_free[4], reads(p, 4, 4))
                pe.wait_ge(bank_free[5], reads(p, 5, 4))
                pe.wait_ge(bank_free[6], reads(p, 6))
                pe.wait_ge(bank_free[7], reads(p, 7))
                for n in range(HG):
                    e = (g * HG + n) * HD
                    mm = pe.matmul(bank(6)[:, n * HD:(n + 1) * HD], prob_t[:, n, 0:P],
                                   vtok[:, 0, e:e + HD], start=True, stop=True)
                mm.then_inc(signal["full6"], 1)
                for n in range(HG):
                    e = (g * HG + n) * HD
                    o = bank(7)[:, n * HD:(n + 1) * HD]
                    pe.matmul(o, prob_t[:, n, P:2 * P], vtok[:, 0, e:e + HD], start=True, stop=False)
                    mm = pe.matmul(o, prob_t[:, n, 2 * P:3 * P], vtok[:, 1, e:e + HD], start=False, stop=True)
                mm.then_inc(signal["full7"], 1)

            def combine(p):
                pe.wait_ge(signal["mixed"], p.of("mixed", 1))
                for f in range(4):
                    b = 6 + f // 2
                    if f % 2 == 0:
                        pe.wait_ge(bank_free[b], reads(p, b))
                    for t in range(TT):
                        c = (f % 2) * S + t * P
                        mm = pe.transpose(bank(b)[:, c:c + P], o_tok[:, t, f * P:(f + 1) * P], ident[:, :])
                    if f % 2:
                        mm.then_inc(signal[f"full{b}"], 1)

            pe.wait_ge(small_in, 128)
            p = place("load_x")
            for f in range(DT):
                b = f // 2
                if f % 2 == 0:
                    pe.wait_ge(bank_free[b], reads(p, b))
                for t in range(TT):
                    c = (f % 2) * S + t * P
                    mm = pe.transpose(bank(b)[:, c:c + P], x_tok[:, t, f * P:(f + 1) * P], ident[:, :])
                if f % 2:
                    mm.then_inc(signal[f"full{b}"], 1)
            p = place("bias_rows")
            pe.wait_ge(bank_free[4], reads(p, 4))
            pe.matmul(psum[0:NG * HG, 4 * 512:4 * 512 + 383], table, one_hot, start=True, stop=True)\
                .then_inc(signal["full4"], 1)
            pe.wait_ge(ones_set, 1)
            linear(place("ada0"), None)

            with pe.Fori(0, DEPTH) as l:
                on = lambda name: place(name, l)
                norm(on("norm0"))
                ffn(on("up0"), on("down0"), on("norm0"))
                norm(on("norm1"))
                linear(on("qk"), lambda k, n: h[:, k, :], on("norm1"))
                v_product(on("v"))
                logits(on("logits0"), 0)
                linear(on("ccch"), lambda k, n: h[:, k, :])
                mix(on("mix0"), 0, on("logits0"))
                logits(on("logits1"), 1)
                linear(on("cb"), lambda k, n: h[:, k, :])
                linear(on("gate_a"), lambda k, n: h[:, k, :])
                mix(on("mix1"), 1, on("logits1"))
                logits(on("logits2"), 2)
                linear(on("gate_b"), lambda k, n: h[:, k, :])
                linear(on("conv_out"), lambda k, n: conv_t[:, k, :])
                mix(on("mix2"), 2, on("logits2"))
                combine(on("combine"))
                pe.wait_ge(bank_free[6], reads(on("attn_out"), 6))
                pe.wait_ge(bank_free[7], reads(on("attn_out"), 7))
                linear(on("attn_out"), lambda k, n: o_t[:, k, :])
                pe.wait_ge(signal["merged"], on("attn_out").of("merged", 1))
                linear(on("wo"), lambda k, n: merged[:, k, :])
                norm(on("norm2"))
                ffn(on("up2"), on("down2"), on("norm2"))

            norm(place("final_norm"))
            pe.wait_ge(signal["h"], place("mod3").of("h", 1))
            linear(place("xm"), lambda k, n: h[:, k, :])
            linear(place("z"), lambda k, n: h[:, k, :])
            pe.wait_ge(signal["xc"], place("mconv").of("xc", 1))
            linear(place("q"), lambda k, n: xc[:, n, :])
            linear(place("k"), lambda k, n: xc[:, n, :])
            linear(place("vT"), lambda k, n: xm[:, n, :])
            p = place("vtok")
            for b in range(LIN):
                pe.wait_ge(bank_free[b], reads(p, b))
            slot = chunk_landed(p.slot(0))
            for t in range(TT):
                for b in range(LIN):
                    m = t * LIN + b
                    pe.wait_ge(bank_free[b], reads(p, b, t))
                    for n in range(4):
                        f = 4 * b + n
                        mm = pe.matmul(bank(b)[:, n * P:(n + 1) * P], xm[:, f, t * P:(t + 1) * P],
                                       ring[:, slot, f * P:(f + 1) * P], start=True, stop=True)
                    close(mm, p, 0, m, slot)
            p = place("gates")
            pe.wait_ge(mgate_in, 32)
            pe.wait_ge(bank_free[4], reads(p, 4))
            for t in range(TT):
                for k in range(3 * MT):
                    src = (mq, mk, mvt)[k // MT][:, k % MT, t * P:(t + 1) * P]
                    mm = pe.matmul(psum[:, 4 * 512 + t * 8:4 * 512 + t * 8 + 8], src, w_gate_m[:, k, :],
                                   start=(k == 0), stop=(k == 3 * MT - 1))
            mm.then_inc(signal["full4"], 1)
            pe.wait_ge(bank_free[4], reads(p, 4, 0) + 1)
            pe.wait_ge(bank_free[5], reads(p, 5))
            gsb = small[:, 0:TT * 2 * MH].rearrange("p (t n) -> p t n", t=TT)
            for n in range(2):
                for t in range(TT):
                    mm = pe.transpose(psum[0:MH, 5 * 512 + n * S + t * P:5 * 512 + n * S + (t + 1) * P],
                                      gsb[:, t, n * MH:(n + 1) * MH], ident[:, :])
            mm.then_inc(signal["full5"], 1)
            pe.wait_ge(signal["rows"], p.of("rows", 1))
            p = place("rows_t")
            pe.wait_ge(bank_free[4], reads(p, 4))
            for n in range(2):
                for t in range(TT):
                    c = 4 * 512 + n * 8 + t * MH
                    mm = pe.transpose(psum[:, c:c + MH], row(5 + n)[:, t * P:(t + 1) * P],
                                      ident[0:MH, 0:MH])
            mm.then_inc(signal["full4"], 1)
            for b in (5, 6):
                pe.wait_ge(bank_free[b], reads(p, b))
                for n in range(2):
                    hd = (b - 5) * 2 + n
                    mm = pe.matmul(half(b, n), ident[0:MH, hd:hd + 1].to_broadcast([MH, P]), row(4), start=True, stop=True)
                mm.then_inc(signal[f"full{b}"], 1)
            p = place("scores")
            for n in range(MH):
                pe.wait_ge(bank_free[n], reads(p, n))
                for c, (a, z, lo) in enumerate(((0, P, 0), (P, S, P))):
                    for k in range(4):
                        mm = pe.matmul(bank(n)[:, c * S:c * S + S - lo], mk[:, 4 * n + k, a:z],
                                       mq[:, 4 * n + k, lo:S], start=(k == 0), stop=(k == 3))
                mm.then_inc(signal[f"full{n}"], 1)
            p = place("numer")
            for b in range(LIN):
                pe.wait_ge(bank_free[b], reads(p, b))
            parts = lambda t: ((0, 0),) if t == 0 else ((P, 0), (S, 1))
            pe.wait_ge(bank_free[7], reads(p, 7))
            for n in range(MH):
                for t in range(TT):
                    for q, (c, s_t) in enumerate(parts(t)):
                        mm = pe.matmul(psum[:, 7 * 512 + t * MH + n:7 * 512 + t * MH + n + 1],
                                       score[:, n, c:c + P], ones[:, 0:1], start=(q == 0),
                                       stop=(q == len(parts(t)) - 1))
            mm.then_inc(signal["full7"], 1)
            for n in range(MH):
                for t in range(TT):
                    b, u = (2 * n + t) % LIN, (2 * n + t) // LIN
                    pe.wait_ge(bank_free[b], reads(p, b, u))
                    for q, (c, s_t) in enumerate(parts(t)):
                        mm = pe.matmul(bank(b), score[:, n, c:c + P], mv[:, s_t, n * 512:(n + 1) * 512],
                                       start=(q == 0), stop=(q == len(parts(t)) - 1))
                    mm.then_inc(signal[f"full{b}"], 1)
            pe.wait_ge(signal["hn"], p.of("hn", 1))
            p = place("h_t")
            for f in range(MT):
                b, u = (f // 2) % LIN, f // 8
                if f % 2 == 0:
                    pe.wait_ge(bank_free[b], reads(p, b, u))
                for t in range(TT):
                    c = (f % 2) * S + t * P
                    mm = pe.transpose(bank(b)[:, c:c + P], hn[:, t, f * P:(f + 1) * P], ident[:, :])
                if f % 2:
                    mm.then_inc(signal[f"full{b}"], 1)
            pe.wait_ge(signal["mh"], p.of("mh", 1))
            linear(place("m_out"), lambda k, n: mh[:, k, :])
            layer_norm(place("ln0"))
            pe.wait_ge(signal["h"], place("ln0").of("h", 1))
            ffn(place("up3"), place("down3"))
            layer_norm(place("ln1"))
            p = place("s5_b")
            pe.wait_ge(signal["s5_bar"], p.of("s5_bar", 1))
            for r, src in enumerate((bar_re, bar_im)):
                for f in range(DT):
                    b, c = 2 * r + f // 4, (f % 4) * P
                    if f % 4 == 0:
                        pe.wait_ge(bank_free[b], reads(p, b))
                    mm = pe.transpose(bank(b)[:, c:c + P], src[:, f * P:(f + 1) * P], ident[:, :])
                    if f % 4 == 3:
                        mm.then_inc(signal[f"full{b}"], 1)
            p = place("s5")
            for b in range(LIN):
                pe.wait_ge(bank_free[b], reads(p, b))
            pe.wait_ge(signal["h"], place("ln1").of("h", 1))
            for f in range(DT):
                for j in range(4):
                    rows = slice(32 * j, 32 * j + 32)
                    pe.wait_ge(bank_free[j], reads(p, j, f))
                    for r in range(2):
                        mm = pe.matmul(half(j, r), bar_t[rows, r, f, :], h[rows, f, :], start=True, stop=True)
                    mm.then_inc(signal[f"full{j}"], 1)
                pe.wait_ge(signal["states"], p.of("states", f + 1))
                pe.wait_ge(signal["reals"], p.of("reals", f + 1))
                pe.wait_ge(bank_free[4], reads(p, 4, f))
                for j in range(4):
                    rows = slice(32 * j, 32 * j + 32)
                    o = psum[rows, 4 * 512:4 * 512 + S]
                    pe.matmul(o, c_re[:, f * P + 32 * j:f * P + 32 * j + 32], xs_r[:, j, :], start=True, stop=False)
                    mm = pe.matmul(o, c_im[:, f * P + 32 * j:f * P + 32 * j + 32], xs_i[:, j, :], start=False, stop=True)
                mm.then_inc(signal["full4"], 1)
            pe.wait_ge(signal["gelu"], place("s5_gelu").of("gelu", 1))
            linear(place("glu"), lambda k, n: h[:, k, :])
            layer_norm(place("ln2"))
            p = place("router")
            pe.wait_ge(signal["h"], place("ln2").of("h", 1))
            pe.wait_ge(route_in, 16)
            pe.wait_ge(bank_free[4], reads(p, 4))
            for t in range(TT):
                for k in range(DT):
                    mm = pe.matmul(psum[:, 4 * 512 + t * NE:4 * 512 + (t + 1) * NE], h[:, k, t * P:(t + 1) * P],
                                   w_router[:, k, :], start=(k == 0), stop=(k == DT - 1))
            mm.then_inc(signal["full4"], 1)
            pe.wait_ge(signal["gate"], p.of("gate", 1))
            pe.wait_ge(bank_free[5], reads(p, 5))
            for t in range(TT):
                mm = pe.transpose(psum[0:NE, 5 * 512 + t * P:5 * 512 + (t + 1) * P],
                                  small[:, 64 + t * NE:64 + (t + 1) * NE], ident[:, :])
            mm.then_inc(signal["full5"], 1)
            pe.wait_ge(bank_free[5], reads(p, 5, 0) + 1)
            p = place("spread")
            for e in range(NE):
                b = e // 2
                if e % 2 == 0:
                    pe.wait_ge(bank_free[b], reads(p, b))
                mm = pe.matmul(half(b, e % 2), ident[0:NE, e:e + 1].to_broadcast([NE, P]), rms[0:NE, :], start=True, stop=True)
                if e % 2:
                    mm.then_inc(signal[f"full{b}"], 1)
            with pe.Fori(0, NE) as e:
                ffn(place("upE", e), place("downE", e))
            layer_norm(place("ln3"))
            p = place("store")
            pe.wait_ge(signal["h"], place("ln3").of("h", 1))
            for t in range(TT):
                for f in range(DT):
                    b, c = 2 * t + f // 4, (f % 4) * P
                    if f % 4 == 0:
                        pe.wait_ge(bank_free[b], reads(p, b))
                    mm = pe.transpose(bank(b)[:, c:c + P], x[:, f, t * P:(t + 1) * P], ident[:, :])
                    if f % 4 == 3:
                        mm.then_inc(signal[f"full{b}"], 1)

        @block.scalar
        def _(act):
            steps = Steps(act, periods["act"])

            def evacuate(p, mine, do):
                lin = p.what

                def chunk(j, i, where):
                    for m in mine:
                        b, _, k = lin.at[j][m]
                        act.wait_ge(*group_end(p, j, m, i, where))
                        do(j, m, i, half(b)).then_inc(bank_free[b], 1)

                walk(p, loop_on(act), chunk)

            def gated(p, func, buf, bias_col=None):
                lin = p.what

                def chunk(j, i, where):
                    for m in (0, 2):
                        b, _, k = lin.at[j][m]
                        act.wait_ge(*group_end(p, j, m, i, where))
                        act.wait_ge(bank_free[b + 1], reads(p, b + 1, k, i, 0 if isinstance(i, int) else lin.per_free[b]))
                        act.activation(buf[:, m // 2, :], half(b), func).then_inc(bank_free[b], 1)

                walk(p, loop_on(act), chunk)

            def root(p, b):
                act.wait_ge(bank_free[b], reads(p, b, 0) + 1)
                act.activation(rms[:, :], rms[:, :], ACT.Sqrt).then_inc(signal["root"], 1)

            def norm(p):
                for b in range(LIN):
                    act.wait_ge(bank_free[b], reads(p, b))
                act.activation(h[:, :, :], x[:, :, :], ACT.Square).then_inc(signal["squares"], 1)
                root(p, 5)

            def layer_norm(p):
                act.wait_ge(signal["mean"], p.of("mean", 1))
                act.activation(h[:, :, :], x[:, :, :], ACT.Square).then_inc(signal["squares"], 1)
                root(p, 6)

            def exps(p, g):
                act.wait_ge(signal["maxima"], p.of("maxima", 1))
                for n in range(HG):
                    for t, (a, z) in enumerate(((0, P), (P, P + S))):
                        e = act.activation(logit[:, n, a:z], logit[:, n, a:z], ACT.Exp,
                                           bias=att[:, 1, g, t * HG + n:t * HG + n + 1],
                                           accum_out=att[:, 2, g, t * HG + n:t * HG + n + 1])
                        if t:
                            e.then_inc(signal["probs"], 1)
                        else:
                            e.then_inc(act_done, steps.one())

            def mix(p, g):
                for b in range(LIN):
                    act.wait_ge(bank_free[b], reads(p, b))
                for n in range(1, HG, 2):
                    act.wait_ge(bank_full[5], products(p, 5, n // 2))
                    act.activation(prob_t[:, n, :], bank(5)[:, 0:3 * P], ACT.Copy).then_inc(bank_free[5], 1)
                act.wait_ge(bank_full[7], products(p, 7))
                act.activation(o_g[:, g, 1, :], bank(7), ACT.Copy).then_inc(bank_free[7], 1)

            act.wait_ge(small_in, 128)
            for n, name in enumerate(("c", "c_2")):
                act.activation(cond[:, n * DT:(n + 1) * DT], vcol(name, 0, DT), ACT.Silu).then_inc(cond_set, 1)
            for l in steps.loop("layer", DEPTH):
                on = lambda name: place(name, l)
                norm(on("norm0"))
                gated(on("up0"), ACT.Silu, act2)
                norm(on("norm1"))
                evacuate(on("qk"), (0, 2), lambda j, m, i, ps:
                         act.activation(qk[:, at(i, 12, 4 * j + m), :], ps, ACT.Copy))
                evacuate(on("v"), (0, 2), lambda j, m, i, ps:
                         act.activation(vtok[:, m // 2, j * 512:j * 512 + S], ps, ACT.Copy))
                exps(on("logits0"), 0)
                gated(on("ccch"), ACT.Copy, cc2)
                mix(on("mix0"), 0)
                exps(on("logits1"), 1)
                evacuate(on("gate_a"), range(4), lambda j, m, i, ps:
                         act.activation(sig_c[:, 4 * j + m, :], ps, ACT.Sigmoid))
                mix(on("mix1"), 1)
                exps(on("logits2"), 2)
                evacuate(on("gate_b"), range(4), lambda j, m, i, ps:
                         act.activation(sig_a[:, 4 * j + m, :], ps, ACT.Sigmoid))
                mix(on("mix2"), 2)
                p = on("combine")
                act.wait_ge(signal["shift"], p.of("shift", 1))
                act.activation(att[:, 3, :, :], att[:, 3, :, :], ACT.Exp).then_inc(signal["weights"], 1)
                act.wait_ge(bank_full[7], products(p, 7))
                act.activation(o_t[:, 2:4, :], bank(7), ACT.Copy).then_inc(bank_free[7], 1)
                norm(on("norm2"))
                gated(on("up2"), ACT.Silu, act2)
            norm(place("final_norm"))
            evacuate(place("xm"), (0, 2), lambda j, m, i, ps:
                     act.activation(xm[:, at(i, 12, 4 * j + m), :], ps, ACT.Copy))
            evacuate(place("z"), range(4), lambda j, m, i, ps:
                     act.activation(zs[:, at(i, 12, 4 * j + m), :], ps, ACT.Silu))
            p = place("mconv")
            for f in range(MT):
                act.wait_ge(signal["conv"], p.of("conv", f + 1))
                e = act.activation(xc[:, f, :], xc[:, f, :], ACT.Silu, bias=vcol("mlstm_conv_b_2", f))
                if f == MT - 1:
                    e.then_inc(signal["xc"], 1)
            for name, dst in (("q", mq), ("k", mk), ("vT", mvt)):
                evacuate(place(name), range(0, 16, 2), lambda j, m, i, ps:
                         act.activation(dst[:, m, :], ps, ACT.Copy))
            p = place("vtok")
            for t in range(TT):
                for b in (0, 2):
                    act.wait_ge(*group_end(p, 0, t * LIN + b, 0, p.slot(0)))
                    act.activation(mv[:, t, b * 512:(b + 1) * 512], bank(b), ACT.Copy).then_inc(bank_free[b], 1)
            p = place("gates")
            act.wait_ge(bank_free[5], reads(p, 5, 0) + 1)
            act.activation(row(2), row(1), ACT.Abs).then_inc(act_done, steps.one())
            act.wait_ge(act_done, steps.count())
            act.activation(row(2), row(2), ACT.Exp, scale=-1.0).then_inc(act_done, steps.one())
            act.wait_ge(act_done, steps.count())
            act.activation(row(2), row(2), ACT.Ln, bias=1.0).then_inc(signal["gate_logs"], 1)
            p = place("rows_t")
            act.wait_ge(bank_free[4], reads(p, 4, 0) + 1)
            act.activation(small[:, 32:40], small[:, 24:32], ACT.Exp, scale=-1.0).then_inc(signal["floor"], 1)
            act.wait_ge(bank_free[6], reads(p, 6, 0) + 1)
            act.activation(decay[:, :, :], decay[:, :, :], ACT.Exp, scale=-1.0).then_inc(signal["decays"], 1)
            p = place("numer")
            act.wait_ge(signal["mvar"], p.of("mvar", 1))
            act.activation(small[:, 56:64], small[:, 56:64], ACT.Sqrt).then_inc(signal["mroot"], 1)
            layer_norm(place("ln0"))
            gated(place("up3"), ACT.Silu, act2)
            layer_norm(place("ln1"))
            p = place("s5_b")
            act.wait_ge(s5_in, 80)
            for b in range(LIN):
                act.wait_ge(bank_free[b], reads(p, b))
            dt, lr_dt, turns_s, turns_c = (s5s[:, k, :] for k in range(4))
            act.activation(dt, vcol("s5_log_dt_2", 0, ST), ACT.Exp).then_inc(signal["s5_dt"], 1)
            act.wait_ge(signal["s5_turns"], p.of("s5_turns", 1))
            act.activation(lr_dt, lr_dt, ACT.Exp).then_inc(act_done, steps.one())
            act.activation(turns_s, turns_s, ACT.Sin, scale=SIN_SCALE).then_inc(act_done, steps.one())
            act.activation(turns_c, turns_c, ACT.Sin, scale=SIN_SCALE).then_inc(signal["s5_trig"], 1)
            p = place("s5")
            for f in range(DT):
                act.wait_ge(signal["turns"], p.of("turns", f + 1))
                if f:
                    act.wait_ge(signal["back"], p.of("back", f))
                act.activation(wave_s[:, :, :], turn[:, :, :], ACT.Sin, scale=SIN_SCALE).then_inc(act_done, steps.one())
                act.activation(wave_c[:, :, :], turn4[:, :, :], ACT.Sin, scale=SIN_SCALE).then_inc(signal["waves"], 1)
                if f:
                    act.wait_ge(bank_full[4], products(p, 4, f - 1))
                    act.activation(y_t[:, f - 1, :], half(4), ACT.Copy).then_inc(bank_free[4], 1)
            act.wait_ge(bank_full[4], products(p, 4, DT - 1))
            act.activation(y_t[:, DT - 1, :], half(4), ACT.Copy).then_inc(bank_free[4], 1)
            p = place("s5_gelu")
            act.wait_ge(signal["y"], p.of("y", 1))
            act.activation(h[:, :, :], y_t[:, :, :], ACT.Gelu_apprx_tanh).then_inc(signal["gelu"], 1)
            p = place("glu")
            for j in range(4):
                for m in (0, 2):
                    b, _, k = p.what.at[j][m]
                    act.wait_ge(*group_end(p, j, m + 1, 0, p.slot(j)))
                    act.wait_ge(bank_free[b], reads(p, b, k))
                    f = 2 * j + m // 2
                    act.activation(val2[:, m // 2, :], half(b + 1), ACT.Sigmoid,
                                   bias=vcol("s5_b_glu_2", DT + f)).then_inc(bank_free[b + 1], 1)
            layer_norm(place("ln2"))
            p = place("router")
            act.wait_ge(signal["top"], p.of("top", 1))
            act.activation(small[:, 128:130], small[:, 128:130], ACT.Exp).then_inc(signal["ratio"], 1)
            for e in steps.loop("expert", NE):
                gated(place("upE", e), ACT.Silu, act2)
            layer_norm(place("ln3"))
            p = place("store")
            for b in (1, 3):
                act.wait_ge(bank_full[b], products(p, b))
                act.activation(y_tok[:, b // 2, (b % 2) * 512:(b % 2 + 1) * 512], bank(b), ACT.Copy)\
                    .then_inc(y_set_act, 1)

        @block.vector
        def _(dve):
            steps = Steps(dve, periods["dve"])

            def loop(p):
                return lambda times: steps.loop(f"{p.name} chunks", times)

            def ada_sums(p, cond_at):
                def chunk(n, i, where):
                    slot, use = where
                    dve.wait_ge(chunk_in[slot], use * 16 + 16)
                    dve.wait_ge(signal["ada_cols"], p.of("ada_cols", n + 1, i, SLOTS))
                    w = ring[:, slot, 0:32 * P].rearrange("p (m k c) -> p m k c", m=4, k=DT)
                    o = ada_sum[:, n % SLOTS, :].rearrange("p (m c) -> p m c", m=4)
                    for k in range(DT):
                        if k == 0:
                            e = dve.tensor_scalar(o, w[:, :, k, :], cond_at(k), None, ALU.mult)
                        else:
                            e = dve.scalar_tensor_tensor(o, w[:, :, k, :], cond_at(k), o, ALU.mult, ALU.add)
                        if k < DT - 1:
                            e.then_inc(dve_done, steps.one())
                            dve.wait_ge(dve_done, steps.count())
                    e.then_inc(chunk_done[slot], 1)
                return chunk

            first_cond = lambda k: cond[:, k:k + 1]
            second_cond = lambda k: cond[:, DT + k:DT + k + 1]

            def ada_next(p, col, bias_cols):
                n = 4 * p.what.adas
                dve.wait_ge(signal["ada_cols"], p.of("ada_cols", p.what.adas + SLOTS))
                dve.tensor_tensor(mod_next[:, col:col + n], psum[:, 4 * 512:4 * 512 + n], bias_cols,
                                  ALU.add).then_inc(bank_free[4], 1)
                dve.wait_ge(bank_free[4], reads(p, 4, 0) + 1)

            def evacuate(p, mine, do, cond_at=None):
                lin = p.what

                def chunk(j, i, where):
                    for m in mine:
                        dve.wait_ge(*group_end(p, j, m, i, where))
                        do(j, m, i, half(lin.at[j][m][0])).then_inc(bank_free[lin.at[j][m][0]], 1)

                walk(p, loop(p), chunk, cond_at and ada_sums(p, cond_at))

            def gated(p, buf, dst, cond_at=None):
                lin = p.what

                def chunk(j, i, where):
                    for m in (1, 3):
                        b, _, k = lin.at[j][m]
                        dve.wait_ge(*group_end(p, j, m, i, where))
                        dve.wait_ge(bank_free[b - 1], reads(p, b - 1, lin.at[j][m - 1][2], i, 0 if isinstance(i, int) else lin.per_free[b - 1]) + 1)
                        o = dst[:, at(i, 6, 2 * j + m // 2), :]
                        dve.tensor_tensor(o, buf[:, m // 2, :], half(b), ALU.mult).then_inc(bank_free[b], 1)

                walk(p, loop(p), chunk, cond_at and ada_sums(p, cond_at))

            def add_to_x(p, scale):
                lin = p.what
                for j in range(lin.chunks):
                    for m in range(lin.groups):
                        f, b = j * lin.groups + m, lin.at[j][m][0]
                        dve.wait_ge(*group_end(p, j, m, 0, p.slot(j)))
                        dve.scalar_tensor_tensor(x[:, f, :], half(b), scale[:, f:f + 1], x[:, f, :],
                                                 ALU.mult, ALU.add).then_inc(bank_free[b], 1)

            def scale_x():
                dve.tensor_scalar(x[:, :, :], x[:, :, :], ALPHA, None, ALU.mult).then_inc(dve_done, steps.one())
                dve.wait_ge(dve_done, steps.count())

            def per_root(p):
                dve.wait_ge(signal["root"], p.of("root", 1))
                dve.reciprocal(rms[:, :], rms[:, :]).then_inc(dve_done, steps.one())
                dve.wait_ge(dve_done, steps.count())

            def mean_square(p, b, eps):
                dve.wait_ge(bank_full[b], products(p, b))
                dve.tensor_scalar(rms[:, :], half(b), 1.0 / D, eps, ALU.mult, ALU.add).then_inc(bank_free[b], 1)

            def norm(p, dst, gains):
                mean_square(p, 5, EPS)
                per_root(p)
                for k in range(DT):
                    dve.scalar_tensor_tensor(dst[:, k, :], x[:, k, :], gains[:, k:k + 1], rms[:, :],
                                             ALU.mult, ALU.mult).then_inc(dve_done, steps.one())
                dve.wait_ge(dve_done, steps.count())

            def norm_mod(p):
                norm(p, h, gain)
                for k in range(DT):
                    e = dve.tensor_scalar(h[:, k, :], h[:, k, :], mod[:, k:k + 1], None, ALU.add)
                    if k == DT - 1:
                        e.then_inc(signal["h"], 1)

            def modulate(shift, scale):
                for k in range(DT):
                    e = dve.tensor_scalar(h[:, k, :], x[:, k, :], mod1[:, scale + k:scale + k + 1],
                                          mod[:, shift + k:shift + k + 1], ALU.mult, ALU.add)
                e.then_inc(signal["h"], 1)

            def take_first(p, sub, half_gate):
                for b in range(LIN):
                    dve.wait_ge(bank_free[b], reads(p, b))
                dve.tensor_copy(mod[:, 0:3 * DT], mod_next[:, 0:3 * DT]).then_inc(dve_done, steps.one())
                dve.wait_ge(dve_done, steps.count())
                dve.scalar_tensor_tensor(gain[:, :], mod[:, DT:2 * DT], 1.0,
                                         lvec[:, sub * DT:(sub + 1) * DT], ALU.add, ALU.mult).then_inc(dve_done, steps.one())
                if half_gate:
                    dve.tensor_scalar(mod[:, 2 * DT:3 * DT], mod[:, 2 * DT:3 * DT], 0.5, None, ALU.mult).then_inc(dve_done, steps.one())
                dve.wait_ge(dve_done, steps.count())

            def take_second(p, a, z):
                for b in range(LIN):
                    dve.wait_ge(bank_free[b], reads(p, b))
                dve.tensor_copy(mod[:, a:z], mod_next[:, a:z]).then_inc(dve_done, steps.one())
                dve.tensor_scalar(mod1[:, a:z], mod_next[:, a:z], 1.0, None, ALU.add).then_inc(dve_done, steps.one())
                dve.wait_ge(dve_done, steps.count())

            def ada_b(n, l=0):
                c = VEC["ada_b"] + n * 3 * DT
                return vec[:, c:c + 3 * DT] if isinstance(l, int) else vec[:, bass.ds(l * (9 * DT) + c, 3 * DT)]

            def layer_norm(p, g, b):
                dve.wait_ge(bank_full[5], products(p, 5))
                dve.tensor_scalar(rms[:, :], half(5), 1.0 / D, None, ALU.mult).then_inc(bank_free[5], 1)
                dve.wait_ge(bank_free[5], reads(p, 5, 0) + 1)
                dve.tensor_tensor(x[:, :, :], x[:, :, :],
                                  rms[:, :].unsqueeze(1).to_broadcast([P, DT, S]), ALU.subtract).then_inc(signal["mean"], 1)
                mean_square(p, 6, LN_EPS)
                per_root(p)
                for k in range(DT):
                    dve.scalar_tensor_tensor(x[:, k, :], x[:, k, :], g[:, k:k + 1], rms[:, :],
                                             ALU.mult, ALU.mult).then_inc(dve_done, steps.one())
                dve.wait_ge(dve_done, steps.count())
                for k in range(DT):
                    e = dve.tensor_scalar(x[:, k, :], x[:, k, :], b[:, k:k + 1], None, ALU.add)
                    if k < DT - 1 or p.name != "ln3":
                        e.then_inc(dve_done, steps.one())
                if p.name == "ln3":
                    e.then_inc(signal["h"], 1)
                else:
                    dve.wait_ge(dve_done, steps.count())

            def logits(p, g):
                dve.wait_ge(signal["bias_in"], p.of("bias_in", 16))
                for n in range(HG):
                    b = 4 + n % 2
                    dve.wait_ge(bank_full[b], products(p, b, n // 2))
                    dve.scalar_tensor_tensor(logit[:, n, 0:P], bank(b)[:, 0:P], HD ** -0.5,
                                             bias[:, n, P:S], ALU.mult, ALU.add).then_inc(dve_done, steps.one())
                    dve.scalar_tensor_tensor(logit[:, n, P:P + S], bank(b)[:, P:P + S], HD ** -0.5,
                                             bias[:, n, :], ALU.mult, ALU.add).then_inc(bank_free[b], 1)
                dve.wait_ge(bank_free[4], reads(p, 4, 3) + 1)
                dve.wait_ge(bank_free[5], reads(p, 5, 3) + 1)
                dve.reduce_max(att[:, 0, g, 0:HG], logit[:, :, 0:P], AX).then_inc(dve_done, steps.one())
                dve.reduce_max(att[:, 0, g, HG:2 * HG], logit[:, :, P:P + S], AX).then_inc(dve_done, steps.one())
                dve.wait_ge(dve_done, steps.count())
                dve.tensor_scalar(att[:, 1, g, :], att[:, 0, g, :], -1.0, None, ALU.mult).then_inc(signal["maxima"], 1)

            def mix(p, g):
                for b in range(LIN):
                    dve.wait_ge(bank_free[b], reads(p, b))
                for n in range(0, HG, 2):
                    dve.wait_ge(bank_full[4], products(p, 4, n // 2))
                    dve.tensor_copy(prob_t[:, n, :], bank(4)[:, 0:3 * P]).then_inc(bank_free[4], 1)
                dve.wait_ge(bank_full[6], products(p, 6))
                dve.tensor_copy(o_g[:, g, 0, :], bank(6)).then_inc(bank_free[6], 1)

            def conv(p):
                for b in range(LIN):
                    dve.wait_ge(bank_free[b], reads(p, b))
                w = lvec[:, 3 * DT:6 * DT]
                for f in range(DT):
                    dve.tensor_scalar(conv_t[:, f, :], u_t[:, f, :], w[:, 2 * DT + f:2 * DT + f + 1],
                                      None, ALU.mult).then_inc(dve_done, steps.one())
                dve.wait_ge(dve_done, steps.count())
                for k, lag in ((1, 1), (0, 2)):
                    for f in range(DT):
                        dve.scalar_tensor_tensor(conv_t[:, f, lag:S], u_t[:, f, 0:S - lag],
                                                 w[:, k * DT + f:k * DT + f + 1],
                                                 conv_t[:, f, lag:S], ALU.mult, ALU.add).then_inc(dve_done, steps.one())
                    dve.wait_ge(dve_done, steps.count())

            def combine(p, mp):
                mx, sums, w, t = (att[:, k, :, :] for k in (0, 2, 3, 4))
                over = lambda a: a.unsqueeze(1).to_broadcast([P, NG, TT * HG])
                dve.wait_ge(bank_free[6], reads(mp, 6, 0) + 1)
                dve.wait_ge(bank_free[7], reads(mp, 7, 0) + 1)
                dve.tensor_tensor(t[:, 0, :], mx[:, 0, :], mx[:, 1, :], ALU.max).then_inc(dve_done, steps.one())
                dve.wait_ge(dve_done, steps.count())
                dve.tensor_tensor(t[:, 0, :], t[:, 0, :], mx[:, 2, :], ALU.max).then_inc(dve_done, steps.one())
                dve.wait_ge(dve_done, steps.count())
                dve.tensor_tensor(w, mx, over(t[:, 0, :]), ALU.subtract).then_inc(signal["shift"], 1)
                dve.wait_ge(signal["weights"], p.of("weights", 1))
                dve.tensor_tensor(t, w, sums, ALU.mult).then_inc(dve_done, steps.one())
                dve.wait_ge(dve_done, steps.count())
                dve.tensor_tensor(t[:, 0, :], t[:, 0, :], t[:, 1, :], ALU.add).then_inc(dve_done, steps.one())
                dve.wait_ge(dve_done, steps.count())
                dve.tensor_tensor(t[:, 0, :], t[:, 0, :], t[:, 2, :], ALU.add).then_inc(dve_done, steps.one())
                dve.wait_ge(dve_done, steps.count())
                dve.reciprocal(t[:, 0, :], t[:, 0, :]).then_inc(dve_done, steps.one())
                dve.wait_ge(dve_done, steps.count())
                dve.tensor_tensor(w, w, over(t[:, 0, :]), ALU.mult).then_inc(dve_done, steps.one())
                dve.wait_ge(dve_done, steps.count())
                every = lambda g: flat(60 + 4 * g, 4).rearrange("p (a e) -> p a e", e=HD)
                for g in range(NG):
                    dve.tensor_tensor(every(g), every(g),
                                      w[:, g, :].unsqueeze(2).to_broadcast([P, TT * HG, HD]), ALU.mult).then_inc(dve_done, steps.one())
                dve.wait_ge(dve_done, steps.count())
                dve.tensor_tensor(o_tok, o_g[:, 0, :, :], o_g[:, 1, :, :], ALU.add).then_inc(dve_done, steps.one())
                dve.wait_ge(dve_done, steps.count())
                dve.tensor_tensor(o_tok, o_tok, o_g[:, 2, :, :], ALU.add).then_inc(signal["mixed"], 1)
                dve.wait_ge(bank_full[6], products(p, 6))
                dve.tensor_copy(o_t[:, 0:2, :], bank(6)).then_inc(bank_free[6], 1)

            dve.wait_ge(small_in, 128)
            p = place("load_x")
            for b in range(LIN):
                dve.wait_ge(bank_full[b], products(p, b))
                dve.tensor_copy(x[:, 2 * b:2 * b + 2, :], bank(b)).then_inc(bank_free[b], 1)
            p = place("bias_rows")
            dve.wait_ge(bank_full[4], products(p, 4))
            dve.tensor_tensor(bias_row[:, 0:383], psum[0:NG * HG, 4 * 512:4 * 512 + 383], off_mask,
                              ALU.add).then_inc(bank_free[4], 1)
            dve.wait_ge(rows_out, 16)

            dve.wait_ge(cond_set, 2)
            p = place("ada0")
            walk(p, loop(p), None, ada_sums(p, first_cond))
            ada_next(p, 0, ada_b(0))

            for l in steps.loop("layer", DEPTH):
                on = lambda name: place(name, l)
                for b in range(LIN):
                    dve.wait_ge(bank_free[b], reads(on("norm0"), b))
                dve.tensor_copy(lvec[:, 0:3 * DT], vec[:, bass.ds(l * (3 * DT) + VEC["norm_g"], 3 * DT)]).then_inc(dve_done, steps.one())
                dve.tensor_copy(lvec[:, 3 * DT:6 * DT],
                                vec[:, bass.ds(l * (3 * DT) + VEC["conv_w"], 3 * DT)]).then_inc(dve_done, steps.one())
                dve.wait_ge(dve_done, steps.count())
                gate = mod[:, 2 * DT:3 * DT]
                take_first(on("norm0"), 0, True)
                norm_mod(on("norm0"))
                gated(on("up0"), act2, mid, first_cond)
                ada_next(on("up0"), 0, ada_b(1, l))
                add_to_x(on("down0"), gate)
                take_first(on("norm1"), 1, False)
                norm_mod(on("norm1"))
                evacuate(on("qk"), (1, 3), lambda j, m, i, ps:
                         dve.tensor_copy(qk[:, at(i, 12, 4 * j + m), :], ps), first_cond)
                ada_next(on("qk"), 0, ada_b(2, l))
                evacuate(on("v"), (1, 3), lambda j, m, i, ps:
                         dve.tensor_copy(vtok[:, m // 2, j * 512 + S:(j + 1) * 512], ps))
                logits(on("logits0"), 0)
                gated(on("ccch"), cc2, u_t)
                mix(on("mix0"), 0)
                logits(on("logits1"), 1)
                conv(on("cb"))
                evacuate(on("cb"), range(4), lambda j, m, i, ps:
                         dve.tensor_tensor(conv_t[:, 4 * j + m, :], conv_t[:, 4 * j + m, :], ps, ALU.mult))
                mix(on("mix1"), 1)
                logits(on("logits2"), 2)
                evacuate(on("conv_out"), range(4), lambda j, m, i, ps:
                         dve.tensor_tensor(merged[:, 4 * j + m, :], sig_c[:, 4 * j + m, :], ps, ALU.mult))
                mix(on("mix2"), 2)
                combine(on("combine"), on("mix2"))
                p = on("attn_out")
                for m in range(DT):
                    b = p.what.at[0][m][0]
                    dve.wait_ge(*group_end(p, 0, m, 0, p.slot(0)))
                    dve.tensor_tensor(sig_a[:, m, :], sig_a[:, m, :], half(b), ALU.mult).then_inc(bank_free[b], 1)
                for b in range(LIN):
                    dve.wait_ge(bank_free[b], reads(on("wo"), b))
                dve.tensor_tensor(merged[:, :, :], merged[:, :, :], sig_a[:, :, :], ALU.add).then_inc(signal["merged"], 1)
                add_to_x(on("wo"), gate)
                take_first(on("norm2"), 2, True)
                norm_mod(on("norm2"))
                gated(on("up2"), act2, mid, lambda k: cond[:, bass.ds(l * DT + k, 1)])
                ada_next(on("up2"), 0, ada_b(3, l))
                add_to_x(on("down2"), gate)

            p = place("final_norm")
            norm(p, x, vcol("final_g", 0, DT))
            take_second(place("mod3"), 0, 3 * DT)
            modulate(0, DT)
            rest = VEC["ada_b_2"] + 3 * DT
            evacuate(place("xm"), (1, 3), lambda j, m, i, ps:
                     dve.tensor_copy(xm[:, at(i, 12, 4 * j + m), :], ps), second_cond)
            ada_next(place("xm"), 3 * DT, vec[:, rest:rest + 12])
            for b in range(LIN):
                dve.wait_ge(bank_free[b], reads(place("z"), b))
            p = place("z")
            walk(p, loop(p), None, ada_sums(p, second_cond))
            ada_next(p, 3 * DT + 12, vec[:, rest + 12:rest + 24])
            p = place("mconv")
            for f in range(MT):
                dve.tensor_scalar(xc[:, f, :], xm[:, f, :], vcol("mlstm_conv_w_2", (MC - 1) * MT + f),
                                  None, ALU.mult).then_inc(dve_done, steps.one())
            dve.wait_ge(dve_done, steps.count())
            for lag in range(1, MC):
                for f in range(MT):
                    e = dve.scalar_tensor_tensor(xc[:, f, lag:S], xm[:, f, 0:S - lag],
                                                 vcol("mlstm_conv_w_2", (MC - 1 - lag) * MT + f),
                                                 xc[:, f, lag:S], ALU.mult, ALU.add)
                    if lag == MC - 1:
                        e.then_inc(signal["conv"], 1)
                    else:
                        e.then_inc(dve_done, steps.one())
                if lag < MC - 1:
                    dve.wait_ge(dve_done, steps.count())
            for name, dst in (("q", mq), ("k", mk), ("vT", mvt)):
                evacuate(place(name), range(1, 16, 2), lambda j, m, i, ps: dve.tensor_copy(dst[:, m, :], ps))
            p = place("vtok")
            for t in range(TT):
                for b in (1, 3):
                    dve.wait_ge(*group_end(p, 0, t * LIN + b, 0, p.slot(0)))
                    dve.tensor_copy(mv[:, t, b * 512:(b + 1) * 512], bank(b)).then_inc(bank_free[b], 1)
            p = place("gates")
            dve.wait_ge(bank_full[4], products(p, 4))
            dve.tensor_tensor(small[:, 0:16], psum[:, 4 * 512:4 * 512 + 16], bgate[:, :], ALU.add).then_inc(bank_free[4], 1)
            dve.wait_ge(bank_full[5], products(p, 5))
            dve.tensor_copy(row(0), psum[0:MH, 5 * 512:5 * 512 + S]).then_inc(dve_done, steps.one())
            dve.tensor_copy(row(1), psum[0:MH, 5 * 512 + S:6 * 512]).then_inc(bank_free[5], 1)
            dve.wait_ge(bank_free[5], reads(p, 5, 0) + 1)
            dve.tensor_scalar(row(3), row(1), 0.0, None, ALU.min).then_inc(dve_done, steps.one())
            dve.wait_ge(dve_done, steps.count())
            dve.wait_ge(signal["gate_logs"], p.of("gate_logs", 1))
            dve.tensor_tensor(row(3), row(3), row(2), ALU.subtract).then_inc(dve_done, steps.one())
            dve.wait_ge(dve_done, steps.count())
            one_row = ones[0:MH, 0:1].to_broadcast([MH, S])
            dve.tensor_tensor_scan(row(7), one_row, row(3), 0.0, ALU.mult, ALU.add).then_inc(dve_done, steps.one())
            dve.wait_ge(dve_done, steps.count())
            dve.tensor_tensor(row(5), row(0), row(7), ALU.subtract).then_inc(dve_done, steps.one())
            dve.wait_ge(dve_done, steps.count())
            dve.tensor_tensor_scan(row(4), one_row, row(5), 0.0, ALU.mult, ALU.max).then_inc(dve_done, steps.one())
            dve.wait_ge(dve_done, steps.count())
            dve.tensor_tensor(row(6), row(7), row(4), ALU.add).then_inc(signal["rows"], 1)
            p = place("rows_t")
            dve.wait_ge(bank_full[4], products(p, 4))
            dve.tensor_copy(small[:, 16:32], psum[:, 4 * 512:4 * 512 + 16]).then_inc(bank_free[4], 1)
            dve.wait_ge(bank_free[4], reads(p, 4, 0) + 1)
            for n in range(MH):
                b = 5 + n // 2
                c = half(b, n % 2)
                if n % 2 == 0:
                    dve.wait_ge(bank_full[b], products(p, b))
                dve.tensor_scalar(decay[:, n, 0:S], c, small[:, 16 + n:17 + n], 0.0,
                                  ALU.subtract, ALU.max).then_inc(dve_done, steps.one())
                e = dve.tensor_scalar(decay[:, n, S:S + P], c[:, P:S], small[:, 20 + n:21 + n], 0.0,
                                      ALU.subtract, ALU.max)
                if n % 2:
                    e.then_inc(bank_free[b], 1)
                else:
                    e.then_inc(dve_done, steps.one())
            dve.wait_ge(signal["decays"], p.of("decays", 1))
            for a in (0, S):
                dve.tensor_tensor(decay[:, :, a:a + P], decay[:, :, a:a + P],
                                  tri[:, :].unsqueeze(1).to_broadcast([P, MH, P]), ALU.mult).then_inc(dve_done, steps.one())
            dve.wait_ge(dve_done, steps.count())
            p = place("scores")
            for n in range(MH):
                dve.wait_ge(bank_full[n], products(p, n))
                dve.scalar_tensor_tensor(score[:, n, :], bank(n)[:, 0:S + P], 512.0 ** -0.5,
                                         decay[:, n, :], ALU.mult, ALU.mult).then_inc(bank_free[n], 1)
            for f in range(MT):
                dve.tensor_scalar(xc[:, f, :], xc[:, f, :], vcol("mlstm_skip_2", f), None, ALU.mult).then_inc(dve_done, steps.one())
            p = place("numer")
            den, neg, var = small[:, 48:56], small[:, 40:48], small[:, 56:64]
            dve.wait_ge(bank_full[7], products(p, 7))
            dve.tensor_copy(den, psum[:, 7 * 512:7 * 512 + 8]).then_inc(bank_free[7], 1)
            dve.wait_ge(bank_free[7], reads(p, 7, 0) + 1)
            dve.tensor_scalar(neg, den, -1.0, None, ALU.mult).then_inc(dve_done, steps.one())
            dve.wait_ge(dve_done, steps.count())
            dve.tensor_tensor(den, den, neg, ALU.max).then_inc(dve_done, steps.one())
            dve.wait_ge(dve_done, steps.count())
            dve.wait_ge(signal["floor"], place("rows_t").of("floor", 1))
            dve.tensor_tensor(den, den, small[:, 32:40], ALU.max).then_inc(dve_done, steps.one())
            dve.wait_ge(dve_done, steps.count())
            dve.reciprocal(den, den).then_inc(dve_done, steps.one())
            dve.wait_ge(dve_done, steps.count())
            for n in range(MH):
                for t in range(TT):
                    b, u, c = (2 * n + t) % LIN, (2 * n + t) // LIN, t * MH + n
                    dve.wait_ge(bank_full[b], products(p, b, u))
                    dve.tensor_scalar(hn[:, t, n * 512:(n + 1) * 512], bank(b), den[:, c:c + 1], None,
                                      ALU.mult).then_inc(bank_free[b], 1)
            for b in range(LIN):
                dve.wait_ge(bank_free[b], reads(place("h_t"), b))
            stats = small[:, 144:192].rearrange("p (n k) -> p n k", k=6)
            mv2 = small[:, 192:208].rearrange("p (n k) -> p n k", k=2)
            for n in range(MH):
                for t in range(TT):
                    dve.bn_stats(stats[:, t * MH + n, :], hn[:, t, n * 512:(n + 1) * 512]).then_inc(dve_done, steps.one())
            dve.wait_ge(dve_done, steps.count())
            for c in range(8):
                dve.bn_aggr(mv2[:, c, :], stats[:, c, :]).then_inc(dve_done, steps.one())
            dve.wait_ge(dve_done, steps.count())
            dve.tensor_scalar(var, mv2[:, :, 1], LN_EPS, None, ALU.add).then_inc(signal["mvar"], 1)
            dve.wait_ge(signal["mroot"], p.of("mroot", 1))
            dve.reciprocal(var, var).then_inc(dve_done, steps.one())
            dve.wait_ge(dve_done, steps.count())
            for n in range(MH):
                for t in range(TT):
                    c, part = t * MH + n, hn[:, t, n * 512:(n + 1) * 512]
                    e = dve.tensor_scalar(part, part, mv2[:, c, 0:1], var[:, c:c + 1], ALU.subtract, ALU.mult)
            e.then_inc(signal["hn"], 1)
            p = place("h_t")
            for f in range(MT):
                b, u = (f // 2) % LIN, f // 8
                if f % 2 == 0:
                    dve.wait_ge(bank_full[b], products(p, b, u))
                e = dve.scalar_tensor_tensor(mh[:, f, :], half(b, f % 2), vcol("mlstm_norm_w_2", f),
                                             xc[:, f, :], ALU.mult, ALU.add)
                if f % 2:
                    e.then_inc(bank_free[b], 1)
                else:
                    e.then_inc(dve_done, steps.one())
            for b in range(LIN):
                dve.wait_ge(bank_free[b], reads(place("m_out"), b))
            dve.tensor_tensor(mh[:, :, :], mh[:, :, :], zs[:, :, :], ALU.mult).then_inc(signal["mh"], 1)
            take_second(place("m_out"), 3 * DT, 6 * DT)
            scale_x()
            add_to_x(place("m_out"), mod1[:, 2 * DT:3 * DT])
            layer_norm(place("ln0"), vcol("ln_mix_g_2", 0, DT), vcol("ln_mix_b_2", 0, DT))
            modulate(3 * DT, 4 * DT)
            gated(place("up3"), act2, mid, second_cond)
            ada_next(place("up3"), 0, vcol("ada_b_2", 6 * DT, 6 * DT))
            scale_x()
            add_to_x(place("down3"), mod1[:, 5 * DT:6 * DT])
            take_second(place("ln1"), 0, 6 * DT)
            layer_norm(place("ln1"), vcol("ln_ffn_g_2", 0, DT), vcol("ln_ffn_b_2", 0, DT))
            modulate(0, DT)
            p = place("s5_b")
            s = lambda k: s5s[:, k, :]
            lr, li = vcol("s5_lambda_re_2", 0, ST), vcol("s5_lambda_im_2", 0, ST)

            def tt(o, a, b, op):
                dve.tensor_tensor(o, a, b, op).then_inc(dve_done, steps.one())

            dve.wait_ge(s5_in, 80)
            dve.wait_ge(signal["s5_dt"], p.of("s5_dt", 1))
            tt(s(1), lr, s(0), ALU.mult)
            tt(s(6), li, s(0), ALU.mult)
            dve.wait_ge(dve_done, steps.count())
            dve.tensor_scalar(s(5), s(6), 1.0 / PI2, ROUND, ALU.mult, ALU.add).then_inc(dve_done, steps.one())
            dve.wait_ge(dve_done, steps.count())
            dve.tensor_scalar(s(5), s(5), -ROUND, None, ALU.add).then_inc(dve_done, steps.one())
            dve.wait_ge(dve_done, steps.count())
            for part in (PI2_A, PI2_B, PI2_C):
                dve.scalar_tensor_tensor(s(6), s(5), -part, s(6), ALU.mult, ALU.add).then_inc(dve_done, steps.one())
                dve.wait_ge(dve_done, steps.count())
            dve.tensor_scalar(s(4), s(6), 1.0 / PI2, None, ALU.mult).then_inc(dve_done, steps.one())
            dve.wait_ge(dve_done, steps.count())
            dve.tensor_scalar(s(6), s(4), 0.25, None, ALU.add).then_inc(dve_done, steps.one())
            dve.wait_ge(dve_done, steps.count())
            for src, tmp, dst in ((4, 5, 2), (6, 10, 3)):
                dve.tensor_scalar(s(tmp), s(src), 1.0, ROUND, ALU.mult, ALU.add).then_inc(dve_done, steps.one())
                dve.wait_ge(dve_done, steps.count())
                dve.tensor_scalar(s(tmp), s(tmp), -ROUND, None, ALU.add).then_inc(dve_done, steps.one())
                dve.wait_ge(dve_done, steps.count())
                e = dve.tensor_tensor(s(dst), s(src), s(tmp), ALU.subtract)
                if dst == 2:
                    e.then_inc(dve_done, steps.one())
            e.then_inc(signal["s5_turns"], 1)
            dve.wait_ge(signal["s5_trig"], p.of("s5_trig", 1))
            tt(s(5), s(1), s(3), ALU.mult)
            tt(s(6), s(1), s(2), ALU.mult)
            tt(s(9), lr, lr, ALU.mult)
            tt(s(10), li, li, ALU.mult)
            dve.wait_ge(dve_done, steps.count())
            dve.tensor_scalar(s(5), s(5), -1.0, None, ALU.add).then_inc(dve_done, steps.one())
            tt(s(9), s(9), s(10), ALU.add)
            dve.wait_ge(dve_done, steps.count())
            dve.reciprocal(s(9), s(9)).then_inc(dve_done, steps.one())
            tt(s(11), s(5), lr, ALU.mult)
            tt(s(12), s(6), li, ALU.mult)
            tt(s(13), s(6), lr, ALU.mult)
            tt(s(14), s(5), li, ALU.mult)
            dve.wait_ge(dve_done, steps.count())
            tt(s(7), s(11), s(12), ALU.add)
            tt(s(8), s(13), s(14), ALU.subtract)
            dve.wait_ge(dve_done, steps.count())
            tt(s(7), s(7), s(9), ALU.mult)
            tt(s(8), s(8), s(9), ALU.mult)
            dve.wait_ge(dve_done, steps.count())
            wide = lambda a: a.rearrange("p (i n) -> p i n", n=32)
            kr, ki = (s(k).unsqueeze(2).to_broadcast([P, ST, 32]) for k in (7, 8))
            tmp_a, tmp_b = wide(flat(36, 4)), wide(flat(40, 4))
            tt(wide(bar_re), wide(b_re), kr, ALU.mult)
            tt(tmp_a, wide(b_im), ki, ALU.mult)
            tt(wide(bar_im), wide(b_im), kr, ALU.mult)
            tt(tmp_b, wide(b_re), ki, ALU.mult)
            dve.wait_ge(dve_done, steps.count())
            tt(bar_re, bar_re, flat(36, 4), ALU.subtract)
            dve.tensor_tensor(bar_im, bar_im, flat(40, 4), ALU.add).then_inc(signal["s5_bar"], 1)
            for b in range(LIN):
                dve.wait_ge(bank_full[b], products(p, b))
                dve.tensor_copy(bar_t[:, b // 2, 4 * (b % 2):4 * (b % 2) + 4, :],
                                bank(b).rearrange("p (f n) -> p f n", f=4)).then_inc(bank_free[b], 1)
            p = place("s5")
            bu = psum[:, 0:LIN * 512].rearrange("p (b r n) -> p b r n", b=LIN, r=2)
            for f in range(DT):
                dve.wait_ge(signal["waves"], p.of("waves", f + 1))
                for j in range(LIN):
                    dve.wait_ge(bank_full[j], products(p, j, f))
                if f:
                    dve.wait_ge(signal["reals"], p.of("reals", f))
                dve.tensor_tensor(pr[0], wave_c, bu[:, :, 0, :], ALU.mult).then_inc(dve_done, steps.one())
                dve.tensor_tensor(pr[1], wave_s, bu[:, :, 1, :], ALU.mult).then_inc(dve_done, steps.one())
                dve.tensor_tensor(pr[2], wave_c, bu[:, :, 1, :], ALU.mult).then_inc(dve_done, steps.one())
                for j in range(LIN):
                    dve.tensor_tensor(pr[3][:, j, :], wave_s[:, j, :], bu[:, j, 0, :], ALU.mult).then_inc(bank_free[j], 1)
                dve.wait_ge(signal["sums"], p.of("sums", f + 1))
                for j in range(4):
                    mag = s5s[:, 1, 4 * f + j:4 * f + j + 1].to_broadcast([P, S])
                    dve.tensor_tensor_scan(st_r[:, j, :], mag, sum_r[:, j, :], 0.0, ALU.mult, ALU.add).then_inc(dve_done, steps.one())
                    dve.tensor_tensor_scan(st_i[:, j, :], mag, sum_i[:, j, :], 0.0, ALU.mult, ALU.add).then_inc(dve_done, steps.one())
                dve.wait_ge(dve_done, steps.count())
                dve.tensor_tensor(pr[2], wave_s, st_r, ALU.mult).then_inc(dve_done, steps.one())
                dve.tensor_tensor(pr[3], wave_c, st_i, ALU.mult).then_inc(dve_done, steps.one())
                dve.tensor_tensor(pr[0], wave_c, st_r, ALU.mult).then_inc(dve_done, steps.one())
                dve.tensor_tensor(pr[1], wave_s, st_i, ALU.mult).then_inc(signal["back"], 1)
                if f:
                    dve.wait_ge(bank_full[4], products(p, 4, f - 1))
                dve.wait_ge(signal["back"], p.of("back", f + 1))
                dve.scalar_tensor_tensor(xs_i, pr[2], -1.0, pr[3], ALU.mult, ALU.subtract).then_inc(signal["states"], 1)
            p = place("s5_gelu")
            dve.wait_ge(bank_free[4], reads(place("s5"), 4, DT - 1) + 1)
            for f in range(DT):
                e = dve.scalar_tensor_tensor(y_t[:, f, :], h[:, f, :], vcol("s5_d_2", f), y_t[:, f, :],
                                             ALU.mult, ALU.add)
            e.then_inc(signal["y"], 1)
            scale_x()
            p = place("glu")
            for j in range(4):
                for m in (0, 2):
                    b, _, k = p.what.at[j][m]
                    f = 2 * j + m // 2
                    dve.wait_ge(*group_end(p, j, m, 0, p.slot(j)))
                    dve.wait_ge(bank_free[b + 1], reads(p, b + 1, p.what.at[j][m + 1][2]) + 1)
                    dve.scalar_tensor_tensor(y_t[:, f, :], half(b), vcol("s5_b_glu_2", f),
                                             val2[:, m // 2, :], ALU.add, ALU.mult).then_inc(bank_free[b], 1)
            for b in range(LIN):
                dve.wait_ge(bank_free[b], reads(place("ln2"), b))
            for f in range(DT):
                dve.scalar_tensor_tensor(x[:, f, :], y_t[:, f, :], mod1[:, 2 * DT + f:2 * DT + f + 1],
                                         x[:, f, :], ALU.mult, ALU.add).then_inc(dve_done, steps.one())
            dve.wait_ge(dve_done, steps.count())
            dve.sem_inc(x_summed, 1)
            layer_norm(place("ln2"), vcol("ln_mix_g_2", DT, DT), vcol("ln_mix_b_2", DT, DT))
            modulate(3 * DT, 4 * DT)
            p = place("router")
            lg = small[:, 80:96].rearrange("p (t n) -> p t n", t=TT)
            top = small[:, 96:112].rearrange("p (t n) -> p t n", t=TT)
            idx = small[:, 112:128].rearrange("p (t n) -> p t n", t=TT)
            gate = small[:, 64:80].rearrange("p (t n) -> p t n", t=TT)
            gate2 = small[:, 136:152].rearrange("p (t n) -> p t n", t=TT)
            dve.wait_ge(bank_full[4], products(p, 4))
            dve.tensor_copy(small[:, 80:96], psum[:, 4 * 512:4 * 512 + 16]).then_inc(bank_free[4], 1)
            dve.wait_ge(bank_free[4], reads(p, 4, 0) + 1)
            for t in range(TT):
                dve.max(top[:, t, :], lg[:, t, :]).then_inc(dve_done, steps.one())
            dve.wait_ge(dve_done, steps.count())
            for t in range(TT):
                dve.max_index(index8[:, t, :], top[:, t, :], lg[:, t, :]).then_inc(dve_done, steps.one())
            dve.wait_ge(dve_done, steps.count())
            dve.tensor_copy(idx, index8[:, :, :]).then_inc(dve_done, steps.one())
            dve.tensor_tensor(small[:, 128:130], top[:, :, 1], top[:, :, 0], ALU.subtract).then_inc(signal["top"], 1)
            dve.wait_ge(signal["ratio"], p.of("ratio", 1))
            dve.tensor_scalar(small[:, 130:132], small[:, 128:130], 1.0, None, ALU.add).then_inc(dve_done, steps.one())
            dve.wait_ge(dve_done, steps.count())
            dve.reciprocal(small[:, 132:134], small[:, 130:132]).then_inc(dve_done, steps.one())
            dve.wait_ge(dve_done, steps.count())
            dve.tensor_tensor(small[:, 134:136], small[:, 128:130], small[:, 132:134], ALU.mult).then_inc(dve_done, steps.one())
            dve.wait_ge(dve_done, steps.count())
            for t in range(TT):
                dve.tensor_scalar(gate[:, t, :], iota8[:, :], idx[:, t, 0:1], small[:, 132 + t:133 + t],
                                  ALU.is_equal, ALU.mult).then_inc(dve_done, steps.one())
                dve.tensor_scalar(gate2[:, t, :], iota8[:, :], idx[:, t, 1:2], small[:, 134 + t:135 + t],
                                  ALU.is_equal, ALU.mult).then_inc(dve_done, steps.one())
            dve.wait_ge(dve_done, steps.count())
            dve.tensor_tensor(gate, gate, gate2, ALU.add).then_inc(signal["gate"], 1)
            dve.wait_ge(bank_full[5], products(p, 5))
            dve.tensor_copy(rms[0:NE, :], psum[0:NE, 5 * 512:5 * 512 + S]).then_inc(bank_free[5], 1)
            p = place("spread")
            for b in range(LIN):
                dve.wait_ge(bank_full[b], products(p, b))
                dve.tensor_copy(spread_g[:, 2 * b:2 * b + 2, :], bank(b)).then_inc(bank_free[b], 1)
            dve.memset(acc[:, :, :], 0.0).then_inc(dve_done, steps.one())
            scale_x()
            for e in steps.loop("expert", NE):
                gated(place("upE", e), act2, mid)
                p = place("downE", e)
                for j in range(p.what.chunks):
                    for m in range(p.what.groups):
                        f = j * p.what.groups + m
                        b, _, k = p.what.at[j][m]
                        dve.wait_ge(*group_end(p, j, m, 0, p.slot(j)))
                        dve.tensor_tensor(y2[:, f % 2, :], spread_g[:, e, :], half(b), ALU.mult).then_inc(bank_free[b], 1)
                        dve.wait_ge(bank_free[b], reads(p, b, k) + 1)
                        dve.tensor_tensor(acc[:, f, :], acc[:, f, :], y2[:, f % 2, :], ALU.add).then_inc(dve_done, steps.one())
                dve.wait_ge(dve_done, steps.count())
            for f in range(DT):
                dve.scalar_tensor_tensor(x[:, f, :], acc[:, f, :], mod1[:, 5 * DT + f:5 * DT + f + 1],
                                         x[:, f, :], ALU.mult, ALU.add).then_inc(dve_done, steps.one())
            dve.wait_ge(dve_done, steps.count())
            dve.sem_inc(x_summed, 1)
            layer_norm(place("ln3"), vcol("ln_ffn_g_2", DT, DT), vcol("ln_ffn_b_2", DT, DT))
            p = place("store")
            for b in (0, 2):
                dve.wait_ge(bank_full[b], products(p, b))
                dve.tensor_copy(y_tok[:, b // 2, (b % 2) * 512:(b % 2 + 1) * 512], bank(b))\
                    .then_inc(y_set_dve, 1)

        @block.gpsimd
        def _(pool):
            steps = Steps(pool, periods["pool"])
            for b in range(BANKS):
                pool.sem_inc(signal[f"free{b}"], 1)
            for s in range(SLOTS):
                pool.sem_inc(chunk_done[s], 1)
            pool.sem_inc(signal["ada_cols"], SLOTS)
            pool.memset(ones[:, :], 1.0).then_inc(ones_set, 1)
            pool.wait_ge(bank_free[4], reads(place("bias_rows"), 4, 0) + 1)
            pool.dma_start(dram["bias_rows"], bias_row[:, 0:383]).then_inc(rows_out, 16)
            pool.wait_ge(rows_out, 16)
            src = bass.AP(dram["bias_rows"].tensor, P - 1, [[383, NG * HG], [-1, P], [1, S]])
            pool.dma_start(dram["bias_table"], src).then_inc(table_out, 16)
            pool.wait_ge(table_out, 16)
            for l in range(DEPTH):
                for g in range(NG):
                    p = place(f"logits{g}", l)
                    if g:
                        before = place(f"logits{g - 1}", l)
                        pool.wait_ge(bank_free[4], reads(before, 4, 3) + 1)
                        pool.wait_ge(bank_free[5], reads(before, 5, 3) + 1)
                    else:
                        for b in range(LIN):
                            pool.wait_ge(bank_free[b], reads(place("norm1", l), b))
                    src = dram["bias_table"][g * HG:(g + 1) * HG].rearrange("h i j -> i h j")
                    pool.dma_start(bias[:, :, :], src).then_inc(signal["bias_in"], 16)
            for b in range(LIN):
                pool.wait_ge(bank_free[b], reads(place("gates"), b))
            pool.dma_start(w_gate_m, dram["m_gates"]).then_inc(mgate_in, 16)
            pool.dma_start(tri, dram["tri"]).then_inc(mgate_in, 16)
            for b in range(LIN):
                pool.wait_ge(bank_free[b], reads(place("ln1"), b))
            for dst, name in ((b_re, "s5_b_re"), (b_im, "s5_b_im"), (c_re, "s5_c_re"), (c_im, "s5_c_im"),
                              (time, "time")):
                pool.dma_start(dst, dram[name]).then_inc(s5_in, 16)
            pool.wait_ge(s5_in, 80)
            for b in range(LIN):
                pool.wait_ge(bank_free[b], reads(place("s5"), b))
            p = place("s5")
            for f in range(DT):
                if f:
                    pool.wait_ge(signal["waves"], p.of("waves", f))
                pool.tensor_tensor(turn, time.unsqueeze(1).to_broadcast([P, 4, S]),
                                   s5s[:, 4, 4 * f:4 * f + 4].unsqueeze(2).to_broadcast([P, 4, S]), ALU.mult).then_inc(pool_done, steps.one())
                pool.wait_ge(pool_done, steps.count())
                pool.tensor_scalar(turn4, turn, 1.0, 0.25, ALU.mult, ALU.add).then_inc(pool_done, steps.one())
                for n, buf in enumerate((turn, turn4)):
                    pool.tensor_scalar(near, buf, 1.0, ROUND, ALU.mult, ALU.add).then_inc(pool_done, steps.one())
                    pool.wait_ge(pool_done, steps.count())
                    pool.tensor_scalar(near, near, 1.0, -ROUND, ALU.mult, ALU.add).then_inc(pool_done, steps.one())
                    pool.wait_ge(pool_done, steps.count())
                    e = pool.tensor_tensor(buf, buf, near, ALU.subtract)
                    if n:
                        e.then_inc(signal["turns"], 1)
                    else:
                        e.then_inc(pool_done, steps.one())
                        pool.wait_ge(pool_done, steps.count())
                pool.wait_ge(bank_free[3], reads(p, 3, f) + 1)
                pool.tensor_tensor(sum_r, pr[0], pr[1], ALU.add).then_inc(pool_done, steps.one())
                pool.tensor_tensor(sum_i, pr[2], pr[3], ALU.subtract).then_inc(signal["sums"], 1)
                pool.wait_ge(signal["back"], p.of("back", f + 1))
                if f:
                    pool.wait_ge(bank_full[4], products(p, 4, f - 1))
                pool.tensor_tensor(xs_r, pr[0], pr[1], ALU.subtract).then_inc(signal["reals"], 1)
            for b in range(LIN):
                pool.wait_ge(bank_free[b], reads(place("glu"), b))
            pool.wait_ge(bank_free[4], reads(place("s5"), 4, DT - 1) + 1)
            pool.dma_start(w_router, dram["router"]).then_inc(route_in, 16)



def by_tile(w, per_chunk):
    k, n = w.shape
    t = w.reshape(k // P, P, n // P, P).transpose(2, 1, 0, 3).reshape(n // P, P, k)
    return t.reshape(-1, per_chunk, P, k).transpose(0, 2, 1, 3).reshape(-1, P, per_chunk * k)


def paired(a, b):
    k, n = a.shape
    both = np.stack([a.reshape(k, n // P, P), b.reshape(k, n // P, P)], axis=2)
    return by_tile(both.reshape(k, 2 * n), 4)


def by_row(w):
    k, n = w.shape
    return w.reshape(k // P, P, n // 512, 512).transpose(2, 1, 0, 3).reshape(n // 512, P, k // P * 512)


def block_diagonal(w):
    n = w.shape[0] // 32
    t = np.zeros((n, 32, 4, 32, 4), w.dtype)
    w = w.reshape(n, 32, 4, 4)
    for b in range(32):
        t[:, b, :, b, :] = w[:, b]
    return t.reshape(n, P, P).transpose(1, 0, 2).reshape(1, P, n * P)


def states(w):
    t = np.zeros((ST, 2, 64, 2, 16), w.dtype)
    for g in range(2):
        t[:, g, :, g, :] = w.reshape(ST, 2, 64, 16)[:, g]
    return t.reshape(ST, P, 32).transpose(1, 0, 2).reshape(P, ST * 32)


def columns(v):
    return np.ascontiguousarray(v.reshape(-1, P).T)


def bucket_of(dist):
    exact = BUCKETS // 2
    d = np.maximum(dist, 1).astype(np.float32)
    large = exact + (np.log(d / exact) / np.log(MAX_DISTANCE / exact) * (BUCKETS - exact)).astype(np.int32)
    return np.where(dist < exact, dist, np.minimum(large, BUCKETS - 1)).astype(np.int32)


def shape_tables():
    dist = 255 - np.arange(383)
    bucket = bucket_of(np.maximum(dist, 0))
    one_hot = (np.arange(BUCKETS)[:, None] == bucket[None]).astype(np.float32)
    off = np.zeros((NG, HG, 383), np.float32)
    for g, (window, dilation) in enumerate(WINDOWS):
        off[g][:, (dist < 0) | (dist > window) | (dist % dilation != 0)] = NEG
    return {
        "ident": np.eye(P, dtype=np.float32), "one_hot": one_hot, "off_mask": off.reshape(NG * HG, 383),
        "tri": np.triu(np.ones((P, P), np.float32)),
        "iota8": np.tile(np.arange(NE, dtype=np.float32), (P, 1)),
        "time": np.tile(np.arange(1, S + 1, dtype=np.float32), (P, 1)),
    }


def layout(a):
    qkv = 3 * VW
    cat = lambda parts: np.concatenate(parts, axis=0)
    w_in = a["w_in"]
    part = lambda l, n: w_in[l][:, qkv + n * D:qkv + (n + 1) * D]
    two = range(DEPTH)
    arrays = {
        "x": a["x"].reshape(TT, P, D).transpose(1, 0, 2),
        "vec": np.concatenate([columns(s5_states(name, a[name])) for name in VEC], axis=1),
        "rel_bias": a["rel_bias"],
        "b_gates": np.tile(a["mlstm_b_gates_2"], (P, TT)),
        "ada": cat([by_tile(w, 4) for name in ("ada_w", "ada_w_2") for w in a[name]]),
        "up": cat([paired(a["ffn_w_gate"][l, n], a["ffn_w_up"][l, n]) for l in two for n in range(2)]),
        "down": cat([by_tile(a["ffn_w_down"][l, n], 2) for l in two for n in range(2)]),
        "w_qk": cat([by_tile(w[:, 0:2 * VW], 4) for w in w_in]),
        "w_v": cat([by_row(w[:, 2 * VW:qkv]) for w in w_in]),
        "w_ccch": cat([paired(part(l, 1), part(l, 2)) for l in two]),
        "w_cb": cat([by_tile(part(l, 0), 4) for l in two]),
        "w_gates": cat([by_tile(part(l, n), 4) for l in two for n in (3, 4)]),
        "w_conv_out": cat([by_tile(w, 4) for w in a["w_conv_out"]]),
        "w_attn_out": cat([by_tile(w, 8) for w in a["w_attn_out"]]),
        "w_o": cat([by_tile(w, 4) for w in a["w_o"]]),
        "m_xm": by_tile(a["mlstm_w_in_2"][0][:, 0:MT * P], 4),
        "m_z": by_tile(a["mlstm_w_in_2"][0][:, MT * P:], 4),
        "m_q": block_diagonal(a["mlstm_wq_2"][0]),
        "m_k": block_diagonal(a["mlstm_wk_2"][0]),
        "m_v": block_diagonal(a["mlstm_wv_2"][0]),
        "m_gates": a["mlstm_w_gates_2"][0].reshape(3 * MT, P, 2 * MH).transpose(1, 0, 2),
        "m_out": by_tile(a["mlstm_w_out_2"][0], 2),
        "up_3": paired(a["ffn_w13_2"][0][:, 0:FT * P], a["ffn_w13_2"][0][:, FT * P:]),
        "down_3": by_tile(a["ffn_w2_2"][0], 2),
        "s5_b_re": states(a["s5_b_re_2"][0]), "s5_b_im": states(a["s5_b_im_2"][0]),
        "s5_c_re": states(a["s5_c_re_2"][0].transpose(0, 2, 1)),
        "s5_c_im": states(a["s5_c_im_2"][0].transpose(0, 2, 1)),
        "glu": paired(a["s5_w_glu_2"][0][:, 0:D], a["s5_w_glu_2"][0][:, D:]),
        "router": a["moe_router_2"][0].reshape(DT, P, NE).transpose(1, 0, 2),
        "up_e": cat([paired(w[:, 0:FT * P], w[:, FT * P:]) for w in a["moe_w13_2"][0]]),
        "down_e": cat([by_tile(w, 2) for w in a["moe_w2_2"][0]]),
        **shape_tables(),
    }
    return {k: np.ascontiguousarray(v) for k, v in arrays.items()}


def s5_states(name, v):
    return np.repeat(v.reshape(-1), 64) if name == "s5_log_dt_2" else v


def program(nc, arrays, periods):
    dram = {}
    for name, a in arrays.items():
        dram[name] = nc.dram_tensor(f"in_{name}_dram", a.shape, mybir.dt.from_np(a.dtype),
                                    kind="ExternalInput").ap()
    dram["m_v_again"] = dram["m_v"]
    dram["bias_rows"] = nc.dram_tensor("bias_rows_dram", (NG * HG, 383), F32, kind="Internal").ap()
    dram["bias_table"] = nc.dram_tensor("bias_table_dram", (NG * HG, P, S), F32, kind="Internal").ap()
    out = nc.dram_tensor("out_0_dram", (1, S, D), F32, kind="ExternalOutput").ap()
    build(nc, dram, out, periods)


def kernel(**inputs):
    import concourse.bacc as bacc
    from concourse.bass_utils import run_bass_kernel_spmd as run

    arrays = layout({k: np.asarray(v) for k, v in inputs.items()})
    periods = {"act": {}, "dve": {}, "pool": {}}
    program(bacc.Bacc("TRN2", target_bir_lowering=False, num_devices=1), arrays, periods)
    nc = bacc.Bacc("TRN2", target_bir_lowering=False, num_devices=1)
    program(nc, arrays, periods)
    r = run(nc, [{f"in_{name}_dram": a for name, a in arrays.items()}], core_ids=[0])
    return r.results[0]["out_0_dram"]
```

```python
from contextlib import ExitStack

import numpy as np

import concourse.bass as bass
from concourse import mybir

F32 = mybir.dt.float32
U32 = mybir.dt.uint32
I32 = mybir.dt.int32
ALU = mybir.AluOpType
ACT = mybir.ActivationFunctionType
AX = mybir.AxisListType.X

P = 128
D = 1024
S = 256
DEPTH = 2
DT = D // P
TT = S // P
FT = 22
HD = 64
HG = 8
NG = 3
WINDOWS = ((128, 1), (512, 4), (2048, 16))
BUCKETS = 32
MAX_DISTANCE = 2048
QT = NG * HG * HD // P
VW = NG * HG * HD
MT = 16
MH = 4
MK = 4
MC = 4
ST = 32
NE = 8
EPS = 1e-6
LN_EPS = 1e-5
NEG = -1e30
ALPHA = (2 * DEPTH) ** 0.25
PI2 = 2.0 * np.pi
SIN_SCALE = 6.283185
PI2_A = 6.28125
PI2_B = 0.00193500518798828125
PI2_C = PI2 - PI2_A - PI2_B
ROUND = 1.5 * 2.0 ** 23

SLOTS = 3
WIDE = 2 * FT * P
BANKS = 8
LIN = 4


class Linear:

    def __init__(self, chunks, groups, width, source, adas=0, **also):
        self.chunks, self.groups, self.width, self.source = chunks, groups, width, source
        self.adas, self.also = adas, also
        self.full, self.free = [0] * LIN, [0] * LIN
        self.at = []
        for j in range(chunks):
            row = []
            for m in range(groups):
                b = (j * groups + m) % LIN
                row.append((b, self.full[b], self.free[b]))
                self.free[b] += 1
                if m < groups - 1:
                    self.full[b] += 1
            self.at.append(row)
            if j == SLOTS - 1:
                self.per_full, self.per_free = list(self.full), list(self.free)
        self.order = [(kind, n) for n in range(max(chunks, adas))
                      for kind, many in (("ada", adas), ("main", chunks)) if n < many]
        both = bool(chunks and adas)
        self.rounds = (min(chunks, adas) if both else max(chunks, adas)) // SLOTS
        self.step = 2 if both else 1

    def counts(self):
        c = {"chunk": self.chunks + self.adas, "of " + self.source: self.chunks, **self.also}
        for b in range(LIN):
            c[f"full{b}"] = self.full[b]
            c[f"free{b}"] = self.free[b]
        if self.adas:
            c.update({"of ada": self.adas, "ada_cols": self.adas, "free4": 1})
        return c


def uses(**banks):
    c = {}
    for name, n in banks.items():
        c[f"full{name[1:]}"] = n
        c[f"free{name[1:]}"] = n
    return c


def with_(counts, **more):
    return {**counts, **more}


def stages():
    up = lambda src, adas=0: Linear(11, 4, 32 * P, src, adas)
    down = lambda src: Linear(4, 2, 44 * P, src)
    norm = with_(uses(b5=1), squares=DT, root=1, h=DT)
    ln = with_(uses(b5=1, b6=1), mean=DT, squares=DT, root=1, h=DT)
    logits = with_(uses(b4=4, b5=4), maxima=1, probs=HG, bias_in=16)
    mix = uses(b4=4, b5=4, b6=1, b7=1)
    prologue = {
        "load_x": uses(b0=1, b1=1, b2=1, b3=1),
        "bias_rows": uses(b4=1),
        "ada0": Linear(0, 4, 32 * P, "none", adas=6),
    }
    layer = {
        "norm0": norm, "up0": up("up", 6), "down0": down("down"),
        "norm1": norm,
        "qk": Linear(6, 4, 32 * P, "w_qk", 6), "v": Linear(3, 4, 32 * P, "w_v"),
        "logits0": logits,
        "ccch": Linear(4, 4, 32 * P, "w_ccch"),
        "mix0": mix, "logits1": logits,
        "cb": Linear(2, 4, 32 * P, "w_cb"), "gate_a": Linear(2, 4, 32 * P, "w_gates"),
        "mix1": mix, "logits2": logits,
        "gate_b": Linear(2, 4, 32 * P, "w_gates"), "conv_out": Linear(2, 4, 32 * P, "w_conv_out"),
        "mix2": mix, "combine": with_(uses(b6=1, b7=1), shift=1, weights=1, mixed=1),
        "attn_out": Linear(1, 8, 32 * P, "w_attn_out", merged=1),
        "wo": Linear(2, 4, 32 * P, "w_o"),
        "norm2": norm, "up2": up("up", 6), "down2": down("down"),
    }
    second = {
        "final_norm": with_(norm, h=0),
        "mod3": {"h": DT},
        "xm": Linear(4, 4, 32 * P, "m_xm", 3), "z": Linear(4, 4, 32 * P, "m_z", 3),
        "mconv": {"conv": MT, "xc": 1},
        "q": Linear(1, 16, 16 * P, "m_q"), "k": Linear(1, 16, 16 * P, "m_k"),
        "vT": Linear(1, 16, 16 * P, "m_v"), "vtok": Linear(1, 8, 16 * P, "m_v_again"),
        "gates": with_(uses(b4=1, b5=1), gate_logs=1, rows=1),
        "rows_t": with_(uses(b4=1, b5=1, b6=1), floor=1, decays=1),
        "scores": uses(b0=1, b1=1, b2=1, b3=1),
        "numer": with_(uses(b0=2, b1=2, b2=2, b3=2, b7=1), mvar=1, mroot=1, hn=1),
        "h_t": with_(uses(b0=2, b1=2, b2=2, b3=2), mh=1),
        "m_out": Linear(4, 2, 32 * P, "m_out"), "ln0": ln,
        "up3": up("up_3", 12), "down3": down("down_3"),
        "s5_b": with_(uses(b0=1, b1=1, b2=1, b3=1), s5_dt=1, s5_turns=1, s5_trig=1, s5_bar=1),
        "ln1": ln,
        "s5": with_(uses(b0=DT, b1=DT, b2=DT, b3=DT, b4=DT), turns=DT, waves=DT,
                    sums=DT, back=DT, reals=DT, states=DT),
        "s5_gelu": {"y": 1, "gelu": 1},
        "glu": Linear(4, 4, 32 * P, "glu"), "ln2": ln,
        "router": with_(uses(b4=2, b5=1), top=1, ratio=1, gate=1, picked=1),
        "tokens": uses(b0=1, b1=1, b2=1, b3=1),
    }
    expert = {
        "gather": with_(uses(b0=2, b1=2, b2=2, b3=2, b5=1), picked=1),
        "upE": up("up_e"), "downE": Linear(4, 1, 44 * P, "down_e"),
        "scatter": uses(b0=2, b1=2, b2=2, b3=2),
    }
    epilogue = {"ln3": ln, "store": uses(b0=1, b1=1, b2=1, b3=1)}
    return [(prologue, 1), (layer, DEPTH), (second, 1), (expert, NE), (epilogue, 1)]


class Plan:

    def __init__(self):
        self.stage, self.base, self.period = {}, {}, {}
        total = {}
        for part, times in stages():
            start, run = dict(total), dict(total)
            for name, what in part.items():
                self.stage[name] = what
                self.base[name] = dict(run)
                for k, n in (what.counts() if isinstance(what, Linear) else what).items():
                    run[k] = run.get(k, 0) + n
            period = {k: n - start.get(k, 0) for k, n in run.items()}
            if times > 1:
                assert period["chunk"] % SLOTS == 0
            for name in part:
                self.period[name] = period
            total = {k: start.get(k, 0) + n * times for k, n in period.items()}
        self.total = total


class Place:

    def __init__(self, plan, name, rep=0):
        self.name, self.what, self.rep = name, plan.stage[name], rep
        self.base, self.period = plan.base[name], plan.period[name]

    def of(self, signal, k=0, i=0, per=0):
        n = self.base.get(signal, 0) + k
        for reg, step in ((self.rep, self.period.get(signal, 0)), (i, per)):
            if isinstance(reg, int):
                n = n + reg * step
            elif step:
                n = reg * step + n
        return n

    def slot(self, pos, i=0, step=1):
        n = self.base.get("chunk", 0) + pos
        use = n // SLOTS
        for reg, per in ((self.rep, self.period["chunk"] // SLOTS), (i, step)):
            if isinstance(reg, int):
                use = use + reg * per
            elif per:
                use = reg * per + use
        return n % SLOTS, use


def walk(p, loop, main=None, ada=None):
    lin, do = p.what, {"main": main, "ada": ada}
    first = SLOTS * lin.step * lin.rounds
    if lin.rounds > 1:
        for i in loop(lin.rounds):
            for pos, (kind, n) in enumerate(lin.order[:SLOTS * lin.step]):
                if do[kind]:
                    do[kind](n, i, p.slot(pos, i, lin.step))
    else:
        first = 0
    for pos, (kind, n) in enumerate(lin.order):
        if pos >= first and do[kind]:
            do[kind](n, 0, p.slot(pos))


def loop_on(eng):
    def loop(times):
        with eng.Fori(0, times) as i:
            yield i
    return loop


def at(i, step, k):
    return i * step + k if not isinstance(i, int) else i * step + k


class Steps:

    def __init__(self, eng, periods):
        self.eng, self.periods = eng, periods
        self.n, self.rounds = 0, []

    def one(self):
        self.n += 1
        return 1

    def count(self, but=0):
        n = self.n - but
        for reg, step in self.rounds:
            n = reg * step + n
        return n

    def loop(self, name, times):
        with self.eng.Fori(0, times) as i:
            start = self.n
            self.rounds.append((i, self.periods.get(name, 1)))
            yield i
            self.rounds.pop()
            self.periods[name] = self.n - start
        self.n = start + self.periods[name] * times


def vector_columns():
    cols, n = {}, 0
    for name, k in (("c", DT), ("c_2", DT), ("ada_b", DEPTH * 9 * DT), ("ada_b_2", DEPTH * 6 * DT),
                    ("norm_g", DEPTH * 3 * DT),
                    ("conv_w", DEPTH * 3 * DT), ("final_g", DT),
                    ("ln_mix_g_2", DEPTH * DT), ("ln_mix_b_2", DEPTH * DT), ("ln_ffn_g_2", DEPTH * DT),
                    ("ln_ffn_b_2", DEPTH * DT), ("mlstm_conv_w_2", MC * MT), ("mlstm_conv_b_2", MT),
                    ("mlstm_norm_w_2", MT), ("mlstm_skip_2", MT), ("s5_d_2", DT),
                    ("s5_b_glu_2", 2 * DT), ("s5_lambda_re_2", ST), ("s5_lambda_im_2", ST),
                    ("s5_log_dt_2", ST)):
        cols[name] = n
        n += k
    return cols, n


VEC, VECS = vector_columns()


def build(nc, dram, out, periods):
    plan = Plan()
    with ExitStack() as ctx:
        sb = lambda name, shape, dt=F32: ctx.enter_context(nc.sbuf_tensor(name, shape, dt))
        sem = lambda name: ctx.enter_context(nc.semaphore(name))

        psum = ctx.enter_context(nc.psum_tensor("psum", [P, BANKS * 512], F32))
        bank = lambda b: psum[:, b * 512:(b + 1) * 512]
        half = lambda b, k=0: psum[:, b * 512 + k * S:b * 512 + (k + 1) * S]

        ring = sb("ring", [P, SLOTS, WIDE])
        x = sb("x_t", [P, DT, S])
        h = sb("h_t", [P, DT, S])
        work = sb("work", [P, 112 * S])
        vec = sb("vec", [P, VECS])
        ident = sb("ident", [P, P])
        ones = sb("ones", [P, P])
        cond = sb("cond", [P, 2 * DT])
        lvec = sb("lvec", [P, 6 * DT])
        mod = sb("mod", [P, 6 * DT])
        mod_next = sb("mod_next", [P, 6 * DT])
        ada_sum = sb("ada_sum", [P, SLOTS, 512])
        mod1 = sb("mod1", [P, 6 * DT])
        gain = sb("gain", [P, DT])
        rms = sb("rms", [P, S])
        small = sb("small", [P, 256])
        att = sb("att", [P, 5, NG, TT * HG])
        bgate = sb("bgate", [P, TT * 2 * MH])
        iota8 = sb("iota8", [P, NE])
        index8 = sb("index8", [P, TT, NE], U32)
        listed = sb("listed", [P, NE + 1, 2 * TT])
        now = sb("now", [P, 2 * TT])
        count = sb("count", [1, NE], I32)

        def tiles(a, n):
            return work[:, a * S:(a + n) * S].rearrange("p (t s) -> p t s", s=S)

        def flat(a, n):
            return work[:, a * S:(a + n) * S]

        vcol = lambda name, k=0, n=1: vec[:, VEC[name] + k:VEC[name] + k + n]

        mid, act2 = tiles(0, FT), tiles(FT, 2)
        qk = tiles(0, 2 * QT)
        vtok = flat(24, 12).rearrange("p (t n) -> p t n", t=TT)
        logit = flat(36, 12).rearrange("p (h n) -> p h n", h=HG)
        prob_t = flat(48, 12).rearrange("p (h n) -> p h n", h=HG)
        o_g = flat(60, 12).rearrange("p (g t n) -> p g t n", g=NG, t=TT)
        u_t, conv_t, sig_c, sig_a = tiles(72, DT), tiles(80, DT), tiles(88, DT), tiles(96, DT)
        bias = flat(104, 8).rearrange("p (h n) -> p h n", h=HG)
        cc2 = tiles(48, 2)
        o_tok = flat(36, 4).rearrange("p (t n) -> p t n", t=TT)
        o_t = tiles(40, 4)
        merged = u_t
        xm, zs, xc = tiles(0, MT), tiles(16, MT), tiles(32, MT)
        mq, mk, mvt = tiles(48, MT), tiles(64, MT), tiles(80, MT)
        mv = flat(96, MT).rearrange("p (t n) -> p t n", t=TT)
        decay = flat(0, 6).rearrange("p (h n) -> p h n", h=MH)
        score = flat(6, 6).rearrange("p (h n) -> p h n", h=MH)
        row = lambda k: work[0:MH, (12 + k) * S:(13 + k) * S] if k < 4 else work[0:MH, (76 + k) * S:(77 + k) * S]
        hn = flat(80, MT).rearrange("p (t n) -> p t n", t=TT)
        mh = tiles(0, MT)
        tri = flat(10, 1)[:, 0:P]
        w_gate_m = flat(8, 2)[:, 0:3 * MT * 2 * MH].rearrange("p (k n) -> p k n", n=2 * MH)
        b_re, b_im = flat(44, 4), flat(48, 4)
        c_re, c_im = flat(84, 4), flat(88, 4)
        bar_re, bar_im = flat(52, 4), flat(56, 4)
        bar_t = flat(24, 8).rearrange("p (r f n) -> p r f n", r=2, f=DT)
        time = flat(34, 1)
        quad = lambda a: tiles(a, 4)
        turn, turn_abs = quad(36), quad(40)
        wave_s, wave_c = (quad(44), quad(68)), (quad(48), quad(72))
        pr = [quad(52 + 4 * k) for k in range(4)]
        st_r, st_i = quad(76), quad(80)
        back = [quad(k) for k in (0, 4, 16, 20)]
        quarter = small[:, 208:209]
        xs_r, xs_i, near = quad(8), quad(12), quad(92)
        y_t = tiles(96, DT)
        s5s = flat(104, 3).rearrange("p (k n) -> p k n", n=ST)
        val2 = tiles(110, 2)
        sel, sel_gate = tiles(24, TT), tiles(26, TT)
        gate_sel = tiles(28, TT)
        acc = tiles(36, DT)
        chosen = small[:, 152:152 + TT * NE]
        chosen_t, ranks_t = work[0:NE, 30 * S:31 * S], work[0:NE, 31 * S:32 * S]
        h_tok = flat(44, 8).rearrange("p (t n) -> p t n", t=TT)
        y_pos = flat(52, 8).rearrange("p (t n) -> p t n", t=TT)
        w_router = flat(60, 1)[:, 0:DT * NE].rearrange("p (k n) -> p k n", n=NE)
        x_tok = flat(0, 8).rearrange("p (t n) -> p t n", t=TT)
        y_tok = flat(64, 8).rearrange("p (t n) -> p t n", t=TT)
        one_hot = work[0:BUCKETS, 8 * S:8 * S + 383]
        off_mask = work[0:NG * HG, 10 * S:10 * S + 383]
        table = work[0:BUCKETS, 12 * S:12 * S + NG * HG]
        bias_row = work[0:NG * HG, 13 * S:13 * S + 384]

        signal = {k: sem(k.replace(" ", "_")) for k in sorted(plan.total)
                  if k != "chunk" and not k.startswith("of ")}
        bank_free = [signal[f"free{b}"] for b in range(BANKS)]
        bank_full = [signal[f"full{b}"] for b in range(BANKS)]
        chunk_in = [sem(f"chunk_in{s}") for s in range(SLOTS)]
        chunk_done = [sem(f"chunk_done{s}") for s in range(SLOTS)]
        small_in = sem("small_in")
        ones_set = sem("ones_set")
        cond_set = sem("cond_set")
        rows_out = sem("rows_out")
        table_out = sem("table_out")
        s5_in = sem("s5_in")
        route_in = sem("route_in")
        mgate_in = sem("mgate_in")
        y_set_act = sem("y_set_act")
        y_set_dve = sem("y_set_dve")
        stored = sem("stored")
        x_summed = sem("x_summed")
        act_done = sem("act_done")
        dve_done = sem("dve_done")
        pool_done = sem("pool_done")




        block = ctx.enter_context(nc.Block())

        def place(name, rep=0):
            return Place(plan, name, rep)

        def reads(p, b, k=0, i=0, per=0):
            return p.of(f"free{b}", k + 1, i, per)

        def products(p, b, k=0, i=0, per=0):
            return p.of(f"full{b}", k + 1, i, per)

        def group_end(p, j, m, i, where):
            if m == p.what.groups - 1:
                return chunk_done[where[0]], where[1] + 2
            b, k, _ = p.what.at[j][m]
            return bank_full[b], products(p, b, k, i, 0 if isinstance(i, int) else p.what.per_full[b])






        @block.sync
        def _(sp):
            for dst, src in ((x_tok, dram["x"]), (ident[:, :], dram["ident"]), (vec[:, :], dram["vec"]),
                             (one_hot, dram["one_hot"]), (off_mask, dram["off_mask"]),
                             (table, dram["rel_bias"]),
                             (bgate[:, :], dram["b_gates"]),
                             (iota8[:, :], dram["iota8"])):
                sp.dma_start(dst, src).then_inc(small_in, 16)

            def stream(p):
                def load(source, width):
                    def chunk(n, i, where):
                        slot, use = where
                        src = dram[source][p.of("of " + source, n, i, SLOTS)]
                        sp.wait_ge(chunk_done[slot], use + 1)
                        sp.dma_start(ring[:, slot, 0:width], src).then_inc(chunk_in[slot], 16)
                    return chunk

                walk(p, loop_on(sp), load(p.what.source, p.what.width), load("ada", 32 * P))

            for part, times in stages():
                names = [n for n in part if isinstance(plan.stage[n], Linear)]
                if not names:
                    continue
                if times > 1:
                    with sp.Fori(0, times) as rep:
                        for n in names:
                            stream(place(n, rep))
                else:
                    for n in names:
                        stream(place(n))
            sp.wait_ge(y_set_act, 2)
            sp.wait_ge(y_set_dve, 2)
            sp.dma_start(out.rearrange("b (t p) d -> p (b t) d", p=P), y_tok).then_inc(stored, 16)
            sp.wait_ge(stored, 16)

        @block.tensor
        def _(pe):
            loop = loop_on(pe)

            def chunk_landed(where):
                slot, use = where
                pe.wait_ge(chunk_in[slot], use * 16 + 16)
                return slot

            def close(ins, p, j, m, slot):
                b = p.what.at[j][m][0]
                if m == p.what.groups - 1:
                    ins.then_inc(chunk_done[slot], 1)
                else:
                    ins.then_inc(signal[f"full{b}"], 1)

            def linear(p, moving, ready=None, width=S):
                lin = p.what
                depth = lin.width // P // lin.groups
                carried.update(p=p, main=lin.chunks)

                def chunk(j, i, where):
                    slot = chunk_landed(where)
                    for m in range(lin.groups):
                        b, _, k_free = lin.at[j][m]
                        pe.wait_ge(bank_free[b], reads(p, b, k_free, i, 0 if isinstance(i, int) else lin.per_free[b]))
                        for k in range(depth):
                            if ready and j == 0 and m == 0:
                                pe.wait_ge(signal["h"], ready.of("h", k + 1))
                            w = ring[:, slot, (m * depth + k) * P:(m * depth + k + 1) * P]
                            mm = pe.matmul(half(b)[:, 0:width], w, moving(k, j * lin.groups + m),
                                           start=(k == 0), stop=(k == depth - 1))
                        close(mm, p, j, m, slot)
                    if j < lin.adas:
                        ada(p, j, i)

                walk(p, loop, chunk, ada_where)

            carried = {}

            def ada_where(n, i, where):
                carried[n] = where
                if n >= carried["main"]:
                    ada(carried["p"], n, i)

            def ada(p, n, i):
                if n == 0:
                    pe.wait_ge(bank_free[4], reads(p, 4))
                slot, use = carried[n]
                pe.wait_ge(chunk_done[slot], use + 2)
                for m in range(4):
                    c = 4 * 512 + n * 4 + m
                    o = psum[:, c:c + 1] if isinstance(i, int) else psum[:, bass.ds(i * 12 + c, 1)]
                    mm = pe.matmul(o, ada_sum[:, n % SLOTS, m * P:(m + 1) * P], ones[:, 0:1],
                                   start=True, stop=True)
                mm.then_inc(signal["ada_cols"], 1)

            def over_features(b, src):
                for k in range(DT):
                    mm = pe.matmul(half(b), ones[:, :], src[:, k, :], start=(k == 0), stop=(k == DT - 1))
                mm.then_inc(signal[f"full{b}"], 1)

            def norm(p):
                pe.wait_ge(bank_free[5], reads(p, 5))
                for k in range(DT):
                    pe.wait_ge(signal["squares"], p.of("squares", k + 1))
                    mm = pe.matmul(half(5), ones[:, :], h[:, k, :], start=(k == 0), stop=(k == DT - 1))
                mm.then_inc(signal["full5"], 1)

            def layer_norm(p):
                for b in range(LIN):
                    pe.wait_ge(bank_free[b], reads(p, b))
                if p.name in ("ln2", "ln3"):
                    pe.wait_ge(x_summed, 1 if p.name == "ln2" else 2)
                pe.wait_ge(bank_free[5], reads(p, 5))
                over_features(5, x)
                pe.wait_ge(bank_free[6], reads(p, 6))
                for k in range(DT):
                    pe.wait_ge(signal["squares"], p.of("squares", k + 1))
                    mm = pe.matmul(half(6), ones[:, :], h[:, k, :], start=(k == 0), stop=(k == DT - 1))
                mm.then_inc(signal["full6"], 1)

            def ffn(up, down, ready=None):
                linear(up, lambda k, n: h[:, k, :], ready)
                for b in range(LIN):
                    pe.wait_ge(bank_free[b], reads(down, b))
                linear(down, lambda k, n: mid[:, k, :])

            def v_product(p):
                for j in range(3):
                    slot = chunk_landed(p.slot(j))
                    for m in range(4):
                        b, _, k_free = p.what.at[j][m]
                        t, n = m // 2, m % 2
                        pe.wait_ge(bank_free[b], reads(p, b, k_free))
                        for k in range(DT):
                            mm = pe.matmul(half(b), h[:, k, t * P:(t + 1) * P],
                                           ring[:, slot, k * 512 + n * S:k * 512 + (n + 1) * S],
                                           start=(k == 0), stop=(k == DT - 1))
                        close(mm, p, j, m, slot)

            def logits(p, g):
                for n in range(HG):
                    b, off, f = 4 + n % 2, HD * (n % 2), g * HG // 2 + n // 2
                    q, k = qk[off:off + HD, f, :], qk[off:off + HD, QT + f, :]
                    pe.wait_ge(bank_free[b], reads(p, b, n // 2))
                    o = bank(b)
                    pe.matmul(o[:, 0:P], q[:, 0:P], k[:, 0:P], start=True, stop=True)
                    pe.matmul(o[:, P:P + S], q[:, P:S], k, start=True, stop=True)\
                        .then_inc(signal[f"full{b}"], 1)

            def mix(p, g, lp):
                for n in range(HG):
                    b = 4 + n % 2
                    pe.wait_ge(signal["probs"], lp.of("probs", n + 1))
                    pe.wait_ge(bank_free[b], reads(p, b, n // 2))
                    for c in range(3):
                        mm = pe.transpose(bank(b)[:, c * P:(c + 1) * P],
                                          logit[:, n, c * P:(c + 1) * P], ident[:, :])
                    mm.then_inc(signal[f"full{b}"], 1)
                pe.wait_ge(bank_free[4], reads(p, 4, 4))
                pe.wait_ge(bank_free[5], reads(p, 5, 4))
                pe.wait_ge(bank_free[6], reads(p, 6))
                pe.wait_ge(bank_free[7], reads(p, 7))
                for n in range(HG):
                    e = (g * HG + n) * HD
                    mm = pe.matmul(bank(6)[:, n * HD:(n + 1) * HD], prob_t[:, n, 0:P],
                                   vtok[:, 0, e:e + HD], start=True, stop=True)
                mm.then_inc(signal["full6"], 1)
                for n in range(HG):
                    e = (g * HG + n) * HD
                    o = bank(7)[:, n * HD:(n + 1) * HD]
                    pe.matmul(o, prob_t[:, n, P:2 * P], vtok[:, 0, e:e + HD], start=True, stop=False)
                    mm = pe.matmul(o, prob_t[:, n, 2 * P:3 * P], vtok[:, 1, e:e + HD], start=False, stop=True)
                mm.then_inc(signal["full7"], 1)

            def combine(p):
                pe.wait_ge(signal["mixed"], p.of("mixed", 1))
                for f in range(4):
                    b = 6 + f // 2
                    if f % 2 == 0:
                        pe.wait_ge(bank_free[b], reads(p, b))
                    for t in range(TT):
                        c = (f % 2) * S + t * P
                        mm = pe.transpose(bank(b)[:, c:c + P], o_tok[:, t, f * P:(f + 1) * P], ident[:, :])
                    if f % 2:
                        mm.then_inc(signal[f"full{b}"], 1)

            pe.wait_ge(small_in, 128)
            p = place("load_x")
            for f in range(DT):
                b = f // 2
                if f % 2 == 0:
                    pe.wait_ge(bank_free[b], reads(p, b))
                for t in range(TT):
                    c = (f % 2) * S + t * P
                    mm = pe.transpose(bank(b)[:, c:c + P], x_tok[:, t, f * P:(f + 1) * P], ident[:, :])
                if f % 2:
                    mm.then_inc(signal[f"full{b}"], 1)
            p = place("bias_rows")
            pe.wait_ge(bank_free[4], reads(p, 4))
            pe.matmul(psum[0:NG * HG, 4 * 512:4 * 512 + 383], table, one_hot, start=True, stop=True)\
                .then_inc(signal["full4"], 1)
            pe.wait_ge(ones_set, 1)
            linear(place("ada0"), None)

            with pe.Fori(0, DEPTH) as l:
                on = lambda name: place(name, l)
                norm(on("norm0"))
                ffn(on("up0"), on("down0"), on("norm0"))
                norm(on("norm1"))
                linear(on("qk"), lambda k, n: h[:, k, :], on("norm1"))
                v_product(on("v"))
                logits(on("logits0"), 0)
                linear(on("ccch"), lambda k, n: h[:, k, :])
                mix(on("mix0"), 0, on("logits0"))
                logits(on("logits1"), 1)
                linear(on("cb"), lambda k, n: h[:, k, :])
                linear(on("gate_a"), lambda k, n: h[:, k, :])
                mix(on("mix1"), 1, on("logits1"))
                logits(on("logits2"), 2)
                linear(on("gate_b"), lambda k, n: h[:, k, :])
                linear(on("conv_out"), lambda k, n: conv_t[:, k, :])
                mix(on("mix2"), 2, on("logits2"))
                combine(on("combine"))
                pe.wait_ge(bank_free[6], reads(on("attn_out"), 6))
                pe.wait_ge(bank_free[7], reads(on("attn_out"), 7))
                linear(on("attn_out"), lambda k, n: o_t[:, k, :])
                pe.wait_ge(signal["merged"], on("attn_out").of("merged", 1))
                linear(on("wo"), lambda k, n: merged[:, k, :])
                norm(on("norm2"))
                ffn(on("up2"), on("down2"), on("norm2"))

            norm(place("final_norm"))
            linear(place("xm"), lambda k, n: h[:, k, :], place("mod3"))
            linear(place("z"), lambda k, n: h[:, k, :])
            pe.wait_ge(signal["xc"], place("mconv").of("xc", 1))
            linear(place("q"), lambda k, n: xc[:, n, :])
            linear(place("k"), lambda k, n: xc[:, n, :])
            linear(place("vT"), lambda k, n: xm[:, n, :])
            p = place("vtok")
            for b in range(LIN):
                pe.wait_ge(bank_free[b], reads(p, b))
            slot = chunk_landed(p.slot(0))
            for t in range(TT):
                for b in range(LIN):
                    m = t * LIN + b
                    pe.wait_ge(bank_free[b], reads(p, b, t))
                    for n in range(4):
                        f = 4 * b + n
                        mm = pe.matmul(bank(b)[:, n * P:(n + 1) * P], xm[:, f, t * P:(t + 1) * P],
                                       ring[:, slot, f * P:(f + 1) * P], start=True, stop=True)
                    close(mm, p, 0, m, slot)
            p = place("gates")
            pe.wait_ge(mgate_in, 32)
            pe.wait_ge(bank_free[4], reads(p, 4))
            for t in range(TT):
                for k in range(3 * MT):
                    src = (mq, mk, mvt)[k // MT][:, k % MT, t * P:(t + 1) * P]
                    mm = pe.matmul(psum[:, 4 * 512 + t * 8:4 * 512 + t * 8 + 8], src, w_gate_m[:, k, :],
                                   start=(k == 0), stop=(k == 3 * MT - 1))
            mm.then_inc(signal["full4"], 1)
            pe.wait_ge(bank_free[4], reads(p, 4, 0) + 1)
            pe.wait_ge(bank_free[5], reads(p, 5))
            gsb = small[:, 0:TT * 2 * MH].rearrange("p (t n) -> p t n", t=TT)
            for n in range(2):
                for t in range(TT):
                    mm = pe.transpose(psum[0:MH, 5 * 512 + n * S + t * P:5 * 512 + n * S + (t + 1) * P],
                                      gsb[:, t, n * MH:(n + 1) * MH], ident[:, :])
            mm.then_inc(signal["full5"], 1)
            pe.wait_ge(signal["rows"], p.of("rows", 1))
            p = place("rows_t")
            pe.wait_ge(bank_free[4], reads(p, 4))
            for n in range(2):
                for t in range(TT):
                    c = 4 * 512 + n * 8 + t * MH
                    mm = pe.transpose(psum[:, c:c + MH], row(5 + n)[:, t * P:(t + 1) * P],
                                      ident[0:MH, 0:MH])
            mm.then_inc(signal["full4"], 1)
            for b in (5, 6):
                pe.wait_ge(bank_free[b], reads(p, b))
                for n in range(2):
                    hd = (b - 5) * 2 + n
                    mm = pe.matmul(half(b, n), ident[0:MH, hd:hd + 1].to_broadcast([MH, P]), row(4), start=True, stop=True)
                mm.then_inc(signal[f"full{b}"], 1)
            p = place("scores")
            for n in range(MH):
                pe.wait_ge(bank_free[n], reads(p, n))
                for c, (a, z, lo) in enumerate(((0, P, 0), (P, S, P))):
                    for k in range(4):
                        mm = pe.matmul(bank(n)[:, c * S:c * S + S - lo], mk[:, 4 * n + k, a:z],
                                       mq[:, 4 * n + k, lo:S], start=(k == 0), stop=(k == 3))
                mm.then_inc(signal[f"full{n}"], 1)
            p = place("numer")
            for b in range(LIN):
                pe.wait_ge(bank_free[b], reads(p, b))
            parts = lambda t: ((0, 0),) if t == 0 else ((P, 0), (S, 1))
            pe.wait_ge(bank_free[7], reads(p, 7))
            for n in range(MH):
                for t in range(TT):
                    for q, (c, s_t) in enumerate(parts(t)):
                        mm = pe.matmul(psum[:, 7 * 512 + t * MH + n:7 * 512 + t * MH + n + 1],
                                       score[:, n, c:c + P], ones[:, 0:1], start=(q == 0),
                                       stop=(q == len(parts(t)) - 1))
            mm.then_inc(signal["full7"], 1)
            for n in range(MH):
                for t in range(TT):
                    b, u = (2 * n + t) % LIN, (2 * n + t) // LIN
                    pe.wait_ge(bank_free[b], reads(p, b, u))
                    for q, (c, s_t) in enumerate(parts(t)):
                        mm = pe.matmul(bank(b), score[:, n, c:c + P], mv[:, s_t, n * 512:(n + 1) * 512],
                                       start=(q == 0), stop=(q == len(parts(t)) - 1))
                    mm.then_inc(signal[f"full{b}"], 1)
            pe.wait_ge(signal["hn"], p.of("hn", 1))
            p = place("h_t")
            for f in range(MT):
                b, u = (f // 2) % LIN, f // 8
                if f % 2 == 0:
                    pe.wait_ge(bank_free[b], reads(p, b, u))
                for t in range(TT):
                    c = (f % 2) * S + t * P
                    mm = pe.transpose(bank(b)[:, c:c + P], hn[:, t, f * P:(f + 1) * P], ident[:, :])
                if f % 2:
                    mm.then_inc(signal[f"full{b}"], 1)
            pe.wait_ge(signal["mh"], p.of("mh", 1))
            linear(place("m_out"), lambda k, n: mh[:, k, :])
            layer_norm(place("ln0"))
            ffn(place("up3"), place("down3"), place("ln0"))
            p = place("s5_b")
            pe.wait_ge(signal["s5_bar"], p.of("s5_bar", 1))
            for r, src in enumerate((bar_re, bar_im)):
                for f in range(DT):
                    b, c = 2 * r + f // 4, (f % 4) * P
                    if f % 4 == 0:
                        pe.wait_ge(bank_free[b], reads(p, b))
                    mm = pe.transpose(bank(b)[:, c:c + P], src[:, f * P:(f + 1) * P], ident[:, :])
                    if f % 4 == 3:
                        mm.then_inc(signal[f"full{b}"], 1)
            layer_norm(place("ln1"))
            p = place("s5")

            def states_in(f):
                pe.wait_ge(signal["h"], place("ln1").of("h", f + 1))
                for j in range(4):
                    rows = slice(32 * j, 32 * j + 32)
                    pe.wait_ge(bank_free[j], reads(p, j, f))
                    for r in range(2):
                        mm = pe.matmul(half(j, r), bar_t[rows, r, f, :], h[rows, f, :], start=True, stop=True)
                    mm.then_inc(signal[f"full{j}"], 1)

            def sums_out(f):
                pe.wait_ge(signal["states"], p.of("states", f + 1))
                pe.wait_ge(signal["reals"], p.of("reals", f + 1))
                pe.wait_ge(bank_free[4], reads(p, 4, f))
                for j in range(4):
                    rows = slice(32 * j, 32 * j + 32)
                    o = psum[rows, 4 * 512:4 * 512 + S]
                    pe.matmul(o, c_re[:, f * P + 32 * j:f * P + 32 * j + 32], xs_r[:, j, :], start=True, stop=False)
                    mm = pe.matmul(o, c_im[:, f * P + 32 * j:f * P + 32 * j + 32], xs_i[:, j, :], start=False, stop=True)
                mm.then_inc(signal["full4"], 1)

            states_in(0)
            for f in range(DT):
                if f + 1 < DT:
                    states_in(f + 1)
                if f:
                    sums_out(f - 1)
            sums_out(DT - 1)
            pe.wait_ge(signal["gelu"], place("s5_gelu").of("gelu", 1))
            linear(place("glu"), lambda k, n: h[:, k, :])
            layer_norm(place("ln2"))
            p = place("router")
            pe.wait_ge(signal["h"], place("ln2").of("h", DT))
            pe.wait_ge(route_in, 16)
            pe.wait_ge(bank_free[4], reads(p, 4))
            for t in range(TT):
                for k in range(DT):
                    mm = pe.matmul(psum[:, 4 * 512 + t * NE:4 * 512 + (t + 1) * NE], h[:, k, t * P:(t + 1) * P],
                                   w_router[:, k, :], start=(k == 0), stop=(k == DT - 1))
            mm.then_inc(signal["full4"], 1)
            p = place("tokens")
            for t in range(TT):
                for f in range(DT):
                    b, c = 2 * t + f // 4, (f % 4) * P
                    if f % 4 == 0:
                        pe.wait_ge(bank_free[b], reads(p, b))
                    mm = pe.transpose(bank(b)[:, c:c + P], h[:, f, t * P:(t + 1) * P], ident[:, :])
                    if f % 4 == 3:
                        mm.then_inc(signal[f"full{b}"], 1)
            p = place("router")
            pe.wait_ge(signal["gate"], p.of("gate", 1))
            pe.wait_ge(bank_free[5], reads(p, 5))
            for t in range(TT):
                pe.transpose(psum[0:NE, 5 * 512 + t * P:5 * 512 + (t + 1) * P],
                             chosen[:, t * NE:(t + 1) * NE], ident[:, :])
            for t in range(TT):
                mm = pe.matmul(psum[0:1, 5 * 512 + S:5 * 512 + S + NE], ones[:, 0:1],
                               chosen[:, t * NE:(t + 1) * NE], start=(t == 0), stop=(t == TT - 1))
            mm.then_inc(signal["full5"], 1)
            pe.wait_ge(bank_free[5], reads(p, 5, 0) + 1)
            pe.wait_ge(bank_free[4], reads(p, 4, 1))
            for t in range(TT):
                mm = pe.transpose(psum[:, 4 * 512 + t * NE:4 * 512 + (t + 1) * NE],
                                  rms[0:NE, t * P:(t + 1) * P], ident[0:NE, 0:NE])
            mm.then_inc(signal["full4"], 1)

            def expert(e, lists):
                width = lists * P
                p = place("gather", e)
                pe.wait_ge(signal["picked"], p.of("picked", 0))
                for b in range(LIN):
                    pe.wait_ge(bank_free[b], reads(p, b))
                for f in range(DT):
                    b = f % LIN
                    pe.wait_ge(bank_free[b], reads(p, b, f // LIN))
                    for t in range(TT):
                        mm = pe.matmul(half(b)[:, 0:width], h_tok[:, t, f * P:(f + 1) * P],
                                       sel[:, t, 0:width], start=(t == 0), stop=(t == TT - 1))
                    mm.then_inc(signal[f"full{b}"], 1)
                pe.wait_ge(bank_free[5], reads(p, 5))
                for b in range(LIN):
                    pe.wait_ge(bank_free[b], reads(p, b, 1) + 1)
                for n in range(lists):
                    for t in range(TT):
                        mm = pe.transpose(half(5, n)[:, t * P:(t + 1) * P],
                                          sel_gate[:, t, n * P:(n + 1) * P], ident[:, :])
                mm.then_inc(signal["full5"], 1)
                linear(place("upE", e), lambda k, n: h[:, k, 0:width], width=width)
                p = place("downE", e)
                for b in range(LIN):
                    pe.wait_ge(bank_free[b], reads(p, b))
                for j in range(4):
                    slot = chunk_landed(p.slot(j))
                    side, part, depth = j // 2, j % 2, FT // 2
                    for n in reversed(range(lists)):
                        for k in range(depth):
                            mm = pe.matmul(bank(2 * side + n),
                                           mid[:, part * depth + k, n * P:(n + 1) * P],
                                           ring[:, slot, k * 512:(k + 1) * 512],
                                           start=(part == 0 and k == 0), stop=(part == 1 and k == depth - 1))
                    mm.then_inc(chunk_done[slot], 1)
                p = place("scatter", e)
                for b in range(LIN):
                    pe.wait_ge(bank_free[b], reads(p, b))
                pe.wait_ge(bank_free[5], reads(place("gather", e), 5, 0) + 1)
                for f in range(DT):
                    b = f % LIN
                    pe.wait_ge(bank_free[b], reads(p, b, f // LIN))
                    for n in range(lists):
                        mm = pe.matmul(half(b), y_pos[:, n, f * P:(f + 1) * P], gate_sel[:, n, :],
                                       start=(n == 0), stop=(n == lists - 1))
                    mm.then_inc(signal[f"full{b}"], 1)

            with pe.Fori(0, NE) as e:
                many = pe.value_load(count[0:1, bass.ds(e, 1)], min_val=0, max_val=S)
                with pe.If(many <= P):
                    expert(e, 1)
                with pe.Else():
                    expert(e, TT)
            layer_norm(place("ln3"))
            p = place("store")
            pe.wait_ge(signal["h"], place("ln3").of("h", DT))
            for t in range(TT):
                for f in range(DT):
                    b, c = 2 * t + f // 4, (f % 4) * P
                    if f % 4 == 0:
                        pe.wait_ge(bank_free[b], reads(p, b))
                    mm = pe.transpose(bank(b)[:, c:c + P], x[:, f, t * P:(t + 1) * P], ident[:, :])
                    if f % 4 == 3:
                        mm.then_inc(signal[f"full{b}"], 1)

        @block.scalar
        def _(act):
            steps = Steps(act, periods["act"])

            def evacuate(p, mine, do):
                lin = p.what

                def chunk(j, i, where):
                    for m in mine:
                        b, _, k = lin.at[j][m]
                        act.wait_ge(*group_end(p, j, m, i, where))
                        do(j, m, i, half(b)).then_inc(bank_free[b], 1)

                walk(p, loop_on(act), chunk)

            def gated(p, func, buf, bias_col=None):
                lin = p.what

                def chunk(j, i, where):
                    for m in (0, 2):
                        b, _, k = lin.at[j][m]
                        act.wait_ge(*group_end(p, j, m, i, where))
                        act.wait_ge(bank_free[b + 1], reads(p, b + 1, k, i, 0 if isinstance(i, int) else lin.per_free[b]))
                        act.activation(buf[:, m // 2, :], half(b), func).then_inc(bank_free[b], 1)

                walk(p, loop_on(act), chunk)

            def root(p, b):
                act.wait_ge(bank_free[b], reads(p, b, 0) + 1)
                act.activation(rms[:, :], rms[:, :], ACT.Sqrt).then_inc(signal["root"], 1)

            def norm(p):
                for k in range(DT):
                    act.wait_ge(bank_free[k % LIN], reads(p, k % LIN, k // LIN - 1))
                    act.activation(h[:, k, :], x[:, k, :], ACT.Square).then_inc(signal["squares"], 1)
                root(p, 5)

            def layer_norm(p):
                for k in range(DT):
                    act.wait_ge(signal["mean"], p.of("mean", k + 1))
                    act.activation(h[:, k, :], x[:, k, :], ACT.Square).then_inc(signal["squares"], 1)
                root(p, 6)

            def exps(p, g):
                act.wait_ge(signal["maxima"], p.of("maxima", 1))
                for n in range(HG):
                    for t, (a, z) in enumerate(((0, P), (P, P + S))):
                        e = act.activation(logit[:, n, a:z], logit[:, n, a:z], ACT.Exp,
                                           bias=att[:, 1, g, t * HG + n:t * HG + n + 1],
                                           accum_out=att[:, 2, g, t * HG + n:t * HG + n + 1])
                        if t:
                            e.then_inc(signal["probs"], 1)
                        else:
                            e.then_inc(act_done, steps.one())

            def mix(p, g):
                for b in range(LIN):
                    act.wait_ge(bank_free[b], reads(p, b))
                for n in range(1, HG, 2):
                    act.wait_ge(bank_full[5], products(p, 5, n // 2))
                    act.activation(prob_t[:, n, :], bank(5)[:, 0:3 * P], ACT.Copy).then_inc(bank_free[5], 1)
                act.wait_ge(bank_full[7], products(p, 7))
                act.activation(o_g[:, g, 1, :], bank(7), ACT.Copy).then_inc(bank_free[7], 1)

            act.wait_ge(small_in, 128)
            for n, name in enumerate(("c", "c_2")):
                act.activation(cond[:, n * DT:(n + 1) * DT], vcol(name, 0, DT), ACT.Silu).then_inc(cond_set, 1)
            for b in range(LIN):
                act.wait_ge(bank_free[b], reads(place("norm0", 0), b))
            for l in steps.loop("layer", DEPTH):
                on = lambda name: place(name, l)
                norm(on("norm0"))
                gated(on("up0"), ACT.Silu, act2)
                norm(on("norm1"))
                evacuate(on("qk"), (0, 2), lambda j, m, i, ps:
                         act.activation(qk[:, at(i, 12, 4 * j + m), :], ps, ACT.Copy))
                evacuate(on("v"), (0, 2), lambda j, m, i, ps:
                         act.activation(vtok[:, m // 2, j * 512:j * 512 + S], ps, ACT.Copy))
                exps(on("logits0"), 0)
                gated(on("ccch"), ACT.Copy, cc2)
                mix(on("mix0"), 0)
                exps(on("logits1"), 1)
                evacuate(on("gate_a"), range(4), lambda j, m, i, ps:
                         act.activation(sig_c[:, 4 * j + m, :], ps, ACT.Sigmoid))
                mix(on("mix1"), 1)
                exps(on("logits2"), 2)
                evacuate(on("gate_b"), range(4), lambda j, m, i, ps:
                         act.activation(sig_a[:, 4 * j + m, :], ps, ACT.Sigmoid))
                mix(on("mix2"), 2)
                p = on("combine")
                act.wait_ge(signal["shift"], p.of("shift", 1))
                act.activation(att[:, 3, :, :], att[:, 3, :, :], ACT.Exp).then_inc(signal["weights"], 1)
                act.wait_ge(bank_full[7], products(p, 7))
                act.activation(o_t[:, 2:4, :], bank(7), ACT.Copy).then_inc(bank_free[7], 1)
                norm(on("norm2"))
                gated(on("up2"), ACT.Silu, act2)
            norm(place("final_norm"))
            evacuate(place("xm"), (0, 2), lambda j, m, i, ps:
                     act.activation(xm[:, at(i, 12, 4 * j + m), :], ps, ACT.Copy))
            evacuate(place("z"), range(4), lambda j, m, i, ps:
                     act.activation(zs[:, at(i, 12, 4 * j + m), :], ps, ACT.Silu))
            p = place("mconv")
            for f in range(MT):
                act.wait_ge(signal["conv"], p.of("conv", f + 1))
                e = act.activation(xc[:, f, :], xc[:, f, :], ACT.Silu, bias=vcol("mlstm_conv_b_2", f))
                if f == MT - 1:
                    e.then_inc(signal["xc"], 1)
            for name, dst in (("q", mq), ("k", mk), ("vT", mvt)):
                evacuate(place(name), range(0, 16, 2), lambda j, m, i, ps:
                         act.activation(dst[:, m, :], ps, ACT.Copy))
            p = place("vtok")
            for t in range(TT):
                for b in (0, 2):
                    act.wait_ge(*group_end(p, 0, t * LIN + b, 0, p.slot(0)))
                    act.activation(mv[:, t, b * 512:(b + 1) * 512], bank(b), ACT.Copy).then_inc(bank_free[b], 1)
            p = place("gates")
            act.wait_ge(bank_free[5], reads(p, 5, 0) + 1)
            act.activation(row(2), row(1), ACT.Abs).then_inc(act_done, steps.one())
            act.wait_ge(act_done, steps.count())
            act.activation(row(2), row(2), ACT.Exp, scale=-1.0).then_inc(act_done, steps.one())
            act.wait_ge(act_done, steps.count())
            act.activation(row(2), row(2), ACT.Ln, bias=1.0).then_inc(signal["gate_logs"], 1)
            p = place("rows_t")
            act.wait_ge(bank_free[4], reads(p, 4, 0) + 1)
            act.activation(small[:, 32:40], small[:, 24:32], ACT.Exp, scale=-1.0).then_inc(signal["floor"], 1)
            act.wait_ge(bank_free[6], reads(p, 6, 0) + 1)
            act.activation(decay[:, :, :], decay[:, :, :], ACT.Exp, scale=-1.0).then_inc(signal["decays"], 1)
            p = place("numer")
            act.wait_ge(signal["mvar"], p.of("mvar", 1))
            act.activation(small[:, 56:64], small[:, 56:64], ACT.Sqrt).then_inc(signal["mroot"], 1)
            layer_norm(place("ln0"))
            gated(place("up3"), ACT.Silu, act2)
            p = place("s5_b")
            act.wait_ge(s5_in, 80)
            dt, lr_dt, turns_s, turns_c = (s5s[:, k, :] for k in range(4))
            act.activation(dt, vcol("s5_log_dt_2", 0, ST), ACT.Exp).then_inc(signal["s5_dt"], 1)
            act.wait_ge(signal["s5_turns"], p.of("s5_turns", 1))
            act.activation(lr_dt, lr_dt, ACT.Exp).then_inc(act_done, steps.one())
            act.activation(turns_s, turns_s, ACT.Sin, scale=SIN_SCALE).then_inc(act_done, steps.one())
            act.activation(turns_c, turns_c, ACT.Sin, scale=SIN_SCALE).then_inc(signal["s5_trig"], 1)
            layer_norm(place("ln1"))
            p = place("s5")
            for f in range(DT):
                act.wait_ge(signal["turns"], p.of("turns", f + 1))
                if f > 1:
                    act.wait_ge(signal["back"], p.of("back", f - 1))
                act.wait_ge(act_done, steps.count())
                act.activation(turn_abs[:, :, :], turn[:, :, :], ACT.Abs).then_inc(act_done, steps.one())
                act.activation(wave_s[f % 2][:, :, :], turn[:, :, :], ACT.Sin, scale=SIN_SCALE).then_inc(act_done, steps.one())
                act.wait_ge(act_done, steps.count())
                act.activation(wave_c[f % 2][:, :, :], turn_abs[:, :, :], ACT.Sin, bias=quarter,
                               scale=-SIN_SCALE).then_inc(signal["waves"], 1)
                if f > 1:
                    act.wait_ge(bank_full[4], products(p, 4, f - 2))
                    act.activation(y_t[:, f - 2, :], half(4), ACT.Copy).then_inc(bank_free[4], 1)
                act.wait_ge(signal["waves"], p.of("waves", f + 1))
            for f in (DT - 2, DT - 1):
                act.wait_ge(bank_full[4], products(p, 4, f))
                act.activation(y_t[:, f, :], half(4), ACT.Copy).then_inc(bank_free[4], 1)
            p = place("s5_gelu")
            act.wait_ge(signal["y"], p.of("y", 1))
            act.activation(h[:, :, :], y_t[:, :, :], ACT.Gelu_apprx_tanh).then_inc(signal["gelu"], 1)
            p = place("glu")
            for j in range(4):
                for m in (0, 2):
                    b, _, k = p.what.at[j][m]
                    act.wait_ge(*group_end(p, j, m + 1, 0, p.slot(j)))
                    act.wait_ge(bank_free[b], reads(p, b, k))
                    f = 2 * j + m // 2
                    act.activation(val2[:, m // 2, :], half(b + 1), ACT.Sigmoid,
                                   bias=vcol("s5_b_glu_2", DT + f)).then_inc(bank_free[b + 1], 1)
            layer_norm(place("ln2"))
            p = place("router")
            act.wait_ge(signal["top"], p.of("top", 1))
            act.activation(small[:, 128:130], small[:, 128:130], ACT.Exp).then_inc(signal["ratio"], 1)
            p = place("tokens")
            for b in (1, 3):
                act.wait_ge(bank_full[b], products(p, b))
                act.activation(h_tok[:, b // 2, (b % 2) * 512:(b % 2 + 1) * 512], bank(b), ACT.Copy).then_inc(bank_free[b], 1)
            for e in steps.loop("expert", NE):
                p = place("gather", e)
                for f in range(1, DT, 2):
                    act.wait_ge(bank_full[f % LIN], products(p, f % LIN, f // LIN))
                    act.activation(h[:, f, :], half(f % LIN), ACT.Copy).then_inc(bank_free[f % LIN], 1)
                gated(place("upE", e), ACT.Silu, act2)
                p = place("downE", e)
                for side in range(2):
                    act.wait_ge(*group_end(p, 2 * side + 1, 0, 0, p.slot(2 * side + 1)))
                    act.activation(y_pos[:, 1, side * 512:(side + 1) * 512], bank(2 * side + 1),
                                   ACT.Copy).then_inc(bank_free[2 * side + 1], 1)
            layer_norm(place("ln3"))
            p = place("store")
            for b in (1, 3):
                act.wait_ge(bank_full[b], products(p, b))
                act.activation(y_tok[:, b // 2, (b % 2) * 512:(b % 2 + 1) * 512], bank(b), ACT.Copy)\
                    .then_inc(y_set_act, 1)

        @block.vector
        def _(dve):
            steps = Steps(dve, periods["dve"])

            def loop(p):
                return lambda times: steps.loop(f"{p.name} chunks", times)

            def ada_sums(p, cond_at):
                def chunk(n, i, where):
                    slot, use = where
                    dve.wait_ge(chunk_in[slot], use * 16 + 16)
                    dve.wait_ge(signal["ada_cols"], p.of("ada_cols", n + 1, i, SLOTS))
                    w = ring[:, slot, 0:32 * P].rearrange("p (m k c) -> p m k c", m=4, k=DT)
                    o = ada_sum[:, n % SLOTS, :].rearrange("p (m c) -> p m c", m=4)
                    for k in range(DT):
                        if k == 0:
                            e = dve.tensor_scalar(o, w[:, :, k, :], cond_at(k), None, ALU.mult)
                        else:
                            e = dve.scalar_tensor_tensor(o, w[:, :, k, :], cond_at(k), o, ALU.mult, ALU.add)
                        if k < DT - 1:
                            e.then_inc(dve_done, steps.one())
                            dve.wait_ge(dve_done, steps.count())
                    e.then_inc(chunk_done[slot], 1)
                return chunk

            first_cond = lambda k: cond[:, k:k + 1]
            second_cond = lambda k: cond[:, DT + k:DT + k + 1]

            def ada_next(p, col, bias_cols):
                n = 4 * p.what.adas
                dve.wait_ge(signal["ada_cols"], p.of("ada_cols", p.what.adas + SLOTS))
                dve.tensor_tensor(mod_next[:, col:col + n], psum[:, 4 * 512:4 * 512 + n], bias_cols,
                                  ALU.add).then_inc(bank_free[4], 1)
                dve.wait_ge(bank_free[4], reads(p, 4, 0) + 1)

            def evacuate(p, mine, do, cond_at=None):
                lin = p.what

                def chunk(j, i, where):
                    for m in mine:
                        dve.wait_ge(*group_end(p, j, m, i, where))
                        do(j, m, i, half(lin.at[j][m][0])).then_inc(bank_free[lin.at[j][m][0]], 1)

                walk(p, loop(p), chunk, cond_at and ada_sums(p, cond_at))

            def gated(p, buf, dst, cond_at=None):
                lin = p.what

                def chunk(j, i, where):
                    for m in (1, 3):
                        b, _, k = lin.at[j][m]
                        dve.wait_ge(*group_end(p, j, m, i, where))
                        dve.wait_ge(bank_free[b - 1], reads(p, b - 1, lin.at[j][m - 1][2], i, 0 if isinstance(i, int) else lin.per_free[b - 1]) + 1)
                        o = dst[:, at(i, 6, 2 * j + m // 2), :]
                        dve.tensor_tensor(o, buf[:, m // 2, :], half(b), ALU.mult).then_inc(bank_free[b], 1)

                walk(p, loop(p), chunk, cond_at and ada_sums(p, cond_at))

            def add_to_x(p, scale):
                lin = p.what
                for j in range(lin.chunks):
                    for m in range(lin.groups):
                        f, b = j * lin.groups + m, lin.at[j][m][0]
                        dve.wait_ge(*group_end(p, j, m, 0, p.slot(j)))
                        dve.scalar_tensor_tensor(x[:, f, :], half(b), scale[:, f:f + 1], x[:, f, :],
                                                 ALU.mult, ALU.add).then_inc(bank_free[b], 1)

            def scale_x():
                dve.tensor_scalar(x[:, :, :], x[:, :, :], ALPHA, None, ALU.mult).then_inc(dve_done, steps.one())
                dve.wait_ge(dve_done, steps.count())

            def mean_square(p, b, eps):
                dve.wait_ge(bank_full[b], products(p, b))
                dve.tensor_scalar(rms[:, :], half(b), 1.0 / D, eps, ALU.mult, ALU.add).then_inc(bank_free[b], 1)
                dve.wait_ge(signal["root"], p.of("root", 1))
                dve.reciprocal(rms[:, :], rms[:, :]).then_inc(dve_done, steps.one())
                dve.wait_ge(dve_done, steps.count())

            def norm(p, dst, gains):
                mean_square(p, 5, EPS)
                for k in range(DT):
                    dve.scalar_tensor_tensor(dst[:, k, :], x[:, k, :], gains[:, k:k + 1], rms[:, :],
                                             ALU.mult, ALU.mult).then_inc(dve_done, steps.one())
                dve.wait_ge(dve_done, steps.count())

            def norm_mod(p):
                mean_square(p, 5, EPS)
                for k in range(DT + 1):
                    if k < DT:
                        dve.scalar_tensor_tensor(h[:, k, :], x[:, k, :], gain[:, k:k + 1], rms[:, :],
                                                 ALU.mult, ALU.mult).then_inc(dve_done, steps.one())
                    if k:
                        dve.wait_ge(dve_done, steps.count(1 if k < DT else 0))
                        dve.tensor_scalar(h[:, k - 1, :], h[:, k - 1, :], mod[:, k - 1:k], None, ALU.add).then_inc(signal["h"], 1)

            def modulate(shift, scale):
                for k in range(DT):
                    dve.tensor_scalar(h[:, k, :], x[:, k, :], mod1[:, scale + k:scale + k + 1],
                                      mod[:, shift + k:shift + k + 1], ALU.mult, ALU.add).then_inc(signal["h"], 1)

            def take_first(p, sub, half_gate):
                for b in range(LIN):
                    dve.wait_ge(bank_free[b], reads(p, b))
                dve.tensor_copy(mod[:, 0:3 * DT], mod_next[:, 0:3 * DT]).then_inc(dve_done, steps.one())
                dve.wait_ge(dve_done, steps.count())
                dve.scalar_tensor_tensor(gain[:, :], mod[:, DT:2 * DT], 1.0,
                                         lvec[:, sub * DT:(sub + 1) * DT], ALU.add, ALU.mult).then_inc(dve_done, steps.one())
                if half_gate:
                    dve.tensor_scalar(mod[:, 2 * DT:3 * DT], mod[:, 2 * DT:3 * DT], 0.5, None, ALU.mult).then_inc(dve_done, steps.one())
                dve.wait_ge(dve_done, steps.count())

            def take_second(p, a, z):
                for b in range(LIN):
                    dve.wait_ge(bank_free[b], reads(p, b))
                dve.tensor_copy(mod[:, a:z], mod_next[:, a:z]).then_inc(dve_done, steps.one())
                dve.tensor_scalar(mod1[:, a:z], mod_next[:, a:z], 1.0, None, ALU.add).then_inc(dve_done, steps.one())
                dve.wait_ge(dve_done, steps.count())

            def ada_b(n, l=0):
                c = VEC["ada_b"] + n * 3 * DT
                return vec[:, c:c + 3 * DT] if isinstance(l, int) else vec[:, bass.ds(l * (9 * DT) + c, 3 * DT)]

            def layer_norm(p, g, b):
                dve.wait_ge(bank_full[5], products(p, 5))
                dve.tensor_scalar(rms[:, :], half(5), 1.0 / D, None, ALU.mult).then_inc(bank_free[5], 1)
                dve.wait_ge(bank_free[5], reads(p, 5, 0) + 1)
                for k in range(DT):
                    dve.tensor_tensor(x[:, k, :], x[:, k, :], rms[:, :], ALU.subtract).then_inc(signal["mean"], 1)
                mean_square(p, 6, LN_EPS)
                for k in range(DT):
                    dve.scalar_tensor_tensor(x[:, k, :], x[:, k, :], g[:, k:k + 1], rms[:, :],
                                             ALU.mult, ALU.mult).then_inc(dve_done, steps.one())
                dve.wait_ge(dve_done, steps.count())
                for k in range(DT):
                    e = dve.tensor_scalar(x[:, k, :], x[:, k, :], b[:, k:k + 1], None, ALU.add)
                    if p.name == "ln3":
                        e.then_inc(signal["h"], 1)
                    else:
                        e.then_inc(dve_done, steps.one())
                dve.wait_ge(dve_done, steps.count())

            def logits(p, g):
                dve.wait_ge(signal["bias_in"], p.of("bias_in", 16))
                for n in range(HG):
                    b = 4 + n % 2
                    dve.wait_ge(bank_full[b], products(p, b, n // 2))
                    dve.scalar_tensor_tensor(logit[:, n, 0:P], bank(b)[:, 0:P], HD ** -0.5,
                                             bias[:, n, P:S], ALU.mult, ALU.add).then_inc(dve_done, steps.one())
                    dve.scalar_tensor_tensor(logit[:, n, P:P + S], bank(b)[:, P:P + S], HD ** -0.5,
                                             bias[:, n, :], ALU.mult, ALU.add).then_inc(bank_free[b], 1)
                dve.wait_ge(bank_free[4], reads(p, 4, 3) + 1)
                dve.wait_ge(bank_free[5], reads(p, 5, 3) + 1)
                dve.reduce_max(att[:, 0, g, 0:HG], logit[:, :, 0:P], AX).then_inc(dve_done, steps.one())
                dve.reduce_max(att[:, 0, g, HG:2 * HG], logit[:, :, P:P + S], AX).then_inc(dve_done, steps.one())
                dve.wait_ge(dve_done, steps.count())
                dve.tensor_scalar(att[:, 1, g, :], att[:, 0, g, :], -1.0, None, ALU.mult).then_inc(signal["maxima"], 1)

            def mix(p, g):
                for b in range(LIN):
                    dve.wait_ge(bank_free[b], reads(p, b))
                for n in range(0, HG, 2):
                    dve.wait_ge(bank_full[4], products(p, 4, n // 2))
                    dve.tensor_copy(prob_t[:, n, :], bank(4)[:, 0:3 * P]).then_inc(bank_free[4], 1)
                dve.wait_ge(bank_full[6], products(p, 6))
                dve.tensor_copy(o_g[:, g, 0, :], bank(6)).then_inc(bank_free[6], 1)

            def conv(p):
                for b in range(LIN):
                    dve.wait_ge(bank_free[b], reads(p, b))
                w = lvec[:, 3 * DT:6 * DT]
                for f in range(DT):
                    dve.tensor_scalar(conv_t[:, f, :], u_t[:, f, :], w[:, 2 * DT + f:2 * DT + f + 1],
                                      None, ALU.mult).then_inc(dve_done, steps.one())
                dve.wait_ge(dve_done, steps.count())
                for k, lag in ((1, 1), (0, 2)):
                    for f in range(DT):
                        dve.scalar_tensor_tensor(conv_t[:, f, lag:S], u_t[:, f, 0:S - lag],
                                                 w[:, k * DT + f:k * DT + f + 1],
                                                 conv_t[:, f, lag:S], ALU.mult, ALU.add).then_inc(dve_done, steps.one())
                    dve.wait_ge(dve_done, steps.count())

            def combine(p, mp):
                mx, sums, w, t = (att[:, k, :, :] for k in (0, 2, 3, 4))
                over = lambda a: a.unsqueeze(1).to_broadcast([P, NG, TT * HG])
                dve.wait_ge(bank_free[6], reads(mp, 6, 0) + 1)
                dve.wait_ge(bank_free[7], reads(mp, 7, 0) + 1)
                dve.tensor_tensor(t[:, 0, :], mx[:, 0, :], mx[:, 1, :], ALU.max).then_inc(dve_done, steps.one())
                dve.wait_ge(dve_done, steps.count())
                dve.tensor_tensor(t[:, 0, :], t[:, 0, :], mx[:, 2, :], ALU.max).then_inc(dve_done, steps.one())
                dve.wait_ge(dve_done, steps.count())
                dve.tensor_tensor(w, mx, over(t[:, 0, :]), ALU.subtract).then_inc(signal["shift"], 1)
                dve.wait_ge(signal["weights"], p.of("weights", 1))
                dve.tensor_tensor(t, w, sums, ALU.mult).then_inc(dve_done, steps.one())
                dve.wait_ge(dve_done, steps.count())
                dve.tensor_tensor(t[:, 0, :], t[:, 0, :], t[:, 1, :], ALU.add).then_inc(dve_done, steps.one())
                dve.wait_ge(dve_done, steps.count())
                dve.tensor_tensor(t[:, 0, :], t[:, 0, :], t[:, 2, :], ALU.add).then_inc(dve_done, steps.one())
                dve.wait_ge(dve_done, steps.count())
                dve.reciprocal(t[:, 0, :], t[:, 0, :]).then_inc(dve_done, steps.one())
                dve.wait_ge(dve_done, steps.count())
                dve.tensor_tensor(w, w, over(t[:, 0, :]), ALU.mult).then_inc(dve_done, steps.one())
                dve.wait_ge(dve_done, steps.count())
                every = lambda g: flat(60 + 4 * g, 4).rearrange("p (a e) -> p a e", e=HD)
                for g in range(NG):
                    dve.tensor_tensor(every(g), every(g),
                                      w[:, g, :].unsqueeze(2).to_broadcast([P, TT * HG, HD]), ALU.mult).then_inc(dve_done, steps.one())
                dve.wait_ge(dve_done, steps.count())
                dve.tensor_tensor(o_tok, o_g[:, 0, :, :], o_g[:, 1, :, :], ALU.add).then_inc(dve_done, steps.one())
                dve.wait_ge(dve_done, steps.count())
                dve.tensor_tensor(o_tok, o_tok, o_g[:, 2, :, :], ALU.add).then_inc(signal["mixed"], 1)
                dve.wait_ge(bank_full[6], products(p, 6))
                dve.tensor_copy(o_t[:, 0:2, :], bank(6)).then_inc(bank_free[6], 1)

            dve.wait_ge(small_in, 128)
            p = place("load_x")
            for b in range(LIN):
                dve.wait_ge(bank_full[b], products(p, b))
                dve.tensor_copy(x[:, 2 * b:2 * b + 2, :], bank(b)).then_inc(bank_free[b], 1)
            p = place("bias_rows")
            dve.wait_ge(bank_full[4], products(p, 4))
            dve.tensor_tensor(bias_row[:, 0:383], psum[0:NG * HG, 4 * 512:4 * 512 + 383], off_mask,
                              ALU.add).then_inc(bank_free[4], 1)
            dve.wait_ge(rows_out, 16)

            dve.wait_ge(cond_set, 2)
            p = place("ada0")
            walk(p, loop(p), None, ada_sums(p, first_cond))
            ada_next(p, 0, ada_b(0))

            for l in steps.loop("layer", DEPTH):
                on = lambda name: place(name, l)
                for b in range(LIN):
                    dve.wait_ge(bank_free[b], reads(on("norm0"), b))
                dve.tensor_copy(lvec[:, 0:3 * DT], vec[:, bass.ds(l * (3 * DT) + VEC["norm_g"], 3 * DT)]).then_inc(dve_done, steps.one())
                dve.tensor_copy(lvec[:, 3 * DT:6 * DT],
                                vec[:, bass.ds(l * (3 * DT) + VEC["conv_w"], 3 * DT)]).then_inc(dve_done, steps.one())
                dve.wait_ge(dve_done, steps.count())
                gate = mod[:, 2 * DT:3 * DT]
                take_first(on("norm0"), 0, True)
                norm_mod(on("norm0"))
                gated(on("up0"), act2, mid, first_cond)
                ada_next(on("up0"), 0, ada_b(1, l))
                add_to_x(on("down0"), gate)
                take_first(on("norm1"), 1, False)
                norm_mod(on("norm1"))
                evacuate(on("qk"), (1, 3), lambda j, m, i, ps:
                         dve.tensor_copy(qk[:, at(i, 12, 4 * j + m), :], ps), first_cond)
                ada_next(on("qk"), 0, ada_b(2, l))
                evacuate(on("v"), (1, 3), lambda j, m, i, ps:
                         dve.tensor_copy(vtok[:, m // 2, j * 512 + S:(j + 1) * 512], ps))
                logits(on("logits0"), 0)
                gated(on("ccch"), cc2, u_t)
                mix(on("mix0"), 0)
                logits(on("logits1"), 1)
                conv(on("cb"))
                evacuate(on("cb"), range(4), lambda j, m, i, ps:
                         dve.tensor_tensor(conv_t[:, 4 * j + m, :], conv_t[:, 4 * j + m, :], ps, ALU.mult))
                mix(on("mix1"), 1)
                logits(on("logits2"), 2)
                evacuate(on("conv_out"), range(4), lambda j, m, i, ps:
                         dve.tensor_tensor(merged[:, 4 * j + m, :], sig_c[:, 4 * j + m, :], ps, ALU.mult))
                mix(on("mix2"), 2)
                combine(on("combine"), on("mix2"))
                p = on("attn_out")
                for m in range(DT):
                    b = p.what.at[0][m][0]
                    dve.wait_ge(*group_end(p, 0, m, 0, p.slot(0)))
                    dve.tensor_tensor(sig_a[:, m, :], sig_a[:, m, :], half(b), ALU.mult).then_inc(bank_free[b], 1)
                for b in range(LIN):
                    dve.wait_ge(bank_free[b], reads(on("wo"), b))
                dve.tensor_tensor(merged[:, :, :], merged[:, :, :], sig_a[:, :, :], ALU.add).then_inc(signal["merged"], 1)
                add_to_x(on("wo"), gate)
                take_first(on("norm2"), 2, True)
                norm_mod(on("norm2"))
                gated(on("up2"), act2, mid, lambda k: cond[:, bass.ds(l * DT + k, 1)])
                ada_next(on("up2"), 0, ada_b(3, l))
                add_to_x(on("down2"), gate)

            p = place("final_norm")
            norm(p, x, vcol("final_g", 0, DT))
            take_second(place("mod3"), 0, 3 * DT)
            modulate(0, DT)
            rest = VEC["ada_b_2"] + 3 * DT
            evacuate(place("xm"), (1, 3), lambda j, m, i, ps:
                     dve.tensor_copy(xm[:, at(i, 12, 4 * j + m), :], ps), second_cond)
            ada_next(place("xm"), 3 * DT, vec[:, rest:rest + 12])
            for b in range(LIN):
                dve.wait_ge(bank_free[b], reads(place("z"), b))
            p = place("z")
            walk(p, loop(p), None, ada_sums(p, second_cond))
            ada_next(p, 3 * DT + 12, vec[:, rest + 12:rest + 24])
            p = place("mconv")
            for f in range(MT):
                dve.tensor_scalar(xc[:, f, :], xm[:, f, :], vcol("mlstm_conv_w_2", (MC - 1) * MT + f),
                                  None, ALU.mult).then_inc(dve_done, steps.one())
            dve.wait_ge(dve_done, steps.count())
            for lag in range(1, MC):
                for f in range(MT):
                    e = dve.scalar_tensor_tensor(xc[:, f, lag:S], xm[:, f, 0:S - lag],
                                                 vcol("mlstm_conv_w_2", (MC - 1 - lag) * MT + f),
                                                 xc[:, f, lag:S], ALU.mult, ALU.add)
                    if lag == MC - 1:
                        e.then_inc(signal["conv"], 1)
                    else:
                        e.then_inc(dve_done, steps.one())
                if lag < MC - 1:
                    dve.wait_ge(dve_done, steps.count())
            for name, dst in (("q", mq), ("k", mk), ("vT", mvt)):
                evacuate(place(name), range(1, 16, 2), lambda j, m, i, ps: dve.tensor_copy(dst[:, m, :], ps))
            p = place("vtok")
            for t in range(TT):
                for b in (1, 3):
                    dve.wait_ge(*group_end(p, 0, t * LIN + b, 0, p.slot(0)))
                    dve.tensor_copy(mv[:, t, b * 512:(b + 1) * 512], bank(b)).then_inc(bank_free[b], 1)
            p = place("gates")
            dve.wait_ge(bank_full[4], products(p, 4))
            dve.tensor_tensor(small[:, 0:16], psum[:, 4 * 512:4 * 512 + 16], bgate[:, :], ALU.add).then_inc(bank_free[4], 1)
            dve.wait_ge(bank_full[5], products(p, 5))
            dve.tensor_copy(row(0), psum[0:MH, 5 * 512:5 * 512 + S]).then_inc(dve_done, steps.one())
            dve.tensor_copy(row(1), psum[0:MH, 5 * 512 + S:6 * 512]).then_inc(bank_free[5], 1)
            dve.wait_ge(bank_free[5], reads(p, 5, 0) + 1)
            dve.tensor_scalar(row(3), row(1), 0.0, None, ALU.min).then_inc(dve_done, steps.one())
            dve.wait_ge(dve_done, steps.count())
            dve.wait_ge(signal["gate_logs"], p.of("gate_logs", 1))
            dve.tensor_tensor(row(3), row(3), row(2), ALU.subtract).then_inc(dve_done, steps.one())
            dve.wait_ge(dve_done, steps.count())
            one_row = ones[0:MH, 0:1].to_broadcast([MH, S])
            dve.tensor_tensor_scan(row(7), one_row, row(3), 0.0, ALU.mult, ALU.add).then_inc(dve_done, steps.one())
            dve.wait_ge(dve_done, steps.count())
            dve.tensor_tensor(row(5), row(0), row(7), ALU.subtract).then_inc(dve_done, steps.one())
            dve.wait_ge(dve_done, steps.count())
            dve.tensor_tensor_scan(row(4), one_row, row(5), 0.0, ALU.mult, ALU.max).then_inc(dve_done, steps.one())
            dve.wait_ge(dve_done, steps.count())
            dve.tensor_tensor(row(6), row(7), row(4), ALU.add).then_inc(signal["rows"], 1)
            p = place("rows_t")
            dve.wait_ge(bank_full[4], products(p, 4))
            dve.tensor_copy(small[:, 16:32], psum[:, 4 * 512:4 * 512 + 16]).then_inc(bank_free[4], 1)
            dve.wait_ge(bank_free[4], reads(p, 4, 0) + 1)
            for n in range(MH):
                b = 5 + n // 2
                c = half(b, n % 2)
                if n % 2 == 0:
                    dve.wait_ge(bank_full[b], products(p, b))
                dve.tensor_scalar(decay[:, n, 0:S], c, small[:, 16 + n:17 + n], 0.0,
                                  ALU.subtract, ALU.max).then_inc(dve_done, steps.one())
                e = dve.tensor_scalar(decay[:, n, S:S + P], c[:, P:S], small[:, 20 + n:21 + n], 0.0,
                                      ALU.subtract, ALU.max)
                if n % 2:
                    e.then_inc(bank_free[b], 1)
                else:
                    e.then_inc(dve_done, steps.one())
            dve.wait_ge(signal["decays"], p.of("decays", 1))
            for a in (0, S):
                dve.tensor_tensor(decay[:, :, a:a + P], decay[:, :, a:a + P],
                                  tri[:, :].unsqueeze(1).to_broadcast([P, MH, P]), ALU.mult).then_inc(dve_done, steps.one())
            dve.wait_ge(dve_done, steps.count())
            p = place("scores")
            for n in range(MH):
                dve.wait_ge(bank_full[n], products(p, n))
                dve.scalar_tensor_tensor(score[:, n, :], bank(n)[:, 0:S + P], 512.0 ** -0.5,
                                         decay[:, n, :], ALU.mult, ALU.mult).then_inc(bank_free[n], 1)
            for f in range(MT):
                dve.tensor_scalar(xc[:, f, :], xc[:, f, :], vcol("mlstm_skip_2", f), None, ALU.mult).then_inc(dve_done, steps.one())
            p = place("numer")
            den, neg, var = small[:, 48:56], small[:, 40:48], small[:, 56:64]
            dve.wait_ge(bank_full[7], products(p, 7))
            dve.tensor_copy(den, psum[:, 7 * 512:7 * 512 + 8]).then_inc(bank_free[7], 1)
            dve.wait_ge(bank_free[7], reads(p, 7, 0) + 1)
            dve.tensor_scalar(neg, den, -1.0, None, ALU.mult).then_inc(dve_done, steps.one())
            dve.wait_ge(dve_done, steps.count())
            dve.tensor_tensor(den, den, neg, ALU.max).then_inc(dve_done, steps.one())
            dve.wait_ge(dve_done, steps.count())
            dve.wait_ge(signal["floor"], place("rows_t").of("floor", 1))
            dve.tensor_tensor(den, den, small[:, 32:40], ALU.max).then_inc(dve_done, steps.one())
            dve.wait_ge(dve_done, steps.count())
            dve.reciprocal(den, den).then_inc(dve_done, steps.one())
            dve.wait_ge(dve_done, steps.count())
            for n in range(MH):
                for t in range(TT):
                    b, u, c = (2 * n + t) % LIN, (2 * n + t) // LIN, t * MH + n
                    dve.wait_ge(bank_full[b], products(p, b, u))
                    dve.tensor_scalar(hn[:, t, n * 512:(n + 1) * 512], bank(b), den[:, c:c + 1], None,
                                      ALU.mult).then_inc(bank_free[b], 1)
            for b in range(LIN):
                dve.wait_ge(bank_free[b], reads(place("h_t"), b))
            stats = small[:, 144:192].rearrange("p (n k) -> p n k", k=6)
            mv2 = small[:, 192:208].rearrange("p (n k) -> p n k", k=2)
            for n in range(MH):
                for t in range(TT):
                    dve.bn_stats(stats[:, t * MH + n, :], hn[:, t, n * 512:(n + 1) * 512]).then_inc(dve_done, steps.one())
            dve.wait_ge(dve_done, steps.count())
            for c in range(8):
                dve.bn_aggr(mv2[:, c, :], stats[:, c, :]).then_inc(dve_done, steps.one())
            dve.wait_ge(dve_done, steps.count())
            dve.tensor_scalar(var, mv2[:, :, 1], LN_EPS, None, ALU.add).then_inc(signal["mvar"], 1)
            dve.wait_ge(signal["mroot"], p.of("mroot", 1))
            dve.reciprocal(var, var).then_inc(dve_done, steps.one())
            dve.wait_ge(dve_done, steps.count())
            for n in range(MH):
                for t in range(TT):
                    c, part = t * MH + n, hn[:, t, n * 512:(n + 1) * 512]
                    e = dve.tensor_scalar(part, part, mv2[:, c, 0:1], var[:, c:c + 1], ALU.subtract, ALU.mult)
            e.then_inc(signal["hn"], 1)
            p = place("h_t")
            for f in range(MT):
                b, u = (f // 2) % LIN, f // 8
                if f % 2 == 0:
                    dve.wait_ge(bank_full[b], products(p, b, u))
                e = dve.scalar_tensor_tensor(mh[:, f, :], half(b, f % 2), vcol("mlstm_norm_w_2", f),
                                             xc[:, f, :], ALU.mult, ALU.add)
                if f % 2:
                    e.then_inc(bank_free[b], 1)
                else:
                    e.then_inc(dve_done, steps.one())
            for b in range(LIN):
                dve.wait_ge(bank_free[b], reads(place("m_out"), b))
            dve.tensor_tensor(mh[:, :, :], mh[:, :, :], zs[:, :, :], ALU.mult).then_inc(signal["mh"], 1)
            take_second(place("m_out"), 3 * DT, 6 * DT)
            scale_x()
            add_to_x(place("m_out"), mod1[:, 2 * DT:3 * DT])
            layer_norm(place("ln0"), vcol("ln_mix_g_2", 0, DT), vcol("ln_mix_b_2", 0, DT))
            modulate(3 * DT, 4 * DT)
            gated(place("up3"), act2, mid, second_cond)
            ada_next(place("up3"), 0, vcol("ada_b_2", 6 * DT, 6 * DT))
            scale_x()
            p = place("s5_b")
            s = lambda k: s5s[:, k, :]
            lr, li = vcol("s5_lambda_re_2", 0, ST), vcol("s5_lambda_im_2", 0, ST)

            def tt(o, a, b, op):
                dve.tensor_tensor(o, a, b, op).then_inc(dve_done, steps.one())

            dve.wait_ge(s5_in, 80)
            dve.wait_ge(signal["s5_dt"], p.of("s5_dt", 1))
            tt(s(1), lr, s(0), ALU.mult)
            tt(s(6), li, s(0), ALU.mult)
            dve.wait_ge(dve_done, steps.count())
            dve.tensor_scalar(s(5), s(6), 1.0 / PI2, ROUND, ALU.mult, ALU.add).then_inc(dve_done, steps.one())
            dve.wait_ge(dve_done, steps.count())
            dve.tensor_scalar(s(5), s(5), -ROUND, None, ALU.add).then_inc(dve_done, steps.one())
            dve.wait_ge(dve_done, steps.count())
            for part in (PI2_A, PI2_B, PI2_C):
                dve.scalar_tensor_tensor(s(6), s(5), -part, s(6), ALU.mult, ALU.add).then_inc(dve_done, steps.one())
                dve.wait_ge(dve_done, steps.count())
            dve.tensor_scalar(s(4), s(6), 1.0 / PI2, None, ALU.mult).then_inc(dve_done, steps.one())
            dve.wait_ge(dve_done, steps.count())
            dve.tensor_scalar(s(6), s(4), 0.25, None, ALU.add).then_inc(dve_done, steps.one())
            dve.wait_ge(dve_done, steps.count())
            for src, tmp, dst in ((4, 5, 2), (6, 10, 3)):
                dve.tensor_scalar(s(tmp), s(src), 1.0, ROUND, ALU.mult, ALU.add).then_inc(dve_done, steps.one())
                dve.wait_ge(dve_done, steps.count())
                dve.tensor_scalar(s(tmp), s(tmp), -ROUND, None, ALU.add).then_inc(dve_done, steps.one())
                dve.wait_ge(dve_done, steps.count())
                e = dve.tensor_tensor(s(dst), s(src), s(tmp), ALU.subtract)
                if dst == 2:
                    e.then_inc(dve_done, steps.one())
            e.then_inc(signal["s5_turns"], 1)
            dve.wait_ge(signal["s5_trig"], p.of("s5_trig", 1))
            dve.memset(quarter, np.pi / 2).then_inc(dve_done, steps.one())
            tt(s(5), s(1), s(3), ALU.mult)
            tt(s(6), s(1), s(2), ALU.mult)
            tt(s(9), lr, lr, ALU.mult)
            tt(s(10), li, li, ALU.mult)
            dve.wait_ge(dve_done, steps.count())
            dve.tensor_scalar(s(5), s(5), -1.0, None, ALU.add).then_inc(dve_done, steps.one())
            tt(s(9), s(9), s(10), ALU.add)
            dve.wait_ge(dve_done, steps.count())
            dve.reciprocal(s(9), s(9)).then_inc(dve_done, steps.one())
            tt(s(11), s(5), lr, ALU.mult)
            tt(s(12), s(6), li, ALU.mult)
            tt(s(13), s(6), lr, ALU.mult)
            tt(s(14), s(5), li, ALU.mult)
            dve.wait_ge(dve_done, steps.count())
            tt(s(7), s(11), s(12), ALU.add)
            tt(s(8), s(13), s(14), ALU.subtract)
            dve.wait_ge(dve_done, steps.count())
            tt(s(7), s(7), s(9), ALU.mult)
            tt(s(8), s(8), s(9), ALU.mult)
            dve.wait_ge(dve_done, steps.count())
            wide = lambda a: a.rearrange("p (i n) -> p i n", n=32)
            kr, ki = (s(k).unsqueeze(2).to_broadcast([P, ST, 32]) for k in (7, 8))
            tmp_a, tmp_b = wide(flat(36, 4)), wide(flat(40, 4))
            tt(wide(bar_re), wide(b_re), kr, ALU.mult)
            tt(tmp_a, wide(b_im), ki, ALU.mult)
            tt(wide(bar_im), wide(b_im), kr, ALU.mult)
            tt(tmp_b, wide(b_re), ki, ALU.mult)
            dve.wait_ge(dve_done, steps.count())
            tt(bar_re, bar_re, flat(36, 4), ALU.subtract)
            dve.tensor_tensor(bar_im, bar_im, flat(40, 4), ALU.add).then_inc(signal["s5_bar"], 1)
            add_to_x(place("down3"), mod1[:, 5 * DT:6 * DT])
            p = place("s5_b")
            for b in range(LIN):
                dve.wait_ge(bank_full[b], products(p, b))
                dve.tensor_copy(bar_t[:, b // 2, 4 * (b % 2):4 * (b % 2) + 4, :],
                                bank(b).rearrange("p (f n) -> p f n", f=4)).then_inc(bank_free[b], 1)
            take_second(place("ln1"), 0, 6 * DT)
            layer_norm(place("ln1"), vcol("ln_ffn_g_2", 0, DT), vcol("ln_ffn_b_2", 0, DT))
            modulate(0, DT)
            p = place("s5")
            bu = psum[:, 0:LIN * 512].rearrange("p (b r n) -> p b r n", b=LIN, r=2)
            for f in range(DT + 1):
                if f < DT:
                    dve.wait_ge(signal["waves"], p.of("waves", f + 1))
                    for j in range(LIN):
                        dve.wait_ge(bank_full[j], products(p, j, f))
                    dve.wait_ge(dve_done, steps.count())
                    cos, sin = wave_c[f % 2], wave_s[f % 2]
                    dve.tensor_tensor(pr[0], cos, bu[:, :, 0, :], ALU.mult).then_inc(dve_done, steps.one())
                    dve.tensor_tensor(pr[1], sin, bu[:, :, 1, :], ALU.mult).then_inc(dve_done, steps.one())
                    dve.tensor_tensor(pr[2], cos, bu[:, :, 1, :], ALU.mult).then_inc(dve_done, steps.one())
                    for j in range(LIN):
                        dve.tensor_tensor(pr[3][:, j, :], sin[:, j, :], bu[:, j, 0, :], ALU.mult).then_inc(bank_free[j], 1)
                if f:
                    cos, sin = wave_c[(f - 1) % 2], wave_s[(f - 1) % 2]
                    if f == DT:
                        dve.wait_ge(dve_done, steps.count())
                    if f > 1:
                        dve.wait_ge(signal["reals"], p.of("reals", f - 1))
                        dve.wait_ge(signal["states"], p.of("states", f - 1))
                    dve.tensor_tensor(back[2], sin, st_r, ALU.mult).then_inc(dve_done, steps.one())
                    dve.tensor_tensor(back[3], cos, st_i, ALU.mult).then_inc(dve_done, steps.one())
                    dve.tensor_tensor(back[0], cos, st_r, ALU.mult).then_inc(dve_done, steps.one())
                    dve.tensor_tensor(back[1], sin, st_i, ALU.mult).then_inc(signal["back"], 1)
                    if f > 1:
                        dve.wait_ge(bank_full[4], products(p, 4, f - 2))
                    dve.wait_ge(signal["back"], p.of("back", f))
                    dve.scalar_tensor_tensor(xs_i, back[2], -1.0, back[3], ALU.mult, ALU.subtract).then_inc(signal["states"], 1)
                if f < DT:
                    dve.wait_ge(signal["sums"], p.of("sums", f + 1))
                    for j in range(4):
                        mag = s5s[:, 1, 4 * f + j:4 * f + j + 1].to_broadcast([P, S])
                        dve.tensor_tensor_scan(st_r[:, j, :], mag, pr[0][:, j, :], 0.0, ALU.mult, ALU.add).then_inc(dve_done, steps.one())
                        dve.tensor_tensor_scan(st_i[:, j, :], mag, pr[2][:, j, :], 0.0, ALU.mult, ALU.add).then_inc(dve_done, steps.one())
            p = place("s5_gelu")
            dve.wait_ge(bank_free[4], reads(place("s5"), 4, DT - 1) + 1)
            for f in range(DT):
                e = dve.scalar_tensor_tensor(y_t[:, f, :], h[:, f, :], vcol("s5_d_2", f), y_t[:, f, :],
                                             ALU.mult, ALU.add)
            e.then_inc(signal["y"], 1)
            scale_x()
            p = place("glu")
            for j in range(4):
                for m in (0, 2):
                    b, _, k = p.what.at[j][m]
                    f = 2 * j + m // 2
                    dve.wait_ge(*group_end(p, j, m, 0, p.slot(j)))
                    dve.wait_ge(bank_free[b + 1], reads(p, b + 1, p.what.at[j][m + 1][2]) + 1)
                    dve.scalar_tensor_tensor(y_t[:, f, :], half(b), vcol("s5_b_glu_2", f),
                                             val2[:, m // 2, :], ALU.add, ALU.mult).then_inc(bank_free[b], 1)
            for b in range(LIN):
                dve.wait_ge(bank_free[b], reads(place("ln2"), b))
            for f in range(DT):
                dve.scalar_tensor_tensor(x[:, f, :], y_t[:, f, :], mod1[:, 2 * DT + f:2 * DT + f + 1],
                                         x[:, f, :], ALU.mult, ALU.add).then_inc(dve_done, steps.one())
            dve.wait_ge(dve_done, steps.count())
            dve.sem_inc(x_summed, 1)
            layer_norm(place("ln2"), vcol("ln_mix_g_2", DT, DT), vcol("ln_mix_b_2", DT, DT))
            modulate(3 * DT, 4 * DT)
            p = place("router")
            lg = small[:, 80:96].rearrange("p (t n) -> p t n", t=TT)
            top = small[:, 96:112].rearrange("p (t n) -> p t n", t=TT)
            idx = small[:, 112:128].rearrange("p (t n) -> p t n", t=TT)
            gate = small[:, 64:80].rearrange("p (t n) -> p t n", t=TT)
            gate2 = small[:, 136:152].rearrange("p (t n) -> p t n", t=TT)
            dve.wait_ge(bank_full[4], products(p, 4))
            dve.tensor_copy(small[:, 80:96], psum[:, 4 * 512:4 * 512 + 16]).then_inc(bank_free[4], 1)
            dve.wait_ge(bank_free[4], reads(p, 4, 0) + 1)
            for t in range(TT):
                dve.max(top[:, t, :], lg[:, t, :]).then_inc(dve_done, steps.one())
            dve.wait_ge(dve_done, steps.count())
            for t in range(TT):
                dve.max_index(index8[:, t, :], top[:, t, :], lg[:, t, :]).then_inc(dve_done, steps.one())
            dve.wait_ge(dve_done, steps.count())
            dve.tensor_copy(idx, index8[:, :, :]).then_inc(dve_done, steps.one())
            dve.tensor_tensor(small[:, 128:130], top[:, :, 1], top[:, :, 0], ALU.subtract).then_inc(signal["top"], 1)
            dve.wait_ge(signal["ratio"], p.of("ratio", 1))
            dve.tensor_scalar(small[:, 130:132], small[:, 128:130], 1.0, None, ALU.add).then_inc(dve_done, steps.one())
            dve.wait_ge(dve_done, steps.count())
            dve.reciprocal(small[:, 132:134], small[:, 130:132]).then_inc(dve_done, steps.one())
            dve.wait_ge(dve_done, steps.count())
            dve.tensor_tensor(small[:, 134:136], small[:, 128:130], small[:, 132:134], ALU.mult).then_inc(dve_done, steps.one())
            dve.wait_ge(dve_done, steps.count())
            for t in range(TT):
                dve.tensor_scalar(gate[:, t, :], iota8[:, :], idx[:, t, 0:1], small[:, 132 + t:133 + t],
                                  ALU.is_equal, ALU.mult).then_inc(dve_done, steps.one())
                dve.tensor_scalar(gate2[:, t, :], iota8[:, :], idx[:, t, 1:2], small[:, 134 + t:135 + t],
                                  ALU.is_equal, ALU.mult).then_inc(dve_done, steps.one())
            dve.wait_ge(dve_done, steps.count())
            dve.tensor_tensor(gate, gate, gate2, ALU.add).then_inc(dve_done, steps.one())
            dve.wait_ge(dve_done, steps.count())
            for t in range(TT):
                dve.tensor_scalar(gate2[:, t, :], iota8[:, :], idx[:, t, 1:2], None, ALU.is_equal).then_inc(dve_done, steps.one())
            dve.wait_ge(dve_done, steps.count())
            for t in range(TT):
                e = dve.scalar_tensor_tensor(chosen[:, t * NE:(t + 1) * NE], iota8[:, :], idx[:, t, 0:1], gate2[:, t, :],
                                             ALU.is_equal, ALU.add)
                if t == TT - 1:
                    e.then_inc(signal["gate"], 1)
            dve.wait_ge(bank_full[5], products(p, 5))
            dve.tensor_copy(count[:, :], psum[0:1, 5 * 512 + S:5 * 512 + S + NE]).then_inc(dve_done, steps.one())
            dve.tensor_copy(chosen_t, psum[0:NE, 5 * 512:5 * 512 + S]).then_inc(dve_done, steps.one())
            dve.wait_ge(dve_done, steps.count())
            dve.tensor_tensor_scan(ranks_t, ones[0:NE, 0:1].to_broadcast([NE, S]), chosen_t, 0.0,
                                   ALU.mult, ALU.add).then_inc(dve_done, steps.one())
            dve.wait_ge(dve_done, steps.count())
            dve.tensor_tensor(rms[0:NE, :], ranks_t, chosen_t, ALU.mult).then_inc(bank_free[5], 1)
            p = place("tokens")
            for b in (0, 2):
                dve.wait_ge(bank_full[b], products(p, b))
                dve.tensor_copy(h_tok[:, b // 2, (b % 2) * 512:(b % 2 + 1) * 512], bank(b)).then_inc(bank_free[b], 1)
            dve.memset(listed[:, NE, :], 0.0).then_inc(dve_done, steps.one())
            p = place("router")
            dve.wait_ge(bank_full[4], products(p, 4, 1))
            by_token = psum[:, 4 * 512:4 * 512 + TT * NE].rearrange("p (t e) -> p e t", t=TT)
            dve.tensor_copy(listed[:, 0:NE, TT:2 * TT], gate.rearrange("p t e -> p e t")).then_inc(dve_done, steps.one())
            dve.tensor_copy(listed[:, 0:NE, 0:TT], by_token).then_inc(bank_free[4], 1)
            dve.wait_ge(bank_free[4], reads(p, 4, 1) + 1)

            def pick(e):
                dve.wait_ge(dve_done, steps.count())
                dve.tensor_copy(now[:, :], listed[:, e, :]).then_inc(dve_done, steps.one())
                dve.wait_ge(dve_done, steps.count())
                for t in range(TT):
                    dve.tensor_scalar(sel[:, t, :], time, now[:, t:t + 1], None, ALU.is_equal).then_inc(dve_done, steps.one())
                for t in range(TT):
                    e_last = dve.tensor_scalar(sel_gate[:, t, :], time, now[:, t:t + 1],
                                               now[:, TT + t:TT + t + 1], ALU.is_equal, ALU.mult)
                    if t < TT - 1:
                        e_last.then_inc(dve_done, steps.one())
                dve.wait_ge(dve_done, steps.count())
                e_last.then_inc(signal["picked"], 1)
            pick(0)
            dve.memset(acc[:, :, :], 0.0).then_inc(dve_done, steps.one())
            scale_x()
            for e in steps.loop("expert", NE):
                p = place("gather", e)
                for f in range(0, DT, 2):
                    dve.wait_ge(bank_full[f % LIN], products(p, f % LIN, f // LIN))
                    dve.tensor_copy(h[:, f, :], half(f % LIN)).then_inc(bank_free[f % LIN], 1)
                dve.wait_ge(bank_full[5], products(p, 5))
                dve.tensor_copy(gate_sel[:, :, :], bank(5)).then_inc(bank_free[5], 1)
                gated(place("upE", e), act2, mid)
                p = place("downE", e)
                for side in range(2):
                    dve.wait_ge(*group_end(p, 2 * side + 1, 0, 0, p.slot(2 * side + 1)))
                    dve.tensor_copy(y_pos[:, 0, side * 512:(side + 1) * 512], bank(2 * side)).then_inc(bank_free[2 * side], 1)
                pick(at(e, 1, 1))
                p = place("scatter", e)
                for f in range(DT):
                    dve.wait_ge(bank_full[f % LIN], products(p, f % LIN, f // LIN))
                    dve.tensor_tensor(acc[:, f, :], acc[:, f, :], half(f % LIN), ALU.add).then_inc(bank_free[f % LIN], 1)
            for b in range(LIN):
                dve.wait_ge(bank_free[b], reads(place("ln3"), b))
            for f in range(DT):
                dve.scalar_tensor_tensor(x[:, f, :], acc[:, f, :], mod1[:, 5 * DT + f:5 * DT + f + 1],
                                         x[:, f, :], ALU.mult, ALU.add).then_inc(dve_done, steps.one())
            dve.wait_ge(dve_done, steps.count())
            dve.sem_inc(x_summed, 1)
            layer_norm(place("ln3"), vcol("ln_ffn_g_2", DT, DT), vcol("ln_ffn_b_2", DT, DT))
            p = place("store")
            for b in (0, 2):
                dve.wait_ge(bank_full[b], products(p, b))
                dve.tensor_copy(y_tok[:, b // 2, (b % 2) * 512:(b % 2 + 1) * 512], bank(b))\
                    .then_inc(y_set_dve, 1)

        @block.gpsimd
        def _(pool):
            steps = Steps(pool, periods["pool"])
            for b in range(BANKS):
                pool.sem_inc(signal[f"free{b}"], 1)
            for s in range(SLOTS):
                pool.sem_inc(chunk_done[s], 1)
            pool.sem_inc(signal["ada_cols"], SLOTS)
            pool.memset(ones[:, :], 1.0).then_inc(ones_set, 1)
            pool.wait_ge(bank_free[4], reads(place("bias_rows"), 4, 0) + 1)
            pool.dma_start(dram["bias_rows"], bias_row[:, 0:383]).then_inc(rows_out, 16)
            pool.wait_ge(rows_out, 16)
            src = bass.AP(dram["bias_rows"].tensor, P - 1, [[383, NG * HG], [-1, P], [1, S]])
            pool.dma_start(dram["bias_table"], src).then_inc(table_out, 16)
            pool.wait_ge(table_out, 16)
            for l in range(DEPTH):
                for g in range(NG):
                    p = place(f"logits{g}", l)
                    if g:
                        before = place(f"logits{g - 1}", l)
                        pool.wait_ge(bank_free[4], reads(before, 4, 3) + 1)
                        pool.wait_ge(bank_free[5], reads(before, 5, 3) + 1)
                    else:
                        for b in range(LIN):
                            pool.wait_ge(bank_free[b], reads(place("norm1", l), b))
                    src = dram["bias_table"][g * HG:(g + 1) * HG].rearrange("h i j -> i h j")
                    pool.dma_start(bias[:, :, :], src).then_inc(signal["bias_in"], 16)
            for b in range(LIN):
                pool.wait_ge(bank_free[b], reads(place("gates"), b))
            pool.dma_start(w_gate_m, dram["m_gates"]).then_inc(mgate_in, 16)
            pool.dma_start(tri, dram["tri"]).then_inc(mgate_in, 16)
            for b in range(LIN):
                pool.wait_ge(bank_free[b], reads(place("ln0"), b))
            for dst, name in ((b_re, "s5_b_re"), (b_im, "s5_b_im"), (c_re, "s5_c_re"), (c_im, "s5_c_im"),
                              (time, "time")):
                pool.dma_start(dst, dram[name]).then_inc(s5_in, 16)
            pool.wait_ge(s5_in, 80)
            for b in range(LIN):
                pool.wait_ge(bank_free[b], reads(place("s5"), b))
            p = place("s5")

            def turns(f):
                pool.tensor_tensor(turn, time.unsqueeze(1).to_broadcast([P, 4, S]),
                                   s5s[:, 4, 4 * f:4 * f + 4].unsqueeze(2).to_broadcast([P, 4, S]), ALU.mult).then_inc(pool_done, steps.one())
                pool.wait_ge(pool_done, steps.count())
                pool.tensor_scalar(near, turn, 1.0, ROUND, ALU.mult, ALU.add).then_inc(pool_done, steps.one())
                pool.wait_ge(pool_done, steps.count())
                pool.tensor_scalar(near, near, 1.0, -ROUND, ALU.mult, ALU.add).then_inc(pool_done, steps.one())
                pool.wait_ge(pool_done, steps.count())
                pool.tensor_tensor(turn, turn, near, ALU.subtract).then_inc(signal["turns"], 1)

            def reals(f):
                pool.wait_ge(signal["back"], p.of("back", f + 1))
                if f:
                    pool.wait_ge(bank_full[4], products(p, 4, f - 1))
                pool.tensor_tensor(xs_r, back[0], back[1], ALU.subtract).then_inc(signal["reals"], 1)

            turns(0)
            for f in range(DT):
                if f + 1 < DT:
                    pool.wait_ge(signal["waves"], p.of("waves", f + 1))
                    turns(f + 1)
                pool.wait_ge(bank_free[3], reads(p, 3, f) + 1)
                pool.tensor_tensor(pr[0], pr[0], pr[1], ALU.add).then_inc(pool_done, steps.one())
                pool.tensor_tensor(pr[2], pr[2], pr[3], ALU.subtract).then_inc(signal["sums"], 1)
                if f:
                    reals(f - 1)
            reals(DT - 1)
            for b in range(LIN):
                pool.wait_ge(bank_free[b], reads(place("glu"), b))
            pool.wait_ge(bank_free[4], reads(place("s5"), 4, DT - 1) + 1)
            pool.dma_start(w_router, dram["router"]).then_inc(route_in, 16)



def by_tile(w, per_chunk):
    k, n = w.shape
    t = w.reshape(k // P, P, n // P, P).transpose(2, 1, 0, 3).reshape(n // P, P, k)
    return t.reshape(-1, per_chunk, P, k).transpose(0, 2, 1, 3).reshape(-1, P, per_chunk * k)


def paired(a, b):
    k, n = a.shape
    both = np.stack([a.reshape(k, n // P, P), b.reshape(k, n // P, P)], axis=2)
    return by_tile(both.reshape(k, 2 * n), 4)


def by_row(w):
    k, n = w.shape
    return w.reshape(k // P, P, n // 512, 512).transpose(2, 1, 0, 3).reshape(n // 512, P, k // P * 512)


def in_halves(w):
    return w.reshape(w.shape[0], P, 2, -1).transpose(0, 2, 1, 3).reshape(2 * w.shape[0], P, -1)


def block_diagonal(w):
    n = w.shape[0] // 32
    t = np.zeros((n, 32, 4, 32, 4), w.dtype)
    w = w.reshape(n, 32, 4, 4)
    for b in range(32):
        t[:, b, :, b, :] = w[:, b]
    return t.reshape(n, P, P).transpose(1, 0, 2).reshape(1, P, n * P)


def states(w):
    t = np.zeros((ST, 2, 64, 2, 16), w.dtype)
    for g in range(2):
        t[:, g, :, g, :] = w.reshape(ST, 2, 64, 16)[:, g]
    return t.reshape(ST, P, 32).transpose(1, 0, 2).reshape(P, ST * 32)


def columns(v):
    return np.ascontiguousarray(v.reshape(-1, P).T)


def bucket_of(dist):
    exact = BUCKETS // 2
    d = np.maximum(dist, 1).astype(np.float32)
    large = exact + (np.log(d / exact) / np.log(MAX_DISTANCE / exact) * (BUCKETS - exact)).astype(np.int32)
    return np.where(dist < exact, dist, np.minimum(large, BUCKETS - 1)).astype(np.int32)


def shape_tables():
    dist = 255 - np.arange(383)
    bucket = bucket_of(np.maximum(dist, 0))
    one_hot = (np.arange(BUCKETS)[:, None] == bucket[None]).astype(np.float32)
    off = np.zeros((NG, HG, 383), np.float32)
    for g, (window, dilation) in enumerate(WINDOWS):
        off[g][:, (dist < 0) | (dist > window) | (dist % dilation != 0)] = NEG
    return {
        "ident": np.eye(P, dtype=np.float32), "one_hot": one_hot, "off_mask": off.reshape(NG * HG, 383),
        "tri": np.triu(np.ones((P, P), np.float32)),
        "iota8": np.tile(np.arange(NE, dtype=np.float32), (P, 1)),
        "time": np.tile(np.arange(1, S + 1, dtype=np.float32), (P, 1)),
    }


def layout(a):
    qkv = 3 * VW
    cat = lambda parts: np.concatenate(parts, axis=0)
    w_in = a["w_in"]
    part = lambda l, n: w_in[l][:, qkv + n * D:qkv + (n + 1) * D]
    two = range(DEPTH)
    arrays = {
        "x": a["x"].reshape(TT, P, D).transpose(1, 0, 2),
        "vec": np.concatenate([columns(s5_states(name, a[name])) for name in VEC], axis=1),
        "rel_bias": a["rel_bias"],
        "b_gates": np.tile(a["mlstm_b_gates_2"], (P, TT)),
        "ada": cat([by_tile(w, 4) for name in ("ada_w", "ada_w_2") for w in a[name]]),
        "up": cat([paired(a["ffn_w_gate"][l, n], a["ffn_w_up"][l, n]) for l in two for n in range(2)]),
        "down": cat([by_tile(a["ffn_w_down"][l, n], 2) for l in two for n in range(2)]),
        "w_qk": cat([by_tile(w[:, 0:2 * VW], 4) for w in w_in]),
        "w_v": cat([by_row(w[:, 2 * VW:qkv]) for w in w_in]),
        "w_ccch": cat([paired(part(l, 1), part(l, 2)) for l in two]),
        "w_cb": cat([by_tile(part(l, 0), 4) for l in two]),
        "w_gates": cat([by_tile(part(l, n), 4) for l in two for n in (3, 4)]),
        "w_conv_out": cat([by_tile(w, 4) for w in a["w_conv_out"]]),
        "w_attn_out": cat([by_tile(w, 8) for w in a["w_attn_out"]]),
        "w_o": cat([by_tile(w, 4) for w in a["w_o"]]),
        "m_xm": by_tile(a["mlstm_w_in_2"][0][:, 0:MT * P], 4),
        "m_z": by_tile(a["mlstm_w_in_2"][0][:, MT * P:], 4),
        "m_q": block_diagonal(a["mlstm_wq_2"][0]),
        "m_k": block_diagonal(a["mlstm_wk_2"][0]),
        "m_v": block_diagonal(a["mlstm_wv_2"][0]),
        "m_gates": a["mlstm_w_gates_2"][0].reshape(3 * MT, P, 2 * MH).transpose(1, 0, 2),
        "m_out": by_tile(a["mlstm_w_out_2"][0], 2),
        "up_3": paired(a["ffn_w13_2"][0][:, 0:FT * P], a["ffn_w13_2"][0][:, FT * P:]),
        "down_3": by_tile(a["ffn_w2_2"][0], 2),
        "s5_b_re": states(a["s5_b_re_2"][0]), "s5_b_im": states(a["s5_b_im_2"][0]),
        "s5_c_re": states(a["s5_c_re_2"][0].transpose(0, 2, 1)),
        "s5_c_im": states(a["s5_c_im_2"][0].transpose(0, 2, 1)),
        "glu": paired(a["s5_w_glu_2"][0][:, 0:D], a["s5_w_glu_2"][0][:, D:]),
        "router": a["moe_router_2"][0].reshape(DT, P, NE).transpose(1, 0, 2),
        "up_e": cat([paired(w[:, 0:FT * P], w[:, FT * P:]) for w in a["moe_w13_2"][0]]),
        "down_e": cat([in_halves(by_row(w)) for w in a["moe_w2_2"][0]]),
        **shape_tables(),
    }
    return {k: np.ascontiguousarray(v) for k, v in arrays.items()}


def s5_states(name, v):
    return np.repeat(v.reshape(-1), 64) if name == "s5_log_dt_2" else v


def program(nc, arrays, periods):
    dram = {}
    for name, a in arrays.items():
        dram[name] = nc.dram_tensor(f"in_{name}_dram", a.shape, mybir.dt.from_np(a.dtype),
                                    kind="ExternalInput").ap()
    dram["m_v_again"] = dram["m_v"]
    dram["bias_rows"] = nc.dram_tensor("bias_rows_dram", (NG * HG, 383), F32, kind="Internal").ap()
    dram["bias_table"] = nc.dram_tensor("bias_table_dram", (NG * HG, P, S), F32, kind="Internal").ap()
    out = nc.dram_tensor("out_0_dram", (1, S, D), F32, kind="ExternalOutput").ap()
    build(nc, dram, out, periods)


def kernel(**inputs):
    import concourse.bacc as bacc
    from concourse.bass_utils import run_bass_kernel_spmd as run

    arrays = layout({k: np.asarray(v) for k, v in inputs.items()})
    periods = {"act": {}, "dve": {}, "pool": {}}
    program(bacc.Bacc("TRN2", target_bir_lowering=False, num_devices=1), arrays, periods)
    nc = bacc.Bacc("TRN2", target_bir_lowering=False, num_devices=1)
    program(nc, arrays, periods)
    r = run(nc, [{f"in_{name}_dram": a for name, a in arrays.items()}], core_ids=[0])
    return r.results[0]["out_0_dram"]
```
